# Optimizing a Trainium2 kernel written in Bass

```python
import math
import jax, jax.numpy as jnp
from jax import lax
import numpy as np

D_MODEL = 1024
BATCH = 1
SEQ = 256
DEPTH = 2

GRID_W = 64
CTX_LEN = 256
ROPE_THETA = 10000.0
NORM_EPS = 1e-6
NEG_INF = -1e30
Q_BLOCK = 128

HEAD_DIM = 64
A_HEADS = 8
A_KV_HEADS = 2
B_HEADS = 8
B_KV_HEADS = 2
WINDOW = 128
A_Q_W = A_HEADS * HEAD_DIM
A_KV_W = A_KV_HEADS * HEAD_DIM
B_Q_W = B_HEADS * HEAD_DIM
B_KV_W = B_KV_HEADS * HEAD_DIM
EVEN_WIDTHS = (A_Q_W, A_KV_W, A_KV_W, B_Q_W, B_KV_W, B_KV_W)
EVEN_IN_W = sum(EVEN_WIDTHS)
EVEN_OUT_W = (A_HEADS + B_HEADS) * HEAD_DIM

C_HEADS = 8
C_Q_LORA = 384
C_KV_LORA = 256
C_NOPE = 128
C_ROPE = 64
C_V = 128
C_IN_W = C_Q_LORA + C_KV_LORA + C_ROPE

PEER_HEADS = 8
PEER_KEYS = 128
PEER_EXPERTS = PEER_KEYS * PEER_KEYS
PEER_KEY_DIM = 256
PEER_TOPK = 16
PEER_BLOCK = 128

N_EVEN = (DEPTH + 1) // 2
N_ODD = DEPTH // 2

kernel_name = "hybrid_gqa_swa_mla_peer_prefix_dit"

def rmsnorm(x, g):
    xf = x.astype(jnp.float32)
    y = xf * lax.rsqrt(jnp.mean(xf * xf, axis=-1, keepdims=True) + NORM_EPS)
    return (y * g.astype(jnp.float32)).astype(x.dtype)

def modulate(h, shift, scale):
    return h * (1.0 + scale) + shift

def axial_rope_tables(rows, rot_dim):
    row = jnp.repeat(jnp.arange(rows, dtype=jnp.float32), GRID_W)
    col = jnp.tile(jnp.arange(GRID_W, dtype=jnp.float32), rows)
    half = rot_dim // 2
    inv = ROPE_THETA ** (-jnp.arange(0, half, 2, dtype=jnp.float32) / half)
    ang = jnp.concatenate([row[:, None] * inv, col[:, None] * inv], axis=-1)
    return jnp.cos(ang), jnp.sin(ang)

def apply_rope(x, cos, sin):
    xf = x.astype(jnp.float32)
    x1, x2 = xf[..., 0::2], xf[..., 1::2]
    cs, sn = cos[None, :, None, :], sin[None, :, None, :]
    out = jnp.stack([x1 * cs - x2 * sn, x1 * sn + x2 * cs], axis=-1).reshape(x.shape)
    return out.astype(x.dtype)

def attend(q, k, v, scale, mask=None, sink=None):
    B, Tq, Hq, dq = q.shape
    Hkv = k.shape[2]
    G = Hq // Hkv
    qg = q.reshape(B, Tq, Hkv, G, dq).astype(jnp.float32)
    s = jnp.einsum('bqhgd,bkhd->bhgqk', qg, k.astype(jnp.float32)) * scale
    if mask is not None:
        s = jnp.where(mask, s, NEG_INF)
    if sink is not None:
        sk = jnp.broadcast_to(sink.astype(jnp.float32).reshape(1, Hkv, G, 1, 1), s.shape[:-1] + (1,))
        s = jnp.concatenate([sk, s], axis=-1)
    p = jax.nn.softmax(s, axis=-1)
    if sink is not None:
        p = p[..., 1:]
    o = jnp.einsum('bhgqk,bkhd->bqhgd', p, v.astype(jnp.float32))
    return o.reshape(B, Tq, Hq, v.shape[-1]).astype(q.dtype)

def blocked_global(q, k, v, scale):
    B, S, Hq, dq = q.shape
    nb = S // Q_BLOCK
    qb = q.reshape(B, nb, Q_BLOCK, Hq, dq).swapaxes(0, 1)
    ob = lax.map(lambda qi: attend(qi, k, v, scale), qb)
    return ob.swapaxes(0, 1).reshape(B, S, Hq, v.shape[-1])

def blocked_window(q, k_lat, v_lat, k_ctx, v_ctx, sink, scale):
    B, S, Hq, dq = q.shape
    nb = S // Q_BLOCK
    span = Q_BLOCK + 2 * WINDOW
    n_ctx = k_ctx.shape[1]
    pad = ((0, 0), (WINDOW, WINDOW), (0, 0), (0, 0))
    kp, vp = jnp.pad(k_lat, pad), jnp.pad(v_lat, pad)
    qb = q.reshape(B, nb, Q_BLOCK, Hq, dq).swapaxes(0, 1)

    def one(args):
        i, qi = args
        start = i * Q_BLOCK
        kw = lax.dynamic_slice_in_dim(kp, start, span, axis=1)
        vw = lax.dynamic_slice_in_dim(vp, start, span, axis=1)
        q_t = start + jnp.arange(Q_BLOCK)
        k_t = start - WINDOW + jnp.arange(span)
        band = ((jnp.abs(k_t[None, :] - q_t[:, None]) <= WINDOW)
                & (k_t[None, :] >= 0) & (k_t[None, :] < S))
        mask = jnp.concatenate([jnp.ones((Q_BLOCK, n_ctx), dtype=bool), band], axis=1)
        return attend(qi, jnp.concatenate([k_ctx, kw], axis=1),
                      jnp.concatenate([v_ctx, vw], axis=1), scale, mask, sink)

    ob = lax.map(one, (jnp.arange(nb), qb))
    return ob.swapaxes(0, 1).reshape(B, S, Hq, v_lat.shape[-1])

def even_heads(h, w_in, a_qn, a_kn, b_qn, b_kn, rope):
    B, T, _ = h.shape
    offsets = np.cumsum(EVEN_WIDTHS)[:-1].tolist()
    aq, ak, av, bq, bk, bv = jnp.split(h @ w_in, offsets, axis=-1)
    heads = lambda t, n: t.reshape(B, T, n, HEAD_DIM)
    aq, ak = rmsnorm(heads(aq, A_HEADS), a_qn), rmsnorm(heads(ak, A_KV_HEADS), a_kn)
    bq, bk = rmsnorm(heads(bq, B_HEADS), b_qn), rmsnorm(heads(bk, B_KV_HEADS), b_kn)
    av, bv = heads(av, A_KV_HEADS), heads(bv, B_KV_HEADS)
    if rope is not None:
        aq, ak, bq, bk = (apply_rope(t, *rope) for t in (aq, ak, bq, bk))
    return aq, ak, av, bq, bk, bv

def mixer_even(h_ctx, h_lat, w_in, w_out, a_qn, a_kn, b_qn, b_kn, b_sink, rope, ctx_out):
    caq, cak, cav, cbq, cbk, cbv = even_heads(h_ctx, w_in, a_qn, a_kn, b_qn, b_kn, None)
    laq, lak, lav, lbq, lbk, lbv = even_heads(h_lat, w_in, a_qn, a_kn, b_qn, b_kn, rope)
    scale = HEAD_DIM ** -0.5
    B, S = h_lat.shape[:2]
    oa = blocked_global(laq, jnp.concatenate([cak, lak], axis=1),
                        jnp.concatenate([cav, lav], axis=1), scale)
    ob = blocked_window(lbq, lbk, lbv, cbk, cbv, b_sink, scale)
    o_lat = jnp.concatenate([oa.reshape(B, S, A_Q_W), ob.reshape(B, S, B_Q_W)], axis=-1) @ w_out
    o_ctx = None
    if ctx_out:
        T = h_ctx.shape[1]
        oa_c = attend(caq, cak, cav, scale)
        ob_c = attend(cbq, cbk, cbv, scale, sink=b_sink)
        o_ctx = jnp.concatenate([oa_c.reshape(B, T, A_Q_W), ob_c.reshape(B, T, B_Q_W)], axis=-1) @ w_out
    return o_ctx, o_lat

def mla_heads(h, w_in, q_a_norm, kv_a_norm, w_uq, w_ukv, qn_nope, qn_rope, kn_nope, kn_rope, rope):
    B, T, _ = h.shape
    p = h @ w_in
    cq = rmsnorm(p[..., :C_Q_LORA], q_a_norm)
    ckv = rmsnorm(p[..., C_Q_LORA:C_Q_LORA + C_KV_LORA], kv_a_norm)
    k_pe = rmsnorm(p[..., C_Q_LORA + C_KV_LORA:].reshape(B, T, 1, C_ROPE), kn_rope)
    q = (cq @ w_uq).reshape(B, T, C_HEADS, C_NOPE + C_ROPE)
    kv = (ckv @ w_ukv).reshape(B, T, C_HEADS, C_NOPE + C_V)
    q_nope, q_pe = rmsnorm(q[..., :C_NOPE], qn_nope), rmsnorm(q[..., C_NOPE:], qn_rope)
    k_nope, v = rmsnorm(kv[..., :C_NOPE], kn_nope), kv[..., C_NOPE:]
    if rope is not None:
        q_pe, k_pe = apply_rope(q_pe, *rope), apply_rope(k_pe, *rope)
    q = jnp.concatenate([q_nope, q_pe], axis=-1)
    k = jnp.concatenate([k_nope, jnp.broadcast_to(k_pe, (B, T, C_HEADS, C_ROPE))], axis=-1)
    return q, k, v

def mixer_mla(h_ctx, h_lat, w_in, q_a_norm, kv_a_norm, w_uq, w_ukv,
              qn_nope, qn_rope, kn_nope, kn_rope, w_out, rope, ctx_out):
    args = (w_in, q_a_norm, kv_a_norm, w_uq, w_ukv, qn_nope, qn_rope, kn_nope, kn_rope)
    cq, ck, cv = mla_heads(h_ctx, *args, None)
    lq, lk, lv = mla_heads(h_lat, *args, rope)
    scale = (C_NOPE + C_ROPE) ** -0.5
    B, S = h_lat.shape[:2]
    o_lat = blocked_global(lq, jnp.concatenate([ck, lk], axis=1),
                           jnp.concatenate([cv, lv], axis=1), scale)
    o_lat = o_lat.reshape(B, S, C_HEADS * C_V) @ w_out
    o_ctx = None
    if ctx_out:
        o_ctx = attend(cq, ck, cv, scale).reshape(B, h_ctx.shape[1], C_HEADS * C_V) @ w_out
    return o_ctx, o_lat

def peer_ffn(h, w_query, sub_keys, expert_u, expert_v):
    B, T, D = h.shape
    tokens = h.reshape(-1, PEER_BLOCK, D)

    def block(hb):
        q = (hb @ w_query).reshape(PEER_BLOCK, PEER_HEADS, 2, PEER_KEY_DIM // 2)
        s = jnp.einsum('thpk,hpnk->thpn', q.astype(jnp.float32), sub_keys.astype(jnp.float32))
        s_top, i_top = lax.top_k(s, PEER_TOPK)
        cand = (s_top[:, :, 0, :, None] + s_top[:, :, 1, None, :]).reshape(PEER_BLOCK, PEER_HEADS, -1)
        cand_idx = (i_top[:, :, 0, :, None] * PEER_KEYS + i_top[:, :, 1, None, :]).reshape(PEER_BLOCK, PEER_HEADS, -1)
        best, pos = lax.top_k(cand, PEER_TOPK)
        expert = jnp.take_along_axis(cand_idx, pos, axis=-1)
        g = jax.nn.softmax(best, axis=-1)
        u = expert_u[expert]
        v = expert_v[expert]
        a = jax.nn.gelu(jnp.einsum('td,thkd->thk', hb, u).astype(jnp.float32), approximate=False)
        return jnp.einsum('thk,thkd->td', (g * a).astype(hb.dtype), v)

    return lax.map(block, tokens).reshape(B, T, D)

def setup_inputs(seed: int = 0) -> dict:
    key = jax.random.key(seed)
    ks = iter(jax.random.split(key, 40))
    nrm = lambda shape, s: jax.random.normal(next(ks), shape, jnp.float32) * s
    gain = lambda shape: 1.0 + nrm(shape, 0.05)
    D = D_MODEL
    return {
        "x": nrm((BATCH, SEQ, D), 1.0),
        "c": nrm((BATCH, D), 1.0),
        "ctx": nrm((BATCH, CTX_LEN, D), 1.0),
        "c_ctx": nrm((D,), 1.0),
        "mod_w": nrm((DEPTH, D, 6 * D), D ** -0.5),
        "mod_b": nrm((DEPTH, 6 * D), 0.02),
        "mix_norm": gain((DEPTH, D)),
        "ffn_norm": gain((DEPTH, D)),
        "even_w_in": nrm((N_EVEN, D, EVEN_IN_W), D ** -0.5),
        "even_w_out": nrm((N_EVEN, EVEN_OUT_W, D), EVEN_OUT_W ** -0.5),
        "a_q_norm": gain((N_EVEN, HEAD_DIM)),
        "a_k_norm": gain((N_EVEN, HEAD_DIM)),
        "b_q_norm": gain((N_EVEN, HEAD_DIM)),
        "b_k_norm": gain((N_EVEN, HEAD_DIM)),
        "b_sink": nrm((N_EVEN, B_HEADS), 0.5),
        "mla_w_in": nrm((N_ODD, D, C_IN_W), D ** -0.5),
        "mla_q_a_norm": gain((N_ODD, C_Q_LORA)),
        "mla_kv_a_norm": gain((N_ODD, C_KV_LORA)),
        "mla_w_uq": nrm((N_ODD, C_Q_LORA, C_HEADS * (C_NOPE + C_ROPE)), C_Q_LORA ** -0.5),
        "mla_w_ukv": nrm((N_ODD, C_KV_LORA, C_HEADS * (C_NOPE + C_V)), C_KV_LORA ** -0.5),
        "mla_q_nope_norm": gain((N_ODD, C_NOPE)),
        "mla_q_rope_norm": gain((N_ODD, C_ROPE)),
        "mla_k_nope_norm": gain((N_ODD, C_NOPE)),
        "mla_k_rope_norm": gain((N_ODD, C_ROPE)),
        "mla_w_out": nrm((N_ODD, C_HEADS * C_V, D), (C_HEADS * C_V) ** -0.5),
        "peer_w_query": nrm((DEPTH, D, PEER_HEADS * PEER_KEY_DIM), D ** -0.5),
        "peer_sub_keys": nrm((DEPTH, PEER_HEADS, 2, PEER_KEYS, PEER_KEY_DIM // 2), (PEER_KEY_DIM // 2) ** -0.5),
        "peer_u": nrm((DEPTH, PEER_EXPERTS, D), D ** -0.5),
        "peer_v": nrm((DEPTH, PEER_EXPERTS, D), PEER_HEADS ** -0.5),
    }

def reference(x, c, ctx, c_ctx, mod_w, mod_b, mix_norm, ffn_norm,
              even_w_in, even_w_out, a_q_norm, a_k_norm, b_q_norm, b_k_norm, b_sink,
              mla_w_in, mla_q_a_norm, mla_kv_a_norm, mla_w_uq, mla_w_ukv,
              mla_q_nope_norm, mla_q_rope_norm, mla_k_nope_norm, mla_k_rope_norm, mla_w_out,
              peer_w_query, peer_sub_keys, peer_u, peer_v):
    n_lat = x.shape[1]
    rows = n_lat // GRID_W
    rope_attn = axial_rope_tables(rows, HEAD_DIM)
    rope_mla = axial_rope_tables(rows, C_ROPE)
    for l in range(DEPTH):
        ctx_out = l < DEPTH - 1
        lat_mod = [m[:, None, :] for m in jnp.split(jax.nn.silu(c) @ mod_w[l] + mod_b[l], 6, axis=-1)]
        ctx_mod = jnp.split(jax.nn.silu(c_ctx) @ mod_w[l] + mod_b[l], 6, axis=-1)
        h_lat = modulate(rmsnorm(x, mix_norm[l]), lat_mod[0], lat_mod[1])
        h_ctx = modulate(rmsnorm(ctx, mix_norm[l]), ctx_mod[0], ctx_mod[1])
        if l % 2 == 0:
            e = l // 2
            o_ctx, o_lat = mixer_even(h_ctx, h_lat, even_w_in[e], even_w_out[e], a_q_norm[e], a_k_norm[e],
                                      b_q_norm[e], b_k_norm[e], b_sink[e], rope_attn, ctx_out)
        else:
            o = l // 2
            o_ctx, o_lat = mixer_mla(h_ctx, h_lat, mla_w_in[o], mla_q_a_norm[o], mla_kv_a_norm[o],
                                     mla_w_uq[o], mla_w_ukv[o], mla_q_nope_norm[o], mla_q_rope_norm[o],
                                     mla_k_nope_norm[o], mla_k_rope_norm[o], mla_w_out[o], rope_mla, ctx_out)
        x = x + lat_mod[2] * o_lat
        x = x + lat_mod[5] * peer_ffn(modulate(rmsnorm(x, ffn_norm[l]), lat_mod[3], lat_mod[4]),
                                      peer_w_query[l], peer_sub_keys[l], peer_u[l], peer_v[l])
        if ctx_out:
            ctx = ctx + ctx_mod[2] * o_ctx
            ctx = ctx + ctx_mod[5] * peer_ffn(modulate(rmsnorm(ctx, ffn_norm[l]), ctx_mod[3], ctx_mod[4]),
                                              peer_w_query[l], peer_sub_keys[l], peer_u[l], peer_v[l])
    return x


_drawn_inputs = setup_inputs


def setup_inputs(seed=0):
    import zlib

    import numpy as np

    out = dict(_drawn_inputs(seed))
    spreads = {}
    factors = {'mix_norm': 2.847,
     'a_q_norm': 4.464,
     'a_k_norm': 4.454,
     'b_q_norm': 4.562,
     'b_k_norm': 4.609,
     'b_sink': 8.0,
     'mla_q_a_norm': 6.796,
     'mla_kv_a_norm': 3.437,
     'mla_q_nope_norm': 7.796,
     'mla_q_rope_norm': 8.0,
     'mla_k_nope_norm': 7.876,
     'mla_k_rope_norm': 8.0}
    for name, (base, spread) in spreads.items():
        noise = np.random.default_rng([zlib.crc32(name.encode()), seed]).standard_normal(out[name].shape)
        drawn = base * np.exp(spread * noise) if base else spread * noise
        out[name] = __import__('jax').numpy.asarray(drawn.astype(out[name].dtype))
    for name, factor in factors.items():
        out[name] = (out[name] * factor).astype(out[name].dtype)
    return out
```

```python
from contextlib import ExitStack

import concourse.bass as bass
from concourse import mybir

F32 = mybir.dt.float32
U32 = mybir.dt.uint32
ALU = mybir.AluOpType
ACT = mybir.ActivationFunctionType
AX = mybir.AxisListType

P = 128
D = 1024
KD = D // P
SEQ, CTX_LEN = 256, 256
LAT_TILES = SEQ // P
TILES = LAT_TILES + CTX_LEN // P
TOK = TILES * P
EPS = 1e-6
MASKED = -1e30
REMOVED = -3.0e38

HD = 64
QKH = 20
QKW = QKH * HD
EVEN_W = QKW + 4 * HD

QL, KVL, ROPE, NOPE, VD, MH = 384, 256, 64, 128, 128, 8
MLA_W = QL + KVL + ROPE

PH, PK, TOPK = 8, 128, 16
HALF = 8
EXPERTS = PK * PK
WCOLS = 256
SLOTS = 4
MODC = 6 * D // (TILES * PH)


def build(nc, a, out):
    with ExitStack() as ctx:
        def sb(name, shape, dt=F32):
            return ctx.enter_context(nc.sbuf_tensor(name, shape, dt))

        def sem(name):
            return ctx.enter_context(nc.semaphore(name))

        x = sb("x", [P, TILES, D])
        h = sb("h", [P, TILES, D])
        hT = sb("hT", [P, 4096])
        arena = sb("arena", [P, 25088])
        weights = sb("weights", [P, SLOTS, KD * WCOLS])
        mod = sb("mod", [P, 4, D])
        gate = sb("gate", [P, 2, D])
        ident = sb("ident", [P, P])
        rope = sb("rope", [P, LAT_TILES, 2, HD])
        wmask = sb("wmask", [P, 2, P])
        sinks = sb("sinks", [P, 2, 8])
        cond = sb("cond", [P, 3, KD * 2])
        stat = sb("stat", [P, 64])
        heads_stat = sb("heads_stat", [P, 2, 80])
        soft = sb("soft", [P, 4, 64])
        eps = sb("eps", [P, 1])
        iota16 = sb("iota16", [P, TOPK])

        w0 = ctx.enter_context(nc.psum_tensor("w0", [P, 1024], F32))
        w1 = ctx.enter_context(nc.psum_tensor("w1", [P, 1024], F32))
        work = (w0, w1)
        ps_s = ctx.enter_context(nc.psum_tensor("ps_s", [P, 2, 512], F32))
        ps_o = ctx.enter_context(nc.psum_tensor("ps_o", [P, 1024], F32))

        mod_rows = nc.dram_tensor("mod_rows", (2, 2, 6 * D), F32).ap()

        def view(base, at, *dims):
            n = 1
            for d in dims:
                n *= d
            v = base[:, at:at + n]
            if len(dims) == 2:
                v = v.rearrange("p (a b) -> p a b", b=dims[1])
            if len(dims) == 3:
                v = v.rearrange("p (a b c) -> p a b c", b=dims[1], c=dims[2])
            if len(dims) == 4:
                v = v.rearrange("p (a b c d) -> p a b c d", b=dims[1], c=dims[2], d=dims[3])
            return v

        hTk = view(hT, 0, KD, TOK)
        probs = view(arena, 16384, 2, 512)
        probsT = view(arena, 17408, 2, 512)
        o_sb = view(arena, 18432, 1024)
        gated = view(arena, 19456, TILES, WCOLS)
        row = view(arena, 20480, D)
        bias = view(arena, 21504, D)
        gain = view(arena, 22528, D)
        pj = view(arena, 0, TILES, EVEN_W)
        qkT = view(arena, 6144, QKH // 2, TOK)
        sq = view(arena, 11264, TILES, QKW)
        gain_qk = view(arena, 23552, QKW)
        pm = view(arena, 0, TILES, MLA_W)
        qm = view(arena, 2816, LAT_TILES, MH * (NOPE + ROPE))
        kn = view(arena, 5888, TILES, MH * NOPE)
        vm = view(arena, 9984, TILES, MH * VD)
        qnT = view(arena, 14080, MH, SEQ)
        sq1 = view(arena, 16384, 2048)
        cqT = view(arena, 19456, QL // P, SEQ)
        qpT = view(arena, 20480, MH // 2, SEQ)
        ckvT = view(arena, 21504, KVL // P, TOK)
        gain_m = view(arena, 23552, 1024)
        kpT = view(arena, 24576, TOK)
        knT = h[:, :, :].rearrange("p a b -> p (a b)").rearrange("p (h t) -> p h t", t=TOK)
        urows = view(arena, 0, HALF, D)
        vrows = view(arena, 8192, HALF, D)
        queryT = view(arena, 16384, TILES * PH + 1, 2 * P)
        modf = mod[:, :, :].rearrange("p a b -> p (a b)")
        keysT = view(modf, 0, PH + 1, 2 * P)
        mod_w1 = view(modf, 2304, KD, MODC)
        diag = view(hT, 0, HALF, P)
        q_now = view(hT, 1024, 2, P)
        left = view(hT, 1280, 2, P)
        cand = view(hT, 1536, TOPK, TOPK)
        cand_left = view(hT, 1792, 256)
        onehot = view(hT, 2048, 2, TOPK, TOPK)
        top_v = view(hT, 2560, 2, TOPK)
        top_i = view(hT, 2592, 2, TOPK).bitcast(U32)
        top_if = view(hT, 2624, 2, TOPK)
        best_v = view(hT, 2656, TOPK)
        best_p = view(hT, 2672, TOPK).bitcast(U32)
        pos_u = view(hT, 2688, 2, TOPK).bitcast(U32)
        pos_f = view(hT, 2720, 2, TOPK)
        picked = view(hT, 2752, 2, TOPK)
        flat = view(hT, 2784, TOPK)
        idx = view(hT, 2800, TOPK).bitcast(U32)
        idx_u = view(hT, 2816, TOPK).bitcast(U32)
        idx_v = view(hT, 2832, TOPK).bitcast(U32)
        neg_best = view(hT, 2848, 1)
        esum = view(hT, 2849, 1)
        erec = view(hT, 2850, 1)
        expv = view(hT, 2852, TOPK)
        g_next = view(hT, 2868, TOPK)
        g_now = view(hT, 2884, TOPK)
        dots = view(hT, 2900, 2, HALF)
        acts = view(hT, 2916, 2, HALF)
        wts = view(hT, 2932, 2, HALF)
        row1 = view(hT, 2948, MODC)
        bias1 = view(hT, 3140, MODC)
        y_gated = view(arena, 0, D)

        jobs = {}
        emptied_by = {"act": 0, "dve": 0}

        def plan(name, engine):
            emptied_by[engine] += 1
            jobs[name] = (len(jobs), engine, emptied_by[engine])

        units0 = [(t, k) for t in range(TILES) for k in range(16)]
        units1 = [(t, k) for t in range(LAT_TILES) for k in range(MH)]
        for p in range(2):
            plan(("mod", p), "dve")
        for t in range(TILES):
            plan(("hT", 0, t), "act")
        for c in range(EVEN_W // WCOLS):
            plan(("proj", c), "dve" if c % 2 else "act")
        for p in range(2, 6):
            plan(("mod", p), "dve")
        for t in range(TILES):
            plan(("qkT", t, 0), "act")
            plan(("qkT", t, 1), "dve")
        for n, (t, k) in enumerate(units0):
            plan(("PT", 0, n), "dve" if n % 2 else "act")
            if k == 15:
                plan(("OT", 0, t), "act")
        for c in range(D // WCOLS):
            plan(("out", 0, c), "dve")
        for t in range(TILES):
            plan(("hT2", 0, t), "act")
        for k in range(PH):
            plan(("query", 0, k), "dve" if k % 2 else "act")
        for t in range(TILES):
            plan(("hT", 1, t), "act")
        for c in range(3):
            plan(("down", c), "dve" if c % 2 else "act")
        for t in range(TILES):
            plan(("latT", t), "act")
        for c in range(3):
            plan(("uq", c), "dve" if c % 2 else "act")
        for c in range(2):
            for t in range(TILES):
                plan(("ukv", c, t), "dve" if t % 2 else "act")
        for t in range(LAT_TILES):
            plan(("qnT", t), "act")
            plan(("qpT", t), "dve")
        for t in range(TILES):
            plan(("knT", t), "act")
        for n, (t, k) in enumerate(units1):
            plan(("PT", 1, n), "dve" if n % 2 else "act")
            if k == MH - 1:
                plan(("OT", 1, t), "act")
        for c in range(D // WCOLS):
            plan(("out", 1, c), "dve")
        for t in range(LAT_TILES):
            plan(("hT2", 1, t), "act")
        for k in range(PH):
            plan(("query", 1, k), "dve" if k % 2 else "act")

        def cols(w, kk, n, width):
            return w.rearrange("(k p) n -> p k n", p=P)[:, 0:kk, n:n + width]

        stream = []
        for p in (0, 1):
            stream += [(("mod", p, c), cols(a["mod_w"][0], KD, p * D + c * WCOLS, WCOLS)) for c in range(4)]
        stream += [(("proj", c), cols(a["even_w_in"], KD, c * WCOLS, WCOLS)) for c in range(EVEN_W // WCOLS)]
        for p in range(2, 6):
            stream += [(("mod", p, c), cols(a["mod_w"][0], KD, p * D + c * WCOLS, WCOLS)) for c in range(4)]
        stream += [(("out", 0, c), cols(a["even_w_out"], KD, c * WCOLS, WCOLS)) for c in range(D // WCOLS)]
        stream += [(("query", 0, c), cols(a["peer_w_query"][0], KD, c * WCOLS, WCOLS)) for c in range(PH)]
        stream += [(("down", c), cols(a["mla_w_in"], KD, c * WCOLS, min(WCOLS, MLA_W - c * WCOLS)))
                   for c in range(3)]
        stream += [(("uq", c), cols(a["mla_w_uq"], QL // P, c * 512, 512)) for c in range(3)]
        stream += [(("ukv", c), cols(a["mla_w_ukv"], KVL // P, c * D, D)) for c in range(2)]
        stream += [(("out", 1, c), cols(a["mla_w_out"], KD, c * WCOLS, WCOLS)) for c in range(D // WCOLS)]
        stream += [(("query", 1, c), cols(a["peer_w_query"][1], KD, c * WCOLS, WCOLS)) for c in range(PH)]
        place = {name: i for i, (name, _) in enumerate(stream)}

        def chunk(name):
            _, kk, width = stream[place[name]][1].shape
            return view(weights[:, place[name] % SLOTS, :], 0, kk, width)

        consts_in = sem("consts_in")
        made = sem("made")
        cond_exp = sem("cond_exp")
        cond_silu = sem("cond_silu")
        w_in = [sem(f"w_in{s}") for s in range(SLOTS)]
        w_used = sem("w_used")
        filled = sem("filled")
        act_emptied = sem("act_emptied")
        dve_emptied = sem("dve_emptied")
        bias_in = sem("bias_in")
        row_out = sem("row_out")
        mod_in = {k: sem(f"in_{k}") for k in ("mix0", "gate0", "ffn0", "gate0b", "mix1", "gate1", "ffn1", "gate1b")}
        mod_made = sem("mod_made")
        sumsq = sem("sumsq")
        h_made = sem("h_made")
        sq_made = sem("sq_made")
        sq_read = sem("sq_read")
        ss_made = sem("ss_made")
        root_made = sem("root_made")
        roped = sem("roped")
        scores_made = sem("scores_made")
        scores_biased = sem("scores_biased")
        probs_made = sem("probs_made")
        pv_done = sem("pv_done")
        sink_shift = sem("sink_shift")
        sink_exp = sem("sink_exp")
        o_made = sem("o_made")
        x_mixed = sem("x_mixed")
        keys_in = sem("keys_in")
        q_copied = sem("q_copied")
        keys_scored = sem("keys_scored")
        scores_taken = sem("scores_taken")
        best_made = sem("best_made")
        best_exp = sem("best_exp")
        idx_made = sem("idx_made")
        idx_taken = sem("idx_taken")
        idx_staged = sem("idx_staged")
        u_in = [sem(f"u_in{j}") for j in range(HALF)]
        v_in = [sem(f"v_in{j}") for j in range(HALF)]
        u_used = sem("u_used")
        v_used = sem("v_used")
        acts_made = sem("acts_made")
        wts_made = sem("wts_made")
        diag_made = sem("diag_made")
        y_read = sem("y_read")
        mod1_in = sem("mod1_in")
        mod1_sum = sem("mod1_sum")
        mod1_row = sem("mod1_row")
        mod1_out = sem("mod1_out")
        out_done = sem("out_done")
        held = {e: sem(f"held_{e}") for e in ("act", "dve", "pool")}

        block = ctx.enter_context(nc.Block())

        def wait_filled(eng, name):
            eng.wait_ge(filled, jobs[name][0] + 1)

        def wait_emptied(eng, name):
            _, engine, count = jobs[name]
            eng.wait_ge(act_emptied if engine == "act" else dve_emptied, count)

        def wait_multiplied(eng, name):
            if name[0] == "mod" and name[2] < 3:
                eng.wait_ge(w_used, 3 * name[1] + name[2] + 1)
            elif name[0] == "mod":
                wait_filled(eng, name[:2])
            elif name[0] == "ukv":
                wait_filled(eng, (*name, TILES - 1))
            else:
                wait_filled(eng, name)

        names = list(jobs)

        def buffer_free(pe, name):
            n = jobs[name][0]
            if n >= 2:
                wait_emptied(pe, names[n - 2])

        def buffer(name):
            return work[jobs[name][0] % 2]

        heads_before = (0, TILES * PH)
        peer_tiles = (TILES, LAT_TILES)
        n_const_loads = 8

        LOADS = {"mix0": 5, "gate0": 2, "ffn0": 5, "gate0b": 2, "mix1": 5, "gate1": 1, "ffn1": 3, "gate1b": 1}

        def wait_mod(eng, what):
            eng.wait_ge(mod_in[what], 16 * LOADS[what])

        H_MADE = {(0, 0): 4, (0, 1): 8, (1, 0): 12, (1, 1): 14}

        def experts_pool(pool, layer):
            G0 = heads_before[layer]
            pool.wait_ge(h_made, H_MADE[layer, 1])
            pool.dma_start(keysT[:, 0:PH, :], a["keysT"][layer]).then_inc(keys_in, 16)
            pool.dma_start(keysT[:, PH, :], a["keysT"][layer][:, 0, :]).then_inc(keys_in, 16)

            def gather(dst, table, index, landed):
                pool.indirect_dma_start(dst, None, table, bass.IndirectOffsetOnAxis(ap=index, axis=0)).then_inc(landed, 16)

            def gather_u(G, half, j, free):
                if free:
                    pool.wait_ge(u_used, 16 * G + (HALF * (half - 1) + j + 1))
                    pool.sem_inc(held["pool"], 1)
                gather(urows[:, j, :], a["peer_u"], idx_u[:, half * HALF + j:half * HALF + j + 1], u_in[j])

            def gather_v(G, half, j, free):
                if free:
                    pool.wait_ge(v_used, 16 * G + (HALF * (half - 1) + j + 1))
                    pool.sem_inc(held["pool"], 1)
                gather(vrows[:, j, :], a["peer_v"], idx_v[:, half * HALF + j:half * HALF + j + 1], v_in[j])

            def head(G, first):
                free = not (first and layer == 0)
                pool.wait_ge(idx_made, G + (layer + 1))
                pool.sem_inc(held["pool"], 1)
                if not first:
                    pool.tensor_copy(idx_v[:, HALF:TOPK], idx_u[:, HALF:TOPK]).then_inc(idx_staged, 1)
                pool.tensor_copy(idx_u[:, 0:HALF], idx[:, 0:HALF]).then_inc(idx_staged, 1)
                pool.wait_ge(idx_staged, 3 * G + 1)
                pool.sem_inc(held["pool"], 1)
                for j in range(HALF):
                    gather_u(G, 0, j, free)
                    if not first:
                        gather_v(G - 1, 1, j, True)
                pool.tensor_copy(idx_u[:, HALF:TOPK], idx[:, HALF:TOPK]).then_inc(idx_taken, 1)
                pool.tensor_copy(idx_v[:, 0:HALF], idx_u[:, 0:HALF]).then_inc(idx_staged, 1)
                pool.wait_ge(idx_taken, G + 1)
                pool.sem_inc(held["pool"], 1)
                pool.wait_ge(idx_staged, 3 * G + 2)
                pool.sem_inc(held["pool"], 1)
                for j in range(HALF):
                    gather_u(G, 1, j, True)
                    gather_v(G, 0, j, free)

            n_heads = peer_tiles[layer] * PH
            head(G0, True)
            with pool.Fori(1, n_heads, 1) as n:
                head(n + G0, False)
            G = G0 + n_heads
            pool.tensor_copy(idx_v[:, HALF:TOPK], idx_u[:, HALF:TOPK]).then_inc(idx_staged, 1)
            pool.wait_ge(idx_staged, 3 * G)
            for j in range(HALF):
                gather_v(G - 1, 1, j, True)

        def keys_of(layer, t):
            return TOK if t < LAT_TILES else CTX_LEN

        def empty_query(eng, layer, k):
            tiles = peer_tiles[layer]
            name = ("query", layer, k)
            src = buffer(name)[:, :].rearrange("p (s t n) -> p t s n", s=2, n=P)[:, 0:tiles]
            dst = view(arena, 16384, tiles, PH, 2, P)[:, :, k]
            if eng is nc.scalar:
                return eng.activation(dst, src, ACT.Copy)
            return eng.tensor_copy(dst, src)

        def experts_act(act, layer):
            G0 = heads_before[layer]
            n_heads = peer_tiles[layer] * PH

            def copy_query(G, n):
                if not (isinstance(G, int) and G == 0):
                    act.wait_ge(keys_scored, G)
                    act.sem_inc(held["act"], 1)
                act.activation(q_now, queryT[:, bass.ds(n, 1), :].rearrange("p a (s t) -> p (a s) t", t=P),
                               ACT.Copy).then_inc(q_copied, 1)

            def exp_best(G):
                act.wait_ge(best_made, G + 1)
                act.activation(expv, best_v, ACT.Exp, bias=neg_best, accum_out=esum).then_inc(best_exp, 1)

            def gelu(G, half):
                act.wait_ge(u_used, 16 * G + HALF * (half + 1))
                act.activation(acts[:, half, :], dots[:, half, :], ACT.Gelu).then_inc(acts_made, 1)

            def diags(G, half):
                act.wait_ge(wts_made, 2 * G + half + 1)
                for j in range(HALF):
                    if isinstance(G, int):
                        used = 16 * G + HALF * half - HALF + j + 1
                    else:
                        used = 16 * G + (HALF * half - HALF + j + 1)
                    if not (isinstance(used, int) and used <= 0):
                        act.wait_ge(v_used, used)
                    act.activation(diag[:, j, :], ident[:, :], ACT.Copy,
                                   scale=wts[:, half, j:j + 1]).then_inc(diag_made, 1)

            wait_emptied(act, ("query", layer, PH - 1))
            wait_filled(act, ("query", layer, PH - 1))
            act.drain()
            act.activation(queryT[:, n_heads, :], queryT[:, 0, :], ACT.Copy)
            act.drain()
            E0 = G0 + layer
            copy_query(E0, 0)
            exp_best(E0)
            def body(n, first):
                G = G0 + n
                if not first:
                    gelu(G - 1, 1)
                    diags(G - 1, 1)
                copy_query(E0 + n + 1, n + 1)
                exp_best(E0 + n + 1)
                gelu(G, 0)
                diags(G, 0)
            body(0, True)
            with act.Fori(1, n_heads, 1) as n:
                body(n, False)
            gelu(G0 + n_heads - 1, 1)
            diags(G0 + n_heads - 1, 1)

        def experts_pe(pe, layer, silu):
            G0 = heads_before[layer]
            E0 = G0 + layer
            tiles = peer_tiles[layer]

            def score_keys(E, k):
                pe.wait_ge(q_copied, E + 1)
                if not (isinstance(E, int) and E == 0):
                    pe.wait_ge(scores_taken, E)
                for s in range(2):
                    keys = keysT[:, bass.ds(k, 1), s * P:(s + 1) * P].rearrange("p a n -> p (a n)")
                    mm = pe.matmul(ps_s[:, 0, s * P:(s + 1) * P], q_now[:, s, :], keys, start=True, stop=True)
                mm.then_inc(keys_scored, 1)

            def sum_half(G, half, starts, stops):
                for j in range(HALF):
                    pe.wait_ge(v_in[j], 16 * (2 * G + half) + 16)
                    pe.wait_ge(diag_made, 16 * G + (HALF * half + j + 1))
                    for b in range(2):
                        mm = pe.matmul(ps_o[:, b * 512:(b + 1) * 512], diag[:, j, :], vrows[:, j, b * 512:(b + 1) * 512],
                                       start=(starts and j == 0), stop=(stops and j == HALF - 1), skip_group_check=True)
                    mm.then_inc(v_used, 1)

            def mod_strip(n):
                pe.wait_ge(mod1_in, 32 * n + 32)
                if not isinstance(n, int):
                    pe.wait_ge(mod1_row, n)
                elif n:
                    pe.wait_ge(mod1_row, n)
                for k in range(KD):
                    mm = pe.matmul(ps_s[0:2, 1, 0:MODC], silu[:, k, :], mod_w1[:, k, :],
                                   start=(k == 0), stop=(k == KD - 1))
                mm.then_inc(mod1_sum, 1)

            pe.wait_ge(keys_in, 32 * (layer + 1))
            score_keys(E0, 0)
            for t in range(tiles):
                n0 = t * PH
                score_keys(E0 + n0 + 1, 1)
                if t:
                    sum_half(G0 + n0 - 1, 1, False, True)
                    pe.wait_ge(y_read, (0 if layer == 0 else TILES) + t)
                sum_half(G0 + n0, 0, True, False)
                if layer == 0:
                    mod_strip(n0)
                with pe.Fori(1, PH, 1) as k:
                    score_keys(k + (E0 + n0 + 1), k + 1)
                    sum_half(k + (G0 + n0 - 1), 1, False, False)
                    sum_half(k + (G0 + n0), 0, False, False)
                    if layer == 0:
                        mod_strip(k + n0)
            sum_half(G0 + tiles * PH - 1, 1, False, True)

        def experts_dve(dve, layer):
            G0 = heads_before[layer]
            E0 = G0 + layer
            tiles = peer_tiles[layer]

            def choose(E):
                s = ps_s[:, 0, 0:2 * P].rearrange("p (s n) -> p s n", n=PK)
                dve.wait_ge(keys_scored, E + 1)
                dve.sem_inc(held["dve"], 1)
                for i in range(2):
                    dve.max(top_v[:, i, 0:8], s[:, i, :])
                dve.drain()
                for i in range(2):
                    dve.max_index(top_i[:, i, 0:8], top_v[:, i, 0:8], s[:, i, :])
                    ins = dve.match_replace(left[:, i, :], top_v[:, i, 0:8], s[:, i, :], REMOVED)
                ins.then_inc(scores_taken, 1)
                dve.drain()
                for i in range(2):
                    dve.max(top_v[:, i, 8:16], left[:, i, :])
                dve.drain()
                for i in range(2):
                    dve.max_index(top_i[:, i, 8:16], top_v[:, i, 8:16], left[:, i, :])
                dve.tensor_tensor(cand, top_v[:, 0, :].unsqueeze(2).broadcast_to([P, TOPK, TOPK]),
                                  top_v[:, 1, :].unsqueeze(1).broadcast_to([P, TOPK, TOPK]), ALU.add)
                dve.drain()
                dve.tensor_copy(top_if, top_i)
                flat_cand = cand.rearrange("p a b -> p (a b)")
                dve.max(best_v[:, 0:8], flat_cand)
                dve.drain()
                dve.max_index(best_p[:, 0:8], best_v[:, 0:8], flat_cand)
                dve.match_replace(cand_left, best_v[:, 0:8], flat_cand, REMOVED)
                dve.tensor_scalar(neg_best, best_v[:, 0:1], -1.0, None, ALU.mult)
                dve.drain()
                dve.max(best_v[:, 8:16], cand_left).then_inc(best_made, 1)
                dve.drain()
                dve.max_index(best_p[:, 8:16], best_v[:, 8:16], cand_left)
                dve.drain()
                dve.tensor_scalar(pos_u[:, 0, :], best_p, 4, None, ALU.logical_shift_right)
                dve.tensor_scalar(pos_u[:, 1, :], best_p, 15, None, ALU.bitwise_and)
                dve.drain()
                dve.tensor_copy(pos_f, pos_u)
                dve.drain()
                dve.tensor_tensor(onehot.rearrange("p s k a -> p (s k) a"),
                                  pos_f.rearrange("p s k -> p (s k)").unsqueeze(2).broadcast_to([P, 2 * TOPK, TOPK]),
                                  iota16[:, :].unsqueeze(1).broadcast_to([P, 2 * TOPK, TOPK]), ALU.is_equal)
                dve.drain()
                dve.tensor_tensor(onehot, onehot, top_if.unsqueeze(2).broadcast_to([P, 2, TOPK, TOPK]), ALU.mult)
                dve.drain()
                dve.tensor_reduce(picked.rearrange("p s k -> p (s k)"), onehot.rearrange("p s k a -> p (s k) a"),
                                  AX.X, ALU.add)
                dve.drain()
                dve.scalar_tensor_tensor(out=flat, in0=picked[:, 0, :], scalar=float(PK), in1=picked[:, 1, :],
                                         op0=ALU.mult, op1=ALU.add)
                dve.drain()
                if not (isinstance(E, int) and E == 0):
                    dve.wait_ge(idx_taken, E - layer)
                dve.tensor_scalar(idx, flat, float(layer * EXPERTS), None, ALU.add).then_inc(idx_made, 1)
                dve.wait_ge(best_exp, E + 1)
                dve.reciprocal(erec, esum)
                dve.drain()
                dve.tensor_scalar(g_next, expv, erec, None, ALU.mult)
                dve.drain()

            def dot(G, half, t, js):
                for j in js:
                    dve.wait_ge(u_in[j], 16 * (2 * G + half) + 16)
                    if j == 0 and not (isinstance(G, int) and G == 0):
                        dve.wait_ge(acts_made, 2 * G + half - 1)
                    u = urows[:, j, :]
                    dve.tensor_tensor_reduce(out=u, in0=u, in1=h[:, t, :], scale=1.0, scalar=0.0, op0=ALU.mult,
                                             op1=ALU.add, accum_out=dots[:, half, j:j + 1]).then_inc(u_used, 1)

            def weigh(G, half):
                dve.wait_ge(acts_made, 2 * G + half + 1)
                if not (isinstance(G, int) and G == 0):
                    dve.wait_ge(diag_made, 16 * G + (HALF * half - HALF))
                dve.tensor_tensor(wts[:, half, :], acts[:, half, :], g_now[:, half * HALF:(half + 1) * HALF],
                                  ALU.mult).then_inc(wts_made, 1)

            def add_tile(t):
                dve.wait_ge(v_used, 16 * (G0 + (t + 1) * PH))
                wait_mod(dve, f"gate{layer}b")
                y = h[:, t, :]
                dve.tensor_tensor(y, ps_o[:, :], gate[:, t // LAT_TILES, :], ALU.mult)
                dve.drain()
                dve.tensor_tensor(x[:, t, :], x[:, t, :], y, ALU.add).then_inc(y_read, 1)
                dve.drain()

            def strip(n):
                dve.wait_ge(mod1_sum, n + 1)
                dve.wait_ge(mod1_in, 32 * n + 32)
                if not (isinstance(n, int) and n == 0):
                    dve.wait_ge(mod1_out, 16 * n)
                dve.tensor_tensor(row1[0:2, :], ps_s[0:2, 1, 0:MODC], bias1[0:2, :], ALU.add).then_inc(mod1_row, 1)

            def head(n, t, first, in_tile):
                G = n + G0
                if first:
                    dot(G, 0, t, range(HALF))
                    dve.tensor_copy(g_now, g_next)
                    dve.drain()
                    choose(n + (E0 + 1))
                else:
                    dot(G, 0, t, range(4))
                    weigh(G - 1, 1)
                    dve.drain()
                    dve.tensor_copy(g_now, g_next)
                    dve.drain()
                    choose(n + (E0 + 1))
                    dot(G, 0, t, range(4, HALF))
                dot(G, 1, t, range(4))
                weigh(G, 0)
                if not in_tile and t:
                    add_tile(t - 1)
                dot(G, 1, t, range(4, HALF))
                if layer == 0:
                    strip(n)

            choose(E0)
            for t in range(tiles):
                head(t * PH, t, t == 0, False)
                with dve.Fori(1, PH, 1) as k:
                    head(k + t * PH, t, False, True)
            weigh(G0 + tiles * PH - 1, 1)
            add_tile(tiles - 1)
        @block.sync
        def _(sp):
            sp.dma_start(cond[:, 0, :], a["cond"]).then_inc(consts_in, 16)
            for t in range(LAT_TILES):
                sp.dma_start(x[:, t, :], a["x"][t * P:(t + 1) * P, :]).then_inc(consts_in, 16)
                sp.dma_start(x[:, LAT_TILES + t, :], a["ctx"][t * P:(t + 1) * P, :]).then_inc(consts_in, 16)
            sp.dma_start(rope[:, :, :, :], a["rope"]).then_inc(consts_in, 16)
            sp.dma_start(wmask[:, :, :], a["wmask"]).then_inc(consts_in, 16)
            sp.dma_start(sinks[:, 0, :], a["b_sink"].partition_broadcast(P)).then_inc(consts_in, 16)

            def load(names_):
                for name in names_:
                    i = place[name]
                    if i >= SLOTS:
                        wait_multiplied(sp, order[i - SLOTS])
                    sp.dma_start(chunk(name), stream[i][1]).then_inc(w_in[i % SLOTS], 16)

            order = [name for name, _ in stream]
            first1 = place[("down", 0)]
            load(order[:first1])
            sp.wait_ge(h_made, H_MADE[0, 1])
            wait_filled(sp, ("query", 0, PH - 1))

            def strip(n, first):
                at = bass.ds(n * MODC, MODC)
                if not first:
                    sp.wait_ge(mod1_sum, n)
                sp.dma_start(mod_w1, a["mod_w"][1].rearrange("(k p) n -> p k n", p=P)[:, :, at]).then_inc(mod1_in, 16)
                if not first:
                    sp.wait_ge(mod1_row, n)
                sp.dma_start(bias1[0:2, :], a["mod_b2"][1, :, at]).then_inc(mod1_in, 16)
                sp.wait_ge(mod1_row, n + 1)
                sp.dma_start(mod_rows[1, :, at], row1[0:2, :]).then_inc(mod1_out, 16)

            strip(0, True)
            with sp.Fori(1, TILES * PH, 1) as n:
                strip(n, False)
            load(order[first1:])
            for t in range(LAT_TILES):
                sp.wait_ge(y_read, TILES + t + 1)
                sp.dma_start(out[t * P:(t + 1) * P, :], x[:, t, :]).then_inc(out_done, 16)
            sp.wait_ge(out_done, 16 * LAT_TILES)
            sp.wait_ge(mod1_out, 16 * TILES * PH)

        @block.gpsimd
        def _(pool):
            pool.memset(ident[:, :], 0.0).then_inc(made, 1)
            pool.wait_ge(made, 1)
            pool.affine_select(out=ident[:, :], in_=ident[:, :], compare_op=ALU.not_equal, fill=1.0,
                               base=0, pattern=[[-1, P]], channel_multiplier=1).then_inc(made, 1)
            pool.iota(iota16[:, :], [[1, TOPK]], base=0, channel_multiplier=0,
                      allow_small_or_imprecise_dtypes=True).then_inc(made, 1)
            pool.memset(eps[:, :], EPS).then_inc(made, 1)

            def broadcast(what, dst, src):
                pool.dma_start(dst, src.partition_broadcast(P)).then_inc(mod_in[what], 16)

            def piece(layer, who, p):
                return mod_rows[layer, who, p * D:(p + 1) * D]

            def make_rows(pieces):
                for p in pieces:
                    if p:
                        pool.wait_ge(dve_emptied, jobs[("mod", p - 1)][2])
                    pool.dma_start(bias[0:2, :], a["mod_b2"][0, :, p * D:(p + 1) * D]).then_inc(bias_in, 16)
                    wait_emptied(pool, ("mod", p))
                    pool.dma_start(mod_rows[0, :, p * D:(p + 1) * D], row[0:2, :]).then_inc(row_out, 16)
                    pool.wait_ge(row_out, 16 * (p + 1))

            broadcast("mix0", gain, a["mix_norm"][0])
            pool.dma_start(gain_qk, a["gain_qk"].partition_broadcast(P)).then_inc(bias_in, 16)
            make_rows((0, 1))
            for who in range(2):
                broadcast("mix0", mod[:, 2 * who, :], piece(0, who, 1))
                broadcast("mix0", mod[:, 2 * who + 1, :], piece(0, who, 0))
            make_rows((2, 3, 4, 5))
            for who in range(2):
                broadcast("gate0", gate[:, who, :], piece(0, who, 2))
            pool.wait_ge(h_made, H_MADE[0, 0])
            broadcast("ffn0", gain, a["ffn_norm"][0])
            for who in range(2):
                broadcast("ffn0", mod[:, 2 * who, :], piece(0, who, 4))
                broadcast("ffn0", mod[:, 2 * who + 1, :], piece(0, who, 3))
            pool.wait_ge(x_mixed, D // WCOLS)
            for who in range(2):
                broadcast("gate0b", gate[:, who, :], piece(0, who, 5))
            experts_pool(pool, 0)
            pool.wait_ge(y_read, TILES)
            pool.wait_ge(mod1_out, 16 * TILES * PH)
            broadcast("mix1", gain, a["mix_norm"][1])
            for who in range(2):
                broadcast("mix1", mod[:, 2 * who, :], piece(1, who, 1))
                broadcast("mix1", mod[:, 2 * who + 1, :], piece(1, who, 0))
            broadcast("gate1", gate[:, 0, :], piece(1, 0, 2))
            pool.dma_start(gain_m, a["gain_m"].partition_broadcast(P)).then_inc(bias_in, 16)
            pool.wait_ge(h_made, H_MADE[1, 0])
            broadcast("ffn1", gain, a["ffn_norm"][1])
            broadcast("ffn1", mod[:, 0, :], piece(1, 0, 4))
            broadcast("ffn1", mod[:, 1, :], piece(1, 0, 3))
            pool.wait_ge(x_mixed, 2 * D // WCOLS)
            broadcast("gate1b", gate[:, 0, :], piece(1, 0, 5))
            experts_pool(pool, 1)

        @block.scalar
        def _(act):
            act.wait_ge(consts_in, 16 * n_const_loads)
            act.wait_ge(made, 4)
            act.activation(cond[:, 1, :], cond[:, 0, :], ACT.Exp, scale=-1.0).then_inc(cond_exp, 1)

            def empty(name, dst, src):
                wait_filled(act, name)
                act.activation(dst, src, ACT.Copy).then_inc(act_emptied, 1)

            def rms(tiles, base):
                for n, t in enumerate(tiles):
                    act.activation(h[:, t, :], x[:, t, :], ACT.Square, accum_out=stat[:, t:t + 1])
                act.drain()
                act.activation(stat[:, 8:8 + len(tiles)], stat[:, tiles[0]:tiles[0] + len(tiles)], ACT.Sqrt,
                               bias=eps[:, :], scale=1.0 / D).then_inc(sumsq, 1)

            def empty_hT(layer, kind, tiles):
                for t in tiles:
                    name = (kind, layer, t)
                    empty(name, hTk[:, :, t * P:(t + 1) * P],
                          buffer(name)[:, :].rearrange("p (k t) -> p k t", t=P))

            def attention(layer, units, scale, sink):
                last = 16 if layer == 0 else MH
                base = 0 if layer == 0 else len(units0)
                for n, (t, k) in enumerate(units):
                    N = base + n
                    act.wait_ge(scores_biased, N + 1)
                    if n >= 2:
                        act.wait_ge(filled, jobs[("PT", layer, n - 2)][0] + 1)
                    kk = keys_of(layer, t)
                    act.activation(probs[:, n % 2, 0:kk], ps_s[:, n % 2, 0:kk], ACT.Exp, scale=scale,
                                   bias=soft[:, 1, n:n + 1], accum_out=soft[:, 2, n:n + 1]).then_inc(probs_made, 1)
                    if n % 2 == 0:
                        if n >= 2:
                            act.wait_ge(pv_done, N - 1)
                        name = ("PT", layer, n)
                        empty(name, probsT[:, n % 2, 0:kk], buffer(name)[:, 0:kk])
                    if k == last - 1:
                        if sink:
                            act.wait_ge(sink_shift, t + 1)
                            act.activation(stat[:, 24:32], stat[:, 16:24], ACT.Exp).then_inc(sink_exp, 1)
                        name = ("OT", layer, t)
                        empty(name, hTk[:, :, t * P:(t + 1) * P],
                              buffer(name)[:, :].rearrange("p (k t) -> p k t", t=P))

            def empty_queries(layer, parity=0):
                for k in range(0, PH, 2):
                    name = ("query", layer, k)
                    wait_filled(act, name)
                    empty_query(act, layer, k).then_inc(act_emptied, 1)

            rms(range(TILES), 0)
            act.wait_ge(h_made, H_MADE[0, 0])
            empty_hT(0, "hT", range(TILES))
            for c in range(0, EVEN_W // WCOLS, 2):
                name = ("proj", c)
                empty(name, pj[:, :, c * WCOLS:(c + 1) * WCOLS],
                      buffer(name)[:, :].rearrange("p (t n) -> p t n", n=WCOLS))
            wait_emptied(act, ("proj", 5))
            act.drain()
            for t in range(TILES):
                act.activation(sq[:, t, :], pj[:, t, 0:QKW], ACT.Square).then_inc(sq_made, 1)
            act.wait_ge(ss_made, 1)
            act.activation(heads_stat[:, 1, :], heads_stat[:, 0, :], ACT.Sqrt, bias=eps[:, :],
                           scale=1.0 / HD).then_inc(root_made, 1)
            for t in range(TILES):
                name = ("qkT", t, 0)
                empty(name, qkT[:, 0:8, t * P:(t + 1) * P], buffer(name)[:, :].rearrange("p (k t) -> p k t", t=P))
            attention(0, units0, HD ** -0.5, True)
            act.wait_ge(x_mixed, D // WCOLS)
            rms(range(TILES), 0)
            empty_hT(0, "hT2", range(TILES))
            empty_queries(0)
            experts_act(act, 0)
            act.wait_ge(y_read, TILES)
            rms(range(TILES), 0)
            empty_hT(1, "hT", range(TILES))
            for c in (0, 2):
                name = ("down", c)
                width = chunk(name).shape[2]
                empty(name, pm[:, :, c * WCOLS:c * WCOLS + width],
                      buffer(name)[:, :].rearrange("p (t n) -> p t n", n=WCOLS)[:, :, 0:width])
            wait_emptied(act, ("down", 1))
            act.drain()
            squares = [(pm[:, t, :], MLA_W) for t in range(TILES)]
            n_sq = TILES
            for n, (src, width) in enumerate(squares):
                if n:
                    act.wait_ge(sq_read, n)
                act.activation(sq1[:, 0:width], src, ACT.Square).then_inc(sq_made, 1)
            act.wait_ge(sq_read, n_sq)
            for c, width in enumerate((QL, KVL, ROPE)):
                ins = act.activation(heads_stat[:, 1, c * 4:c * 4 + 4], heads_stat[:, 0, c * 4:c * 4 + 4], ACT.Sqrt,
                                     bias=eps[:, :], scale=1.0 / width)
            ins.then_inc(root_made, 1)
            for t in range(TILES):
                name = ("latT", t)
                b = buffer(name)[:, :].rearrange("p (k t) -> p k t", t=P)
                wait_filled(act, name)
                at = slice(t * P, (t + 1) * P)
                if t < LAT_TILES:
                    act.activation(cqT[:, :, at], b[:, 0:3, :], ACT.Copy)
                act.activation(ckvT[:, :, at], b[:, 3:5, :], ACT.Copy)
                act.activation(kpT[:, at], b[:, 5, :], ACT.Copy).then_inc(act_emptied, 1)
            for c in (0, 2):
                name = ("uq", c)
                empty(name, qm[:, :, c * 512:(c + 1) * 512], buffer(name)[:, :].rearrange("p (t n) -> p t n", n=512))
            for c, dst in enumerate((kn, vm)):
                for t in range(0, TILES, 2):
                    empty(("ukv", c, t), dst[:, t, :], buffer(("ukv", c, t))[:, :])
            act.drain()
            wait_emptied(act, ("ukv", 1, 3))
            for t in range(LAT_TILES):
                act.wait_ge(sq_read, n_sq + t)
                act.activation(sq1[:, 0:1536], qm[:, t, :], ACT.Square).then_inc(sq_made, 1)
            for t in range(TILES):
                act.wait_ge(sq_read, n_sq + LAT_TILES + t)
                act.activation(sq1[:, 0:D], kn[:, t, :], ACT.Square).then_inc(sq_made, 1)
            act.wait_ge(sq_read, n_sq + LAT_TILES + TILES)
            act.activation(heads_stat[:, 1, 0:48], heads_stat[:, 0, 0:48], ACT.Sqrt, bias=eps[:, :], scale=1.0 / NOPE)
            act.activation(heads_stat[:, 1, 48:64], heads_stat[:, 0, 48:64], ACT.Sqrt, bias=eps[:, :],
                           scale=1.0 / ROPE).then_inc(root_made, 1)
            for t in range(LAT_TILES):
                name = ("qnT", t)
                empty(name, qnT[:, :, t * P:(t + 1) * P], buffer(name)[:, :].rearrange("p (k t) -> p k t", t=P))
            for t in range(TILES):
                name = ("knT", t)
                empty(name, knT[:, :, t * P:(t + 1) * P], buffer(name)[:, :].rearrange("p (k t) -> p k t", t=P))
            attention(1, units1, (NOPE + ROPE) ** -0.5, False)
            act.wait_ge(x_mixed, 2 * D // WCOLS)
            rms(range(LAT_TILES), 0)
            empty_hT(1, "hT2", range(LAT_TILES))
            empty_queries(1)
            experts_act(act, 1)

        @block.tensor
        def _(pe):
            pe.wait_ge(consts_in, 16 * n_const_loads)
            pe.wait_ge(made, 4)
            pe.wait_ge(cond_silu, 1)
            silu = cond[:, 2, :].rearrange("p (k w) -> p k w", w=2)

            def wait_chunk(name):
                i = place[name]
                pe.wait_ge(w_in[i % SLOTS], 16 * (i // SLOTS + 1))

            def mod_rows_job(p):
                name = ("mod", p)
                buffer_free(pe, name)
                for c in range(4):
                    wait_chunk(("mod", p, c))
                    for k in range(KD):
                        mm = pe.matmul(buffer(name)[0:2, c * WCOLS:(c + 1) * WCOLS], silu[:, k, :],
                                       chunk(("mod", p, c))[:, k, :], start=(k == 0), stop=(k == KD - 1))
                    mm.then_inc(w_used if c < 3 else filled, 1)

            def transposes(name, sources):
                buffer_free(pe, name)
                for n, src in enumerate(sources):
                    mm = pe.transpose(buffer(name)[:, n * P:n * P + P], src, ident[:, :])
                mm.then_inc(filled, 1)

            def product_all(name, c_name, tiles, width, kk, lhs):
                buffer_free(pe, name)
                wait_chunk(c_name)
                w = chunk(c_name)
                for n, t in enumerate(tiles):
                    for k in range(kk):
                        mm = pe.matmul(buffer(name)[:, n * WCOLS:n * WCOLS + width], lhs[:, k, t * P:(t + 1) * P],
                                       w[:, k, :], start=(k == 0), stop=(k == kk - 1))
                mm.then_inc(filled, 1)

            def turn_h(layer, kind, tiles, made_):
                for n, t in enumerate(tiles):
                    pe.wait_ge(h_made, made_ - len(tiles) + n + 1)
                    transposes((kind, layer, t), [h[:, t, k * P:(k + 1) * P] for k in range(KD)])

            def attention(layer, units):
                last = 16 if layer == 0 else MH
                base = 0 if layer == 0 else len(units0)

                def scores(n):
                    t, k = units[n]
                    if base + n >= 2:
                        pe.wait_ge(probs_made, base + n - 1)
                    q_at = slice(t * P, (t + 1) * P)
                    k_at = slice(0, TOK) if t < LAT_TILES else slice(SEQ, TOK)
                    kk = keys_of(layer, t)
                    dst = ps_s[:, n % 2, 0:kk]
                    if layer == 0:
                        g, kh = divmod(k, 8)
                        half = slice(HD * (kh % 2), HD * (kh % 2) + HD)
                        mm = pe.matmul(dst, qkT[half, 5 * g + kh // 2, q_at], qkT[half, 5 * g + 4, k_at],
                                       start=True, stop=True)
                    else:
                        half = slice(ROPE * (k % 2), ROPE * (k % 2) + ROPE)
                        pe.matmul(dst, qnT[:, k, q_at], knT[:, k, k_at], start=True, stop=False)
                        mm = pe.matmul(dst, qpT[half, k // 2, q_at], kpT[half, k_at], start=False, stop=True)
                    mm.then_inc(scores_made, 1)

                scores(0)
                for n, (t, k) in enumerate(units):
                    if n + 1 < len(units):
                        scores(n + 1)
                    kk = keys_of(layer, t)
                    pe.wait_ge(probs_made, base + n + 1)
                    transposes(("PT", layer, n), [probs[:, n % 2, i * P:(i + 1) * P] for i in range(kk // P)])
                    wait_emptied(pe, ("PT", layer, n))
                    if k == 0:
                        o_before = t if layer == 0 else TILES + t
                        if o_before:
                            pe.wait_ge(o_made, o_before)
                    for i in range(kk // P):
                        key_tile = i if t < LAT_TILES else LAT_TILES + i
                        if layer == 0:
                            g, kh = divmod(k, 8)
                            v_at = QKW + 2 * HD * g + HD * (kh % 2)
                            rhs = pj[:, key_tile, v_at:v_at + HD]
                            o_at = slice(k * HD, (k + 1) * HD)
                        else:
                            rhs = vm[:, key_tile, k * VD:(k + 1) * VD]
                            o_at = slice(k * VD, (k + 1) * VD)
                        mm = pe.matmul(ps_o[:, o_at], probsT[:, n % 2, i * P:(i + 1) * P], rhs,
                                       start=(i == 0), stop=(i == kk // P - 1))
                    mm.then_inc(pv_done, 1)
                    if k == last - 1:
                        pe.wait_ge(o_made, (0 if layer == 0 else TILES) + t + 1)
                        transposes(("OT", layer, t), [o_sb[:, i * P:(i + 1) * P] for i in range(KD)])

            def queries(layer):
                tiles = peer_tiles[layer]
                wait_emptied(pe, ("hT2", layer, tiles - 1))
                for k in range(PH):
                    name = ("query", layer, k)
                    buffer_free(pe, name)
                    wait_chunk(name)
                    for s in range(2):
                        for kk in range(KD):
                            mm = pe.matmul(buffer(name)[:, s * 512:s * 512 + tiles * P],
                                           chunk(name)[:, kk, s * P:(s + 1) * P], hTk[:, kk, 0:tiles * P],
                                           start=(kk == 0), stop=(kk == KD - 1))
                    mm.then_inc(filled, 1)

            for p in range(2):
                mod_rows_job(p)
            turn_h(0, "hT", range(TILES), H_MADE[0, 0])
            wait_emptied(pe, ("hT", 0, TILES - 1))
            for c in range(EVEN_W // WCOLS):
                product_all(("proj", c), ("proj", c), range(TILES), WCOLS, KD, hTk)
            for p in range(2, 6):
                mod_rows_job(p)
            for t in range(TILES):
                pe.wait_ge(roped, t + 1)
                blocks = [pj[:, t, k * P:(k + 1) * P] for k in range(QKH // 2)]
                transposes(("qkT", t, 0), blocks[:8])
                transposes(("qkT", t, 1), blocks[8:])
            wait_emptied(pe, ("qkT", TILES - 1, 0))
            wait_emptied(pe, ("qkT", TILES - 1, 1))
            attention(0, units0)
            wait_emptied(pe, ("OT", 0, TILES - 1))
            for c in range(D // WCOLS):
                product_all(("out", 0, c), ("out", 0, c), range(TILES), WCOLS, KD, hTk)
            turn_h(0, "hT2", range(TILES), H_MADE[0, 1])
            queries(0)
            experts_pe(pe, 0, silu)
            turn_h(1, "hT", range(TILES), H_MADE[1, 0])
            wait_emptied(pe, ("hT", 1, TILES - 1))
            for c in range(3):
                product_all(("down", c), ("down", c), range(TILES), chunk(("down", c)).shape[2], KD, hTk)
            for t in range(TILES):
                pe.wait_ge(roped, TILES + t + 1)
                name = ("latT", t)
                buffer_free(pe, name)
                for n in range(0 if t < LAT_TILES else 3, 5):
                    pe.transpose(buffer(name)[:, n * P:(n + 1) * P], pm[:, t, n * P:(n + 1) * P], ident[:, :])
                pe.transpose(buffer(name)[:, 5 * P:6 * P], o_sb[:, t * P:(t + 1) * P], ident[:, :]).then_inc(filled, 1)
            wait_emptied(pe, ("latT", TILES - 1))
            for c in range(3):
                name = ("uq", c)
                buffer_free(pe, name)
                wait_chunk(name)
                for t in range(LAT_TILES):
                    for k in range(QL // P):
                        mm = pe.matmul(buffer(name)[:, t * 512:(t + 1) * 512], cqT[:, k, t * P:(t + 1) * P],
                                       chunk(name)[:, k, :], start=(k == 0), stop=(k == QL // P - 1))
                mm.then_inc(filled, 1)
            for c in range(2):
                wait_chunk(("ukv", c))
                for t in range(TILES):
                    name = ("ukv", c, t)
                    buffer_free(pe, name)
                    for half in range(2):
                        for k in range(KVL // P):
                            mm = pe.matmul(buffer(name)[:, half * 512:(half + 1) * 512], ckvT[:, k, t * P:(t + 1) * P],
                                           chunk(("ukv", c))[:, k, half * 512:(half + 1) * 512],
                                           start=(k == 0), stop=(k == KVL // P - 1))
                    mm.then_inc(filled, 1)
            for t in range(LAT_TILES):
                pe.wait_ge(roped, 2 * TILES + t + 1)
                transposes(("qnT", t), [qm[:, t, k * P:(k + 1) * P] for k in range(MH)])
                transposes(("qpT", t), [qm[:, t, (MH + k) * P:(MH + k + 1) * P] for k in range(MH // 2)])
            for t in range(TILES):
                pe.wait_ge(roped, 2 * TILES + LAT_TILES + t + 1)
                transposes(("knT", t), [kn[:, t, k * P:(k + 1) * P] for k in range(MH)])
            wait_emptied(pe, ("knT", TILES - 1))
            wait_emptied(pe, ("qpT", LAT_TILES - 1))
            attention(1, units1)
            wait_emptied(pe, ("OT", 1, LAT_TILES - 1))
            for c in range(D // WCOLS):
                product_all(("out", 1, c), ("out", 1, c), range(LAT_TILES), WCOLS, KD, hTk)
            turn_h(1, "hT2", range(LAT_TILES), H_MADE[1, 1])
            queries(1)
            experts_pe(pe, 1, silu)

        @block.vector
        def _(dve):
            dve.wait_ge(consts_in, 16 * n_const_loads)
            dve.wait_ge(made, 4)
            dve.wait_ge(cond_exp, 1)
            dve.tensor_scalar(cond[:, 1, :], cond[:, 1, :], 1.0, None, ALU.add)
            dve.tensor_scalar(sinks[:, 1, :], sinks[:, 0, :], -1.0, None, ALU.mult)
            dve.drain()
            dve.reciprocal(cond[:, 1, :], cond[:, 1, :])
            dve.drain()
            dve.tensor_tensor(cond[:, 2, :], cond[:, 0, :], cond[:, 1, :], ALU.mult).then_inc(cond_silu, 1)

            def empty(name, dst, src):
                wait_filled(dve, name)
                dve.tensor_copy(dst, src).then_inc(dve_emptied, 1)

            def empty_mod(p):
                name = ("mod", p)
                wait_filled(dve, name)
                dve.wait_ge(bias_in, 16 * (p + 2))
                if p:
                    dve.wait_ge(row_out, 16 * p)
                dve.tensor_tensor(row[0:2, :], buffer(name)[0:2, :], bias[0:2, :], ALU.add).then_inc(dve_emptied, 1)

            def norm(landed, tiles, count):
                wait_mod(dve, landed)
                for who in range(2 if len(tiles) > LAT_TILES else 1):
                    dve.scalar_tensor_tensor(out=mod[:, 2 * who, :], in0=mod[:, 2 * who, :], scalar=1.0, in1=gain,
                                             op0=ALU.add, op1=ALU.mult)
                dve.wait_ge(sumsq, count)
                dve.reciprocal(stat[:, 8:8 + len(tiles)], stat[:, 8:8 + len(tiles)])
                dve.drain()
                for t in tiles:
                    who = t // LAT_TILES
                    dve.scalar_tensor_tensor(out=h[:, t, :], in0=x[:, t, :], scalar=stat[:, 8 + t:9 + t],
                                             in1=mod[:, 2 * who, :], op0=ALU.mult, op1=ALU.mult)
                    dve.drain()
                    dve.tensor_tensor(h[:, t, :], h[:, t, :], mod[:, 2 * who + 1, :], ALU.add).then_inc(h_made, 1)

            def turn(v, t, n_heads, width=HD):
                cs = rope[:, t, 0, :].unsqueeze(1).broadcast_to([P, n_heads, width])
                sn = rope[:, t, 1, :].rearrange("p (i two) -> p i two", two=2)
                pairs = v.rearrange("p h (i two) -> p h i two", two=2)
                tmp = view(sq_tmp(n_heads), 0, n_heads, width)
                tpairs = tmp.rearrange("p h (i two) -> p h i two", two=2)
                for e in range(2):
                    dve.tensor_tensor(tpairs[:, :, :, e], pairs[:, :, :, 1 - e],
                                      sn[:, :, e].unsqueeze(1).broadcast_to([P, n_heads, width // 2]), ALU.mult)
                dve.drain()
                dve.tensor_tensor(v, v, cs, ALU.mult)
                dve.drain()
                return dve.tensor_tensor(v, v, tmp, ALU.add)

            def sq_tmp(n_heads):
                return arena[:, 11264:11264 + n_heads * HD] if n_heads == QKH else arena[:, 18432 + 512:18432 + 512 + n_heads * HD]

            def scale_heads(v, stats, gains):
                heads, width = v.shape[1], v.shape[2]
                dve.tensor_tensor(v, v, stats.unsqueeze(2).broadcast_to([P, heads, width]), ALU.mult)
                dve.drain()
                return dve.tensor_tensor(v, v, gains, ALU.mult)

            def attention(layer, units, scale, sink):
                last = 16 if layer == 0 else MH
                base = 0 if layer == 0 else len(units0)
                width = HD if layer == 0 else VD
                for n, (t, k) in enumerate(units):
                    N = base + n
                    kk = keys_of(layer, t)
                    s = ps_s[:, n % 2, 0:kk]
                    dve.wait_ge(scores_made, N + 1)
                    if sink and k >= 8 and t < LAT_TILES:
                        other = 1 - t
                        dve.tensor_tensor(s[:, other * P:(other + 1) * P], s[:, other * P:(other + 1) * P],
                                          wmask[:, t, :], ALU.add)
                        dve.drain()
                    dve.tensor_reduce(soft[:, 0, n:n + 1], s, AX.X, ALU.max, negate=True)
                    dve.drain()
                    if sink and k >= 8:
                        dve.tensor_scalar(soft[:, 1, n:n + 1], soft[:, 0, n:n + 1], scale, sinks[:, 1, k - 8:k - 7],
                                          ALU.mult, ALU.min).then_inc(scores_biased, 1)
                    else:
                        dve.tensor_scalar(soft[:, 1, n:n + 1], soft[:, 0, n:n + 1], scale, None,
                                          ALU.mult).then_inc(scores_biased, 1)
                    if n >= 1 and (n - 1) % 2 == 1:
                        empty_probs(layer, n - 1)
                    if k == last - 1:
                        if n % 2 == 1:
                            empty_probs(layer, n, True)
                        first = n - last + 1
                        dve.wait_ge(probs_made, N + 1)
                        if sink:
                            dve.tensor_tensor(stat[:, 16:24], soft[:, 1, first + 8:n + 1], sinks[:, 0, :],
                                              ALU.add).then_inc(sink_shift, 1)
                            dve.wait_ge(sink_exp, t + 1)
                            dve.tensor_tensor(soft[:, 2, first + 8:n + 1], soft[:, 2, first + 8:n + 1],
                                              stat[:, 24:32], ALU.add)
                            dve.drain()
                        dve.reciprocal(soft[:, 3, first:n + 1], soft[:, 2, first:n + 1])
                        dve.drain()
                        dve.wait_ge(pv_done, N + 1)
                        if t or layer:
                            before = ("OT", 0, t - 1) if layer == 0 else (("OT", 1, t - 1) if t else ("latT", TILES - 1))
                            wait_filled(dve, before)
                        dve.tensor_tensor(o_sb.rearrange("p (k w) -> p k w", w=width),
                                          ps_o[:, :].rearrange("p (k w) -> p k w", w=width),
                                          soft[:, 3, first:n + 1].unsqueeze(2).broadcast_to([P, last, width]),
                                          ALU.mult).then_inc(o_made, 1)

            done_probs = set()

            def empty_probs(layer, n, force=False):
                if (layer, n) in done_probs:
                    return
                done_probs.add((layer, n))
                base = 0 if layer == 0 else len(units0)
                units = units0 if layer == 0 else units1
                kk = keys_of(layer, units[n][0])
                if n >= 2:
                    dve.wait_ge(pv_done, base + n - 1)
                name = ("PT", layer, n)
                empty(name, probsT[:, n % 2, 0:kk], buffer(name)[:, 0:kk])

            def add_mixed(layer, tiles):
                for c in range(D // WCOLS):
                    name = ("out", layer, c)
                    b = buffer(name)[:, :].rearrange("p (t n) -> p t n", n=WCOLS)
                    wait_filled(dve, name)
                    if c == 0:
                        wait_mod(dve, f"gate{layer}")
                    at = slice(c * WCOLS, (c + 1) * WCOLS)
                    for who in range(tiles // LAT_TILES):
                        ts = slice(who * LAT_TILES, (who + 1) * LAT_TILES)
                        ins = dve.tensor_tensor(gated[:, ts, :], b[:, ts, :],
                                                gate[:, who, at].unsqueeze(1).broadcast_to([P, LAT_TILES, WCOLS]), ALU.mult)
                    ins.then_inc(dve_emptied, 1)
                    dve.drain()
                    dve.tensor_tensor(x[:, 0:tiles, at], x[:, 0:tiles, at], gated[:, 0:tiles, :],
                                      ALU.add).then_inc(x_mixed, 1)
                    dve.drain()

            def empty_queries(layer):
                for k in range(1, PH, 2):
                    wait_filled(dve, ("query", layer, k))
                    empty_query(dve, layer, k).then_inc(dve_emptied, 1)

            for p in range(2):
                empty_mod(p)
            norm("mix0", range(TILES), 1)
            for c in range(1, EVEN_W // WCOLS, 2):
                name = ("proj", c)
                empty(name, pj[:, :, c * WCOLS:(c + 1) * WCOLS],
                      buffer(name)[:, :].rearrange("p (t n) -> p t n", n=WCOLS))
            for p in range(2, 6):
                empty_mod(p)
            for t in range(TILES):
                dve.wait_ge(sq_made, t + 1)
                ins = dve.tensor_reduce(heads_stat[:, 0, t * QKH:(t + 1) * QKH],
                                        sq[:, t, :].rearrange("p (h w) -> p h w", w=HD), AX.X, ALU.add)
            ins.then_inc(ss_made, 1)
            dve.wait_ge(root_made, 1)
            dve.reciprocal(heads_stat[:, 1, :], heads_stat[:, 1, :])
            dve.drain()
            for t in range(TILES):
                v = pj[:, t, 0:QKW].rearrange("p (h w) -> p h w", w=HD)
                ins = scale_heads(v, heads_stat[:, 1, t * QKH:(t + 1) * QKH],
                                  gain_qk.rearrange("p (h w) -> p h w", w=HD))
                if t < LAT_TILES:
                    dve.drain()
                    ins = turn(v, t, QKH)
                ins.then_inc(roped, 1)
            for t in range(TILES):
                name = ("qkT", t, 1)
                empty(name, qkT[:, 8:10, t * P:(t + 1) * P],
                      buffer(name)[:, 0:2 * P].rearrange("p (k t) -> p k t", t=P))
            attention(0, units0, HD ** -0.5, True)
            add_mixed(0, TILES)
            norm("ffn0", range(TILES), 2)
            empty_queries(0)
            experts_dve(dve, 0)
            norm("mix1", range(TILES), 3)
            name = ("down", 1)
            empty(name, pm[:, :, WCOLS:2 * WCOLS], buffer(name)[:, :].rearrange("p (t n) -> p t n", n=WCOLS))
            for t in range(TILES):
                dve.wait_ge(sq_made, TILES + t + 1)
                at = 0
                for c, width in enumerate((QL, KVL, ROPE)):
                    ins = dve.tensor_reduce(heads_stat[:, 0, c * 4 + t:c * 4 + t + 1], sq1[:, at:at + width], AX.X, ALU.add)
                    at += width
                ins.then_inc(sq_read, 1)
            dve.wait_ge(root_made, 2)
            dve.reciprocal(heads_stat[:, 1, 0:12], heads_stat[:, 1, 0:12])
            dve.drain()
            dve.wait_ge(bias_in, 16 * 8)
            for t in range(TILES):
                at = 0
                for c, width in enumerate((QL, KVL, ROPE)):
                    dve.scalar_tensor_tensor(out=pm[:, t, at:at + width], in0=pm[:, t, at:at + width],
                                             scalar=heads_stat[:, 1, c * 4 + t:c * 4 + t + 1], in1=gain_m[:, at:at + width],
                                             op0=ALU.mult, op1=ALU.mult)
                    at += width
                dve.drain()
                kp = pm[:, t, QL + KVL:MLA_W].unsqueeze(1)
                if t < LAT_TILES:
                    turn(kp, t, 1)
                    dve.drain()
                dve.tensor_copy(o_sb[:, t * P:(t + 1) * P].rearrange("p (two w) -> p two w", two=2),
                                kp.broadcast_to([P, 2, ROPE])).then_inc(roped, 1)
                dve.drain()
            name = ("uq", 1)
            empty(name, qm[:, :, 512:1024], buffer(name)[:, :].rearrange("p (t n) -> p t n", n=512))
            for c, dst in enumerate((kn, vm)):
                for t in range(1, TILES, 2):
                    empty(("ukv", c, t), dst[:, t, :], buffer(("ukv", c, t))[:, :])
            for t in range(LAT_TILES):
                dve.wait_ge(sq_made, 2 * TILES + t + 1)
                dve.tensor_reduce(heads_stat[:, 0, t * MH:(t + 1) * MH],
                                  sq1[:, 0:D].rearrange("p (h w) -> p h w", w=NOPE), AX.X, ALU.add)
                dve.tensor_reduce(heads_stat[:, 0, 48 + t * MH:48 + (t + 1) * MH],
                                  sq1[:, D:D + MH * ROPE].rearrange("p (h w) -> p h w", w=ROPE), AX.X,
                                  ALU.add).then_inc(sq_read, 1)
            for t in range(TILES):
                dve.wait_ge(sq_made, 2 * TILES + LAT_TILES + t + 1)
                ins = dve.tensor_reduce(heads_stat[:, 0, 16 + t * MH:16 + (t + 1) * MH],
                                        sq1[:, 0:D].rearrange("p (h w) -> p h w", w=NOPE), AX.X, ALU.add)
                ins.then_inc(sq_read, 1)
            dve.wait_ge(root_made, 3)
            dve.reciprocal(heads_stat[:, 1, 0:64], heads_stat[:, 1, 0:64])
            dve.drain()
            g_at = MLA_W
            gains = [gain_m[:, g_at:g_at + NOPE], gain_m[:, g_at + NOPE:g_at + NOPE + ROPE],
                     gain_m[:, g_at + NOPE + ROPE:g_at + 2 * NOPE + ROPE]]

            def over_heads(g):
                return g.unsqueeze(1).broadcast_to([P, MH, g.shape[1]])

            for t in range(LAT_TILES):
                v = qm[:, t, 0:D].rearrange("p (h w) -> p h w", w=NOPE)
                scale_heads(v, heads_stat[:, 1, t * MH:(t + 1) * MH], over_heads(gains[0]))
                v = qm[:, t, D:D + MH * ROPE].rearrange("p (h w) -> p h w", w=ROPE)
                scale_heads(v, heads_stat[:, 1, 48 + t * MH:48 + (t + 1) * MH], over_heads(gains[1]))
                dve.drain()
                turn(v, t, MH).then_inc(roped, 1)
                dve.drain()
            for t in range(TILES):
                v = kn[:, t, :].rearrange("p (h w) -> p h w", w=NOPE)
                scale_heads(v, heads_stat[:, 1, 16 + t * MH:16 + (t + 1) * MH], over_heads(gains[2])).then_inc(roped, 1)
            for t in range(LAT_TILES):
                name = ("qpT", t)
                empty(name, qpT[:, :, t * P:(t + 1) * P],
                      buffer(name)[:, 0:4 * P].rearrange("p (k t) -> p k t", t=P))
            attention(1, units1, (NOPE + ROPE) ** -0.5, False)
            add_mixed(1, LAT_TILES)
            norm("ffn1", range(LAT_TILES), 4)
            empty_queries(1)
            experts_dve(dve, 1)



def kernel(**inputs):
    import numpy as np
    import concourse.bacc as bacc
    from concourse.bass_utils import run_bass_kernel_spmd as run

    i = {k: np.asarray(v) for k, v in inputs.items()}
    layers = 2
    pair = [0, 4, 1, 5, 2, 6, 3, 7]
    head_cols = lambda at, hs: [at + h * 64 + j for h in hs for j in range(64)]
    A_Q, A_K, A_V, B_Q, B_K, B_V = 0, 512, 640, 768, 1280, 1408
    cols = (head_cols(A_Q, pair) + head_cols(A_K, [0, 1]) + head_cols(B_Q, pair) + head_cols(B_K, [0, 1])
            + head_cols(A_V, [0, 1]) + head_cols(B_V, [0, 1]))
    rows = head_cols(0, pair) + head_cols(512, pair)
    gain_qk = np.concatenate([np.tile(i["a_q_norm"][0], 8), np.tile(i["a_k_norm"][0], 2),
                              np.tile(i["b_q_norm"][0], 8), np.tile(i["b_k_norm"][0], 2)])
    uq = i["mla_w_uq"][0].reshape(384, 8, 192)
    uq = np.concatenate([uq[:, :, :128].reshape(384, -1), uq[:, :, 128:].reshape(384, -1)], 1)
    ukv = i["mla_w_ukv"][0].reshape(256, 8, 256)
    ukv = np.concatenate([ukv[:, :, :128].reshape(256, -1), ukv[:, :, 128:].reshape(256, -1)], 1)
    gain_m = np.concatenate([i["mla_q_a_norm"][0], i["mla_kv_a_norm"][0], i["mla_k_rope_norm"][0],
                             i["mla_q_nope_norm"][0], i["mla_q_rope_norm"][0], i["mla_k_nope_norm"][0]])
    pos = np.arange(256)
    inv = (np.float32(10000.0) ** (-np.arange(0, 32, 2, dtype=np.float32) / np.float32(32))).astype(np.float32)
    ang = np.concatenate([(pos // 64).astype(np.float32)[:, None] * inv,
                          (pos % 64).astype(np.float32)[:, None] * inv], 1)
    cos, sin = np.cos(ang), np.sin(ang)
    rope = np.stack([np.repeat(cos, 2, 1), np.stack([-sin, sin], -1).reshape(256, 64)], 1)
    rope = rope.reshape(2, 128, 2, 64).transpose(1, 0, 2, 3)
    q, k = np.arange(128)[:, None], np.arange(128)[None, :]
    wmask = np.stack([np.where(k <= q, 0, MASKED), np.where(k >= q, 0, MASKED)], 1).astype(np.float32)
    keysT = i["peer_sub_keys"].transpose(0, 4, 1, 2, 3).reshape(layers, 128, 8, 256)
    arrays = {
        "x": i["x"][0], "ctx": i["ctx"][0],
        "cond": np.stack([i["c"][0], i["c_ctx"]]).reshape(2, 8, 128).transpose(2, 1, 0).reshape(128, 16),
        "mod_w": i["mod_w"], "mod_b2": np.repeat(i["mod_b"][:, None], 2, 1),
        "mix_norm": i["mix_norm"], "ffn_norm": i["ffn_norm"],
        "even_w_in": i["even_w_in"][0][:, cols], "even_w_out": i["even_w_out"][0][rows],
        "gain_qk": gain_qk, "b_sink": i["b_sink"][0][pair], "rope": rope, "wmask": wmask,
        "mla_w_in": i["mla_w_in"][0], "mla_w_uq": uq, "mla_w_ukv": ukv, "mla_w_out": i["mla_w_out"][0],
        "gain_m": gain_m, "peer_w_query": i["peer_w_query"], "keysT": keysT,
        "peer_u": i["peer_u"].reshape(-1, 1024), "peer_v": i["peer_v"].reshape(-1, 1024),
    }
    arrays = {k: np.ascontiguousarray(v) for k, v in arrays.items()}
    nc = bacc.Bacc("TRN2", target_bir_lowering=False, num_devices=1)
    aps = {k: nc.dram_tensor(f"in_{k}", v.shape, mybir.dt.from_np(v.dtype), kind="ExternalInput").ap()
           for k, v in arrays.items()}
    out = nc.dram_tensor("out", (256, 1024), F32, kind="ExternalOutput").ap()
    build(nc, aps, out)
    r = run(nc, [{f"in_{k}": v for k, v in arrays.items()}], core_ids=[0])
    return np.asarray(r.results[0]["out"]).reshape(1, 256, 1024)
```

```python
from contextlib import ExitStack

import concourse.bass as bass
from concourse import mybir

F32 = mybir.dt.float32
U32 = mybir.dt.uint32
ALU = mybir.AluOpType
ACT = mybir.ActivationFunctionType
AX = mybir.AxisListType

P = 128
D = 1024
KD = D // P
SEQ, CTX_LEN = 256, 256
LAT_TILES = SEQ // P
TILES = LAT_TILES + CTX_LEN // P
TOK = TILES * P
EPS = 1e-6
MASKED = -1e30
REMOVED = -3.0e38

HD = 64
QKH = 20
QKW = QKH * HD
EVEN_W = QKW + 4 * HD

QL, KVL, ROPE, NOPE, VD, MH = 384, 256, 64, 128, 128, 8
MLA_W = QL + KVL + ROPE

PH, PK, TOPK = 8, 128, 16
HALF = 8
EXPERTS = PK * PK
WCOLS = 256
SLOTS = 4
MODC = 6 * D // (TILES * PH)


def build(nc, a, out):
    with ExitStack() as ctx:
        def sb(name, shape, dt=F32):
            return ctx.enter_context(nc.sbuf_tensor(name, shape, dt))

        def sem(name):
            return ctx.enter_context(nc.semaphore(name))

        x = sb("x", [P, TILES, D])
        h = sb("h", [P, TILES, D])
        hT = sb("hT", [P, 4096])
        arena = sb("arena", [P, 25088])
        weights = sb("weights", [P, SLOTS, KD * WCOLS])
        mod = sb("mod", [P, 4, D])
        gate = sb("gate", [P, 2, D])
        ident = sb("ident", [P, P])
        ones = sb("ones", [P, P])
        rope = sb("rope", [P, LAT_TILES, 2, HD])
        wmask = sb("wmask", [P, 2, P])
        sinks = sb("sinks", [P, 2, 8])
        cond = sb("cond", [P, 3, KD * 2])
        stat = sb("stat", [P, 64])
        heads_stat = sb("heads_stat", [P, 2, 80])
        soft = sb("soft", [P, 4, 64])
        eps = sb("eps", [P, 1])
        iota16 = sb("iota16", [P, TOPK])

        w0 = ctx.enter_context(nc.psum_tensor("w0", [P, 1024], F32))
        w1 = ctx.enter_context(nc.psum_tensor("w1", [P, 1024], F32))
        work = (w0, w1)
        ps_s = ctx.enter_context(nc.psum_tensor("ps_s", [P, 2, 512], F32))
        ps_o = ctx.enter_context(nc.psum_tensor("ps_o", [P, 1024], F32))

        mod_rows = nc.dram_tensor("mod_rows", (2, 2, 6 * D), F32).ap()

        def view(base, at, *dims):
            n = 1
            for d in dims:
                n *= d
            v = base[:, at:at + n]
            if len(dims) == 2:
                v = v.rearrange("p (a b) -> p a b", b=dims[1])
            if len(dims) == 3:
                v = v.rearrange("p (a b c) -> p a b c", b=dims[1], c=dims[2])
            if len(dims) == 4:
                v = v.rearrange("p (a b c d) -> p a b c d", b=dims[1], c=dims[2], d=dims[3])
            return v

        hTk = view(hT, 0, KD, TOK)
        probs = view(arena, 16384, 2, 512)
        probsT = view(arena, 17408, 2, 512)
        o_sb = view(arena, 18432, 1024)
        gated = view(arena, 19456, TILES, WCOLS)
        row = view(arena, 20480, D)
        bias = view(arena, 21504, D)
        mod_acc = view(arena, 20480, 2, 2, 512)
        bias_acc = view(arena, 16384, 3 * D)
        gain = view(arena, 22528, D)
        pj = view(arena, 0, TILES, EVEN_W)
        qkT = view(arena, 6144, QKH // 2, TOK)
        sq = view(arena, 11264, TILES, QKW)
        gain_qk = view(arena, 23552, QKW)
        pm = view(arena, 0, TILES, MLA_W)
        qm = view(arena, 2816, LAT_TILES, MH * (NOPE + ROPE))
        kn = view(arena, 5888, TILES, MH * NOPE)
        vm = view(arena, 9984, TILES, MH * VD)
        qnT = view(arena, 14080, MH, SEQ)
        sq1 = view(arena, 16384, 2048)
        cqT = view(arena, 19456, QL // P, SEQ)
        qpT = view(arena, 20480, MH // 2, SEQ)
        ckvT = view(arena, 21504, KVL // P, TOK)
        gain_m = view(arena, 23552, 1024)
        kpT = view(arena, 24576, TOK)
        knT = h[:, :, :].rearrange("p a b -> p (a b)").rearrange("p (h t) -> p h t", t=TOK)
        urows = view(arena, 0, HALF, D)
        vrows = view(arena, 8192, HALF, D)
        queryT = view(arena, 16384, TILES * PH + 1, 2 * P)
        modf = mod[:, :, :].rearrange("p a b -> p (a b)")
        keysT = view(modf, 0, PH + 1, 2 * P)
        mod_w1 = view(modf, 2304, KD, MODC)
        scratch = weights[:, 0:2, :].rearrange("p s n -> p (s n)")
        query_w = view(weights[:, 2, :], 0, KD, WCOLS)
        diag = view(scratch, 0, HALF, P)
        q_now = view(scratch, 1024, 2, P)
        left = view(scratch, 1280, 2, P)
        cand = view(scratch, 1536, TOPK, TOPK)
        cand_left = view(scratch, 1792, 256)
        onehot = view(scratch, 2048, 2, TOPK, TOPK)
        top_v = view(scratch, 2560, 2, TOPK)
        top_i = view(scratch, 2592, 2, TOPK).bitcast(U32)
        top_if = view(scratch, 2624, 2, TOPK)
        best_v = view(scratch, 2656, TOPK)
        best_p = view(scratch, 2672, TOPK).bitcast(U32)
        pos_u = view(scratch, 2688, 2, TOPK).bitcast(U32)
        pos_f = view(scratch, 2720, 2, TOPK)
        picked = view(scratch, 2752, 2, TOPK)
        flat = view(scratch, 2784, TOPK)
        idx = view(scratch, 2800, TOPK).bitcast(U32)
        idx_u = view(scratch, 2816, TOPK).bitcast(U32)
        idx_v = view(scratch, 2832, TOPK).bitcast(U32)
        neg_best = view(scratch, 2848, 1)
        esum = view(scratch, 2849, 1)
        erec = view(scratch, 2850, 1)
        expv = view(scratch, 2852, TOPK)
        g_next = view(scratch, 2868, TOPK)
        g_now = view(scratch, 2884, TOPK)
        dots = view(scratch, 2900, 2, HALF)
        acts = view(scratch, 2916, 2, HALF)
        wts = view(scratch, 2932, 2, HALF)
        row1 = view(scratch, 2948, MODC)
        bias1 = view(scratch, 3140, MODC)

        jobs = {}
        emptied_by = {"act": 0, "dve": 0}

        def plan(name, engine):
            emptied_by[engine] += 1
            jobs[name] = (len(jobs), engine, emptied_by[engine])

        units0 = [(t, k) for t in range(TILES) for k in range(16)]
        units1 = [(t, k) for t in range(LAT_TILES) for k in range(MH)]

        def plan_attention(layer, units):
            for n in range(len(units)):
                plan(("PT", layer, n), "act")
                if n >= 2 and ends_tile(units, n - 2):
                    plan(("OT", layer, units[n - 2][0]), "act")
            plan(("OT", layer, units[-1][0]), "act")

        def ends_tile(units, n):
            return n + 1 < len(units) and units[n + 1][0] != units[n][0]

        for p in range(2):
            plan(("mod", p), "dve")
        for t in range(TILES):
            plan(("hT", 0, t), "act")
        for c in range(EVEN_W // WCOLS):
            plan(("proj", c), "act")
            plan(("modsum", 2 + c // 2, c % 2), "act")
        for t in range(TILES):
            plan(("qkT", t, 0), "act")
            plan(("qkT", t, 1), "dve")
        plan_attention(0, units0)
        for c in range(D // WCOLS):
            plan(("out", 0, c), "dve")
        for half in range(2):
            plan(("modsum", 5, half), "act")
        for t in range(TILES):
            plan(("hT2", 0, t), "act")
        for k in range(2):
            plan(("query", 0, k), "act")
        for t in range(TILES):
            plan(("hT", 1, t), "act")
        for c in range(3):
            plan(("down", c), "dve" if c % 2 else "act")
        for t in range(TILES):
            plan(("latT", t), "act")
        for c in range(3):
            plan(("uq", c), "dve" if c % 2 else "act")
        for c in range(2):
            for t in range(TILES):
                plan(("ukv", c, t), "dve" if t % 2 else "act")
        for t in range(LAT_TILES):
            plan(("qnT", t), "act")
            plan(("qpT", t), "dve")
        for t in range(TILES):
            plan(("knT", t), "act")
        plan_attention(1, units1)
        for c in range(D // WCOLS):
            plan(("out", 1, c), "dve")
        for t in range(LAT_TILES):
            plan(("hT2", 1, t), "act")
        for k in range(2):
            plan(("query", 1, k), "act")

        def cols(w, kk, n, width):
            return w.rearrange("(k p) n -> p k n", p=P)[:, 0:kk, n:n + width]

        def mod_by_rows(p, half, kc):
            w = a["mod_w"][0].rearrange("(k p) n -> p k n", p=P)
            at = p * D + half * 512
            return w[:, kc * (KD // 2):(kc + 1) * (KD // 2), at:at + 512]

        stream = []
        for p in (0, 1):
            stream += [(("mod", p, c), cols(a["mod_w"][0], KD, p * D + c * WCOLS, WCOLS)) for c in range(4)]
        for c in range(EVEN_W // WCOLS):
            stream += [(("proj", c), cols(a["even_w_in"], KD, c * WCOLS, WCOLS))]
            stream += [(("modv", 2 + c // 2, c % 2, kc), mod_by_rows(2 + c // 2, c % 2, kc)) for kc in range(2)]
        for c in range(D // WCOLS):
            stream += [(("out", 0, c), cols(a["even_w_out"], KD, c * WCOLS, WCOLS))]
            stream += [(("modv", 5, c // 2, c % 2), mod_by_rows(5, c // 2, c % 2))]
        first_slot = {0: 0, len(stream) + 2: 2}
        stream += [(("query", 0, c), cols(a["peer_w_query"][0], KD, c * WCOLS, WCOLS)) for c in range(2)]
        stream += [(("down", c), cols(a["mla_w_in"], KD, c * WCOLS, min(WCOLS, MLA_W - c * WCOLS)))
                   for c in range(3)]
        stream += [(("uq", c), cols(a["mla_w_uq"], QL // P, c * 512, 512)) for c in range(3)]
        stream += [(("ukv", c), cols(a["mla_w_ukv"], KVL // P, c * D, D)) for c in range(2)]
        stream += [(("out", 1, c), cols(a["mla_w_out"], KD, c * WCOLS, WCOLS)) for c in range(D // WCOLS)]
        stream += [(("query", 1, c), cols(a["peer_w_query"][1], KD, c * WCOLS, WCOLS)) for c in range(2)]
        place, had, there = {}, [0] * SLOTS, [None] * SLOTS
        for i, (name, _) in enumerate(stream):
            slot = first_slot.get(i, 0) if i in first_slot else (slot + 1) % SLOTS
            had[slot] += 1
            place[name] = (slot, had[slot], there[slot])
            there[slot] = name
        source = dict(stream)
        assert all(place["query", layer, k][0] == 2 + k for layer in range(2) for k in range(2))

        def chunk(name):
            _, kk, width = source[name].shape
            return view(weights[:, place[name][0], :], 0, kk, width)

        consts_in = sem("consts_in")
        made = sem("made")
        cond_in = sem("cond_in")
        cond_exp = sem("cond_exp")
        cond_silu = sem("cond_silu")
        w_in = [sem(f"w_in{s}") for s in range(SLOTS)]
        w_used = sem("w_used")
        filled = sem("filled")
        act_emptied = sem("act_emptied")
        dve_emptied = sem("dve_emptied")
        bias_in = sem("bias_in")
        row_out = sem("row_out")
        mod_in = {k: sem(f"in_{k}") for k in ("mix0", "ffn0", "mix1", "gate1", "ffn1", "gate1b")}
        mod_made = sem("mod_made")
        sumsq = sem("sumsq")
        h_made = sem("h_made")
        bias_acc_in = sem("bias_acc_in")
        modv_used = sem("modv_used")
        acc_made = sem("acc_made")
        sq_made = sem("sq_made")
        sq_read = sem("sq_read")
        ss_made = sem("ss_made")
        root_made = sem("root_made")
        roped = sem("roped")
        scores_made = sem("scores_made")
        scores_biased = sem("scores_biased")
        probs_made = sem("probs_made")
        pv_done = sem("pv_done")
        sink_shift = sem("sink_shift")
        sink_exp = sem("sink_exp")
        o_made = sem("o_made")
        x_mixed = sem("x_mixed")
        keys_in = sem("keys_in")
        query_w_in = sem("query_w_in")
        query_filled = sem("query_filled")
        query_emptied = sem("query_emptied")
        q_copied = sem("q_copied")
        keys_scored = sem("keys_scored")
        scores_taken = sem("scores_taken")
        best_made = sem("best_made")
        best_exp = sem("best_exp")
        idx_made = sem("idx_made")
        idx_taken = sem("idx_taken")
        idx_staged = sem("idx_staged")
        u_in = [sem(f"u_in{j}") for j in range(HALF)]
        v_in = [sem(f"v_in{j}") for j in range(HALF)]
        u_used = sem("u_used")
        v_used = sem("v_used")
        acts_made = sem("acts_made")
        wts_made = sem("wts_made")
        diag_made = sem("diag_made")
        y_read = sem("y_read")
        mod1_in = sem("mod1_in")
        mod1_sum = sem("mod1_sum")
        mod1_row = sem("mod1_row")
        mod1_out = sem("mod1_out")
        out_done = sem("out_done")
        held = {e: sem(f"held_{e}") for e in ("act", "dve", "pool")}

        block = ctx.enter_context(nc.Block())

        def wait_filled(eng, name):
            eng.wait_ge(filled, jobs[name][0] + 1)

        def wait_emptied(eng, name):
            _, engine, count = jobs[name]
            eng.wait_ge(act_emptied if engine == "act" else dve_emptied, count)

        def wait_multiplied(eng, name):
            if name[0] == "mod" and name[2] < 3:
                eng.wait_ge(w_used, 3 * name[1] + name[2] + 1)
            elif name[0] == "modv":
                _, p, half, kc = name
                eng.wait_ge(modv_used, 4 * (p - 2) + 2 * half + kc + 1)
            elif name[0] == "mod":
                wait_filled(eng, name[:2])
            elif name[0] == "ukv":
                wait_filled(eng, (*name, TILES - 1))
            else:
                wait_filled(eng, name)

        def wait_chunk(eng, name):
            slot, count, _ = place[name]
            eng.wait_ge(w_in[slot], 16 * count)

        names = list(jobs)

        def buffer_free(pe, name):
            n = jobs[name][0]
            if n >= 2:
                wait_emptied(pe, names[n - 2])

        def buffer(name):
            return work[jobs[name][0] % 2]

        heads_before = (0, TILES * PH)
        peer_tiles = (TILES, LAT_TILES)
        n_const_loads = 7

        LOADS = {"mix0": 5, "ffn0": 1, "mix1": 5, "gate1": 1, "ffn1": 3, "gate1b": 1}

        def wait_mod(eng, what):
            if what in LOADS:
                eng.wait_ge(mod_in[what], 16 * LOADS[what])
            if what == "gate0":
                wait_emptied(eng, ("modsum", 2, 1))
            if what == "ffn0":
                wait_emptied(eng, ("modsum", 4, 1))
            if what == "gate0b":
                wait_emptied(eng, ("modsum", 5, 1))

        H_MADE = {(0, 0): 4, (0, 1): 8, (1, 0): 12, (1, 1): 14}

        def experts_pool(pool, layer):
            G0 = heads_before[layer]
            pool.wait_ge(h_made, H_MADE[layer, 1])
            pool.dma_start(keysT[:, 0:PH, :], a["keysT"][layer]).then_inc(keys_in, 16)
            pool.dma_start(keysT[:, PH, :], a["keysT"][layer][:, 0, :]).then_inc(keys_in, 16)

            def gather(dst, table, index, landed):
                pool.indirect_dma_start(dst, None, table, bass.IndirectOffsetOnAxis(ap=index, axis=0)).then_inc(landed, 16)

            def gather_u(G, half, j, free):
                if free:
                    pool.wait_ge(u_used, 16 * G + (HALF * (half - 1) + j + 1))
                    pool.sem_inc(held["pool"], 1)
                gather(urows[:, j, :], a["peer_u"], idx_u[:, half * HALF + j:half * HALF + j + 1], u_in[j])

            def gather_v(G, half, j, free):
                if free:
                    pool.wait_ge(v_used, 16 * G + (HALF * (half - 1) + j + 1))
                    pool.sem_inc(held["pool"], 1)
                gather(vrows[:, j, :], a["peer_v"], idx_v[:, half * HALF + j:half * HALF + j + 1], v_in[j])

            def head(G, first):
                free = not (first and layer == 0)
                pool.wait_ge(idx_made, G + (layer + 1))
                pool.sem_inc(held["pool"], 1)
                if not first:
                    pool.tensor_copy(idx_v[:, HALF:TOPK], idx_u[:, HALF:TOPK]).then_inc(idx_staged, 1)
                pool.tensor_copy(idx_u[:, 0:HALF], idx[:, 0:HALF]).then_inc(idx_staged, 1)
                pool.wait_ge(idx_staged, 3 * G + 1)
                pool.sem_inc(held["pool"], 1)
                for j in range(HALF):
                    gather_u(G, 0, j, free)
                    if not first:
                        gather_v(G - 1, 1, j, True)
                pool.tensor_copy(idx_u[:, HALF:TOPK], idx[:, HALF:TOPK]).then_inc(idx_taken, 1)
                pool.tensor_copy(idx_v[:, 0:HALF], idx_u[:, 0:HALF]).then_inc(idx_staged, 1)
                pool.wait_ge(idx_taken, G + 1)
                pool.sem_inc(held["pool"], 1)
                pool.wait_ge(idx_staged, 3 * G + 2)
                pool.sem_inc(held["pool"], 1)
                for j in range(HALF):
                    gather_u(G, 1, j, True)
                    gather_v(G, 0, j, free)

            n_heads = peer_tiles[layer] * PH
            head(G0, True)
            with pool.Fori(1, n_heads, 1) as n:
                head(n + G0, False)
            G = G0 + n_heads
            pool.tensor_copy(idx_v[:, HALF:TOPK], idx_u[:, HALF:TOPK]).then_inc(idx_staged, 1)
            pool.wait_ge(idx_staged, 3 * G)
            for j in range(HALF):
                gather_v(G - 1, 1, j, True)

        def keys_of(layer, t):
            return TOK if t < LAT_TILES else CTX_LEN

        def empty_query(layer, k, src):
            tiles = peer_tiles[layer]
            src = src[:, :].rearrange("p (s t n) -> p t s n", s=2, n=P)[:, 0:tiles]
            dst = view(arena, 16384, tiles, PH, 2 * P)[:, :, bass.ds(k, 1), :]
            return nc.scalar.activation(dst.rearrange("p t a (s n) -> p t (a s) n", n=P), src, ACT.Copy)

        def experts_act(act, layer):
            G0 = heads_before[layer]
            n_heads = peer_tiles[layer] * PH

            def copy_query(G, n):
                if not (isinstance(G, int) and G == 0):
                    act.wait_ge(keys_scored, G)
                    act.sem_inc(held["act"], 1)
                act.activation(q_now, queryT[:, bass.ds(n, 1), :].rearrange("p a (s t) -> p (a s) t", t=P),
                               ACT.Copy).then_inc(q_copied, 1)

            def exp_best(G):
                act.wait_ge(best_made, G + 1)
                act.activation(expv, best_v, ACT.Exp, bias=neg_best, accum_out=esum).then_inc(best_exp, 1)

            def gelu(G, half):
                act.wait_ge(u_used, 16 * G + HALF * (half + 1))
                act.activation(acts[:, half, :], dots[:, half, :], ACT.Gelu).then_inc(acts_made, 1)

            def diags(G, half):
                act.wait_ge(wts_made, 2 * G + half + 1)
                for j in range(HALF):
                    if isinstance(G, int):
                        used = 16 * G + HALF * half - HALF + j + 1
                    else:
                        used = 16 * G + (HALF * half - HALF + j + 1)
                    if not (isinstance(used, int) and used <= 0):
                        act.wait_ge(v_used, used)
                    act.activation(diag[:, j, :], ident[:, :], ACT.Copy,
                                   scale=wts[:, half, j:j + 1]).then_inc(diag_made, 1)

            def next_query(k):
                act.wait_ge(query_filled, k + ((PH - 2) * layer - 1))
                act.sem_inc(held["act"], 1)
                empty_query(layer, k, work[0]).then_inc(query_emptied, 1)
                act.drain()

            act.drain()
            act.activation(queryT[:, n_heads, :], queryT[:, 0, :], ACT.Copy)
            act.drain()
            E0 = G0 + layer
            copy_query(E0, 0)
            exp_best(E0)

            def body(n, first, queries):
                G = G0 + n
                if not first:
                    gelu(G - 1, 1)
                    diags(G - 1, 1)
                if queries:
                    next_query(n + 1)
                copy_query(E0 + n + 1, n + 1)
                exp_best(E0 + n + 1)
                gelu(G, 0)
                diags(G, 0)

            body(0, True, False)
            with act.Fori(1, PH - 1, 1) as n:
                body(n, False, True)
            with act.Fori(PH - 1, n_heads, 1) as n:
                body(n, False, False)
            gelu(G0 + n_heads - 1, 1)
            diags(G0 + n_heads - 1, 1)

        def experts_pe(pe, layer, silu):
            G0 = heads_before[layer]
            E0 = G0 + layer
            tiles = peer_tiles[layer]

            def score_keys(E, k):
                pe.wait_ge(q_copied, E + 1)
                if not (isinstance(E, int) and E == 0):
                    pe.wait_ge(scores_taken, E)
                for s in range(2):
                    keys = keysT[:, bass.ds(k, 1), s * P:(s + 1) * P].rearrange("p a n -> p (a n)")
                    mm = pe.matmul(ps_s[:, 0, s * P:(s + 1) * P], q_now[:, s, :], keys, start=True, stop=True)
                mm.then_inc(keys_scored, 1)

            def sum_half(G, half, starts, stops):
                for j in range(HALF):
                    pe.wait_ge(v_in[j], 16 * (2 * G + half) + 16)
                    pe.wait_ge(diag_made, 16 * G + (HALF * half + j + 1))
                    for b in range(2):
                        mm = pe.matmul(ps_o[:, b * 512:(b + 1) * 512], diag[:, j, :], vrows[:, j, b * 512:(b + 1) * 512],
                                       start=(starts and j == 0), stop=(stops and j == HALF - 1), skip_group_check=True)
                    mm.then_inc(v_used, 1)

            def query(k):
                done = k - 2 + (PH - 2) * layer
                pe.wait_ge(query_w_in, 16 * done + 16)
                if not (isinstance(done, int) and done == 0):
                    pe.wait_ge(query_emptied, done)
                for s in range(2):
                    for kk in range(KD):
                        mm = pe.matmul(work[0][:, s * 512:s * 512 + tiles * P], query_w[:, kk, s * P:(s + 1) * P],
                                       hTk[:, kk, 0:tiles * P], start=(kk == 0), stop=(kk == KD - 1))
                mm.then_inc(query_filled, 1)

            def mod_strip(n):
                pe.wait_ge(mod1_in, 32 * n + 32)
                if not isinstance(n, int):
                    pe.wait_ge(mod1_row, n)
                elif n:
                    pe.wait_ge(mod1_row, n)
                for k in range(KD):
                    mm = pe.matmul(ps_s[0:2, 1, 0:MODC], silu[:, k, :], mod_w1[:, k, :],
                                   start=(k == 0), stop=(k == KD - 1))
                mm.then_inc(mod1_sum, 1)

            pe.wait_ge(keys_in, 32 * (layer + 1))
            score_keys(E0, 0)
            wait_emptied(pe, ("query", layer, 1))
            for t in range(tiles):
                n0 = t * PH

                def head(k, queries):
                    score_keys(k + (E0 + n0 + 1), k + 1)
                    sum_half(k + (G0 + n0 - 1), 1, False, False)
                    sum_half(k + (G0 + n0), 0, False, False)
                    if layer == 0:
                        mod_strip(k + n0)
                    if queries:
                        query(k + 2)

                score_keys(E0 + n0 + 1, 1)
                if t:
                    sum_half(G0 + n0 - 1, 1, False, True)
                    pe.wait_ge(y_read, (0 if layer == 0 else TILES) + t)
                sum_half(G0 + n0, 0, True, False)
                if layer == 0:
                    mod_strip(n0)
                if t == 0:
                    query(2)
                    with pe.Fori(1, PH - 2, 1) as k:
                        head(k, True)
                with pe.Fori(PH - 2 if t == 0 else 1, PH, 1) as k:
                    head(k, False)
            sum_half(G0 + tiles * PH - 1, 1, False, True)

        def experts_dve(dve, layer):
            G0 = heads_before[layer]
            E0 = G0 + layer
            tiles = peer_tiles[layer]

            def choose(E):
                s = ps_s[:, 0, 0:2 * P].rearrange("p (s n) -> p s n", n=PK)
                dve.wait_ge(keys_scored, E + 1)
                dve.sem_inc(held["dve"], 1)
                for i in range(2):
                    dve.max(top_v[:, i, 0:8], s[:, i, :])
                dve.drain()
                for i in range(2):
                    dve.max_index(top_i[:, i, 0:8], top_v[:, i, 0:8], s[:, i, :])
                    ins = dve.match_replace(left[:, i, :], top_v[:, i, 0:8], s[:, i, :], REMOVED)
                ins.then_inc(scores_taken, 1)
                dve.drain()
                for i in range(2):
                    dve.max(top_v[:, i, 8:16], left[:, i, :])
                dve.drain()
                for i in range(2):
                    dve.max_index(top_i[:, i, 8:16], top_v[:, i, 8:16], left[:, i, :])
                dve.tensor_tensor(cand, top_v[:, 0, :].unsqueeze(2).broadcast_to([P, TOPK, TOPK]),
                                  top_v[:, 1, :].unsqueeze(1).broadcast_to([P, TOPK, TOPK]), ALU.add)
                dve.drain()
                dve.tensor_copy(top_if, top_i)
                flat_cand = cand.rearrange("p a b -> p (a b)")
                dve.max(best_v[:, 0:8], flat_cand)
                dve.drain()
                dve.max_index(best_p[:, 0:8], best_v[:, 0:8], flat_cand)
                dve.match_replace(cand_left, best_v[:, 0:8], flat_cand, REMOVED)
                dve.tensor_scalar(neg_best, best_v[:, 0:1], -1.0, None, ALU.mult)
                dve.drain()
                dve.max(best_v[:, 8:16], cand_left).then_inc(best_made, 1)
                dve.drain()
                dve.max_index(best_p[:, 8:16], best_v[:, 8:16], cand_left)
                dve.drain()
                dve.tensor_scalar(pos_u[:, 0, :], best_p, 4, None, ALU.logical_shift_right)
                dve.tensor_scalar(pos_u[:, 1, :], best_p, 15, None, ALU.bitwise_and)
                dve.drain()
                dve.tensor_copy(pos_f, pos_u)
                dve.drain()
                dve.tensor_tensor(onehot.rearrange("p s k a -> p (s k) a"),
                                  pos_f.rearrange("p s k -> p (s k)").unsqueeze(2).broadcast_to([P, 2 * TOPK, TOPK]),
                                  iota16[:, :].unsqueeze(1).broadcast_to([P, 2 * TOPK, TOPK]), ALU.is_equal)
                dve.drain()
                dve.tensor_tensor(onehot, onehot, top_if.unsqueeze(2).broadcast_to([P, 2, TOPK, TOPK]), ALU.mult)
                dve.drain()
                dve.tensor_reduce(picked.rearrange("p s k -> p (s k)"), onehot.rearrange("p s k a -> p (s k) a"),
                                  AX.X, ALU.add)
                dve.drain()
                dve.scalar_tensor_tensor(out=flat, in0=picked[:, 0, :], scalar=float(PK), in1=picked[:, 1, :],
                                         op0=ALU.mult, op1=ALU.add)
                dve.drain()
                if not (isinstance(E, int) and E == 0):
                    dve.wait_ge(idx_taken, E - layer)
                dve.tensor_scalar(idx, flat, float(layer * EXPERTS), None, ALU.add).then_inc(idx_made, 1)
                dve.wait_ge(best_exp, E + 1)
                dve.reciprocal(erec, esum)
                dve.drain()
                dve.tensor_scalar(g_next, expv, erec, None, ALU.mult)
                dve.drain()

            def dot(G, half, t, js):
                for j in js:
                    dve.wait_ge(u_in[j], 16 * (2 * G + half) + 16)
                    if j == 0 and not (isinstance(G, int) and G == 0):
                        dve.wait_ge(acts_made, 2 * G + half - 1)
                    u = urows[:, j, :]
                    dve.tensor_tensor_reduce(out=u, in0=u, in1=h[:, t, :], scale=1.0, scalar=0.0, op0=ALU.mult,
                                             op1=ALU.add, accum_out=dots[:, half, j:j + 1]).then_inc(u_used, 1)

            def weigh(G, half):
                dve.wait_ge(acts_made, 2 * G + half + 1)
                if not (isinstance(G, int) and G == 0):
                    dve.wait_ge(diag_made, 16 * G + (HALF * half - HALF))
                dve.tensor_tensor(wts[:, half, :], acts[:, half, :], g_now[:, half * HALF:(half + 1) * HALF],
                                  ALU.mult).then_inc(wts_made, 1)

            def add_tile(t):
                dve.wait_ge(v_used, 16 * (G0 + (t + 1) * PH))
                wait_mod(dve, f"gate{layer}b")
                y = h[:, t, :]
                dve.tensor_tensor(y, ps_o[:, :], gate[:, t // LAT_TILES, :], ALU.mult)
                dve.drain()
                dve.tensor_tensor(x[:, t, :], x[:, t, :], y, ALU.add).then_inc(y_read, 1)
                dve.drain()

            def strip(n):
                dve.wait_ge(mod1_sum, n + 1)
                dve.wait_ge(mod1_in, 32 * n + 32)
                if not (isinstance(n, int) and n == 0):
                    dve.wait_ge(mod1_out, 16 * n)
                dve.tensor_tensor(row1[0:2, :], ps_s[0:2, 1, 0:MODC], bias1[0:2, :], ALU.add).then_inc(mod1_row, 1)

            def head(n, t, first, in_tile):
                G = n + G0
                if first:
                    dot(G, 0, t, range(HALF))
                    dve.tensor_copy(g_now, g_next)
                    dve.drain()
                    choose(n + (E0 + 1))
                else:
                    dot(G, 0, t, range(4))
                    weigh(G - 1, 1)
                    dve.drain()
                    dve.tensor_copy(g_now, g_next)
                    dve.drain()
                    choose(n + (E0 + 1))
                    dot(G, 0, t, range(4, HALF))
                dot(G, 1, t, range(4))
                weigh(G, 0)
                if not in_tile and t:
                    add_tile(t - 1)
                dot(G, 1, t, range(4, HALF))
                if layer == 0:
                    strip(n)

            choose(E0)
            for t in range(tiles):
                head(t * PH, t, t == 0, False)
                with dve.Fori(1, PH, 1) as k:
                    head(k + t * PH, t, False, True)
            weigh(G0 + tiles * PH - 1, 1)
            add_tile(tiles - 1)
        @block.sync
        def _(sp):
            sp.dma_start(cond[:, 0, :], a["cond"]).then_inc(cond_in, 16)

            def load(names_):
                for name in names_:
                    slot, _, before = place[name]
                    if before:
                        wait_multiplied(sp, before)
                    sp.dma_start(chunk(name), source[name]).then_inc(w_in[slot], 16)

            order = [name for name, _ in stream]
            load(order[:2])
            for t in range(LAT_TILES):
                sp.dma_start(x[:, t, :], a["x"][t * P:(t + 1) * P, :]).then_inc(consts_in, 16)
                sp.dma_start(x[:, LAT_TILES + t, :], a["ctx"][t * P:(t + 1) * P, :]).then_inc(consts_in, 16)
            sp.dma_start(rope[:, :, :, :], a["rope"]).then_inc(consts_in, 16)
            sp.dma_start(wmask[:, :, :], a["wmask"]).then_inc(consts_in, 16)
            sp.dma_start(sinks[:, 0, :], a["b_sink"].partition_broadcast(P)).then_inc(consts_in, 16)
            first1 = order.index(("down", 0))
            load(order[2:first1])

            def load_query(layer, k):
                src = a["peer_w_query"][layer].rearrange("(k p) n -> p k n", p=P)
                sp.dma_start(query_w, src[:, :, bass.ds(k * WCOLS, WCOLS)]).then_inc(query_w_in, 16)

            sp.wait_ge(h_made, H_MADE[0, 1])
            wait_filled(sp, ("query", 0, 1))

            def strip(n, first):
                at = bass.ds(n * MODC, MODC)
                if not first:
                    sp.wait_ge(mod1_sum, n)
                sp.dma_start(mod_w1, a["mod_w"][1].rearrange("(k p) n -> p k n", p=P)[:, :, at]).then_inc(mod1_in, 16)
                if not first:
                    sp.wait_ge(mod1_row, n)
                sp.dma_start(bias1[0:2, :], a["mod_b2"][1, :, at]).then_inc(mod1_in, 16)
                sp.wait_ge(mod1_row, n + 1)
                sp.dma_start(mod_rows[1, :, at], row1[0:2, :]).then_inc(mod1_out, 16)

            load_query(0, 2)
            strip(0, True)
            with sp.Fori(1, PH - 2, 1) as n:
                sp.wait_ge(query_filled, n)
                load_query(0, n + 2)
                strip(n, False)
            with sp.Fori(PH - 2, TILES * PH, 1) as n:
                strip(n, False)
            sp.wait_ge(y_read, TILES)
            sp.wait_ge(mod1_out, 16 * TILES * PH)
            load(order[first1:])
            wait_filled(sp, ("query", 1, 1))
            load_query(1, 2)
            with sp.Fori(1, PH - 2, 1) as n:
                sp.wait_ge(query_filled, n + (PH - 2))
                load_query(1, n + 2)
            for t in range(LAT_TILES):
                sp.wait_ge(y_read, TILES + t + 1)
                sp.dma_start(out[t * P:(t + 1) * P, :], x[:, t, :]).then_inc(out_done, 16)
            sp.wait_ge(out_done, 16 * LAT_TILES)
            sp.wait_ge(mod1_out, 16 * TILES * PH)

        @block.gpsimd
        def _(pool):
            pool.memset(ident[:, :], 0.0).then_inc(made, 1)
            pool.wait_ge(made, 1)
            pool.affine_select(out=ident[:, :], in_=ident[:, :], compare_op=ALU.not_equal, fill=1.0,
                               base=0, pattern=[[-1, P]], channel_multiplier=1).then_inc(made, 1)
            pool.iota(iota16[:, :], [[1, TOPK]], base=0, channel_multiplier=0,
                      allow_small_or_imprecise_dtypes=True).then_inc(made, 1)
            pool.memset(eps[:, :], EPS).then_inc(made, 1)
            pool.memset(ones[:, :], 1.0).then_inc(made, 1)

            def broadcast(what, dst, src):
                pool.dma_start(dst, src.partition_broadcast(P)).then_inc(mod_in[what], 16)

            def piece(layer, who, p):
                return mod_rows[layer, who, p * D:(p + 1) * D]

            def make_rows(pieces):
                for p in pieces:
                    if p:
                        pool.wait_ge(dve_emptied, jobs[("mod", p - 1)][2])
                    pool.dma_start(bias[0:2, :], a["mod_b2"][0, :, p * D:(p + 1) * D]).then_inc(bias_in, 16)
                    wait_emptied(pool, ("mod", p))
                    pool.dma_start(mod_rows[0, :, p * D:(p + 1) * D], row[0:2, :]).then_inc(row_out, 16)
                    pool.wait_ge(row_out, 16 * (p + 1))

            broadcast("mix0", gain, a["mix_norm"][0])
            pool.dma_start(gain_qk, a["gain_qk"].partition_broadcast(P)).then_inc(bias_in, 16)
            pool.dma_start(bias_acc[0:1, :], a["mod_b2"][0, 0:1, 2 * D:5 * D]).then_inc(bias_acc_in, 16)
            make_rows((0, 1))
            for who in range(2):
                broadcast("mix0", mod[:, 2 * who, :], piece(0, who, 1))
                broadcast("mix0", mod[:, 2 * who + 1, :], piece(0, who, 0))
            pool.wait_ge(h_made, H_MADE[0, 0])
            broadcast("ffn0", gain, a["ffn_norm"][0])
            wait_filled(pool, ("OT", 0, TILES - 1))
            pool.dma_start(bias_acc[0:1, 0:D], a["mod_b2"][0, 0:1, 5 * D:6 * D]).then_inc(bias_acc_in, 16)
            experts_pool(pool, 0)
            pool.wait_ge(y_read, TILES)
            pool.wait_ge(mod1_out, 16 * TILES * PH)
            broadcast("mix1", gain, a["mix_norm"][1])
            for who in range(2):
                broadcast("mix1", mod[:, 2 * who, :], piece(1, who, 1))
                broadcast("mix1", mod[:, 2 * who + 1, :], piece(1, who, 0))
            broadcast("gate1", gate[:, 0, :], piece(1, 0, 2))
            pool.dma_start(gain_m, a["gain_m"].partition_broadcast(P)).then_inc(bias_in, 16)
            pool.wait_ge(h_made, H_MADE[1, 0])
            broadcast("ffn1", gain, a["ffn_norm"][1])
            broadcast("ffn1", mod[:, 0, :], piece(1, 0, 4))
            broadcast("ffn1", mod[:, 1, :], piece(1, 0, 3))
            pool.wait_ge(x_mixed, 2 * D // WCOLS)
            broadcast("gate1b", gate[:, 0, :], piece(1, 0, 5))
            experts_pool(pool, 1)

        @block.scalar
        def _(act):
            act.wait_ge(cond_in, 16)
            act.activation(cond[:, 1, :], cond[:, 0, :], ACT.Exp, scale=-1.0).then_inc(cond_exp, 1)
            act.wait_ge(consts_in, 16 * n_const_loads)
            act.wait_ge(made, 5)

            def empty(name, dst, src):
                wait_filled(act, name)
                act.activation(dst, src, ACT.Copy).then_inc(act_emptied, 1)

            def rms(tiles, base):
                for n, t in enumerate(tiles):
                    act.activation(h[:, t, :], x[:, t, :], ACT.Square, accum_out=stat[:, t:t + 1])
                act.drain()
                act.activation(stat[:, 8:8 + len(tiles)], stat[:, tiles[0]:tiles[0] + len(tiles)], ACT.Sqrt,
                               bias=eps[:, :], scale=1.0 / D).then_inc(sumsq, 1)

            def empty_hT(layer, kind, tiles):
                for t in tiles:
                    name = (kind, layer, t)
                    empty(name, hTk[:, :, t * P:(t + 1) * P],
                          buffer(name)[:, :].rearrange("p (k t) -> p k t", t=P))

            def attention(layer, units, scale, sink):
                base = 0 if layer == 0 else len(units0)

                def exp(n):
                    t, k = units[n]
                    act.wait_ge(scores_biased, base + n + 1)
                    if n >= 2:
                        wait_filled(act, ("PT", layer, n - 2))
                    kk = keys_of(layer, t)
                    act.activation(probs[:, n % 2, 0:kk], ps_s[:, n % 2, 0:kk], ACT.Exp, scale=scale,
                                   bias=soft[:, 1, n:n + 1], accum_out=soft[:, 2, n:n + 1]).then_inc(probs_made, 1)
                    if sink and k == 15:
                        act.wait_ge(sink_shift, t + 1)
                        act.activation(stat[:, 24:32], stat[:, 16:24], ACT.Exp).then_inc(sink_exp, 1)

                def turned_out(t):
                    name = ("OT", layer, t)
                    empty(name, hTk[:, :, t * P:(t + 1) * P],
                          buffer(name)[:, :].rearrange("p (k t) -> p k t", t=P))

                exp(0)
                for n, (t, k) in enumerate(units):
                    if n + 1 < len(units):
                        exp(n + 1)
                    if n >= 2:
                        act.wait_ge(pv_done, base + n - 1)
                    kk = keys_of(layer, t)
                    name = ("PT", layer, n)
                    empty(name, probsT[:, n % 2, 0:kk], buffer(name)[:, 0:kk])
                    if n >= 2 and ends_tile(units, n - 2):
                        turned_out(units[n - 2][0])
                turned_out(units[-1][0])

            def empty_modsum(p, half, dst):
                name = ("modsum", p, half)
                empty(name, dst[:, :, half * 512:(half + 1) * 512],
                      buffer(name)[:, :].rearrange("p (w n) -> p w n", n=512))

            def empty_queries(layer):
                for k in range(2):
                    wait_filled(act, ("query", layer, k))
                    empty_query(layer, k, buffer(("query", layer, k))).then_inc(act_emptied, 1)

            rms(range(TILES), 0)
            act.wait_ge(h_made, H_MADE[0, 0])
            empty_hT(0, "hT", range(TILES))
            shifts = mod[:, :, :].rearrange("p (w two) n -> p w two n", two=2)
            for c in range(EVEN_W // WCOLS):
                name = ("proj", c)
                empty(name, pj[:, :, c * WCOLS:(c + 1) * WCOLS],
                      buffer(name)[:, :].rearrange("p (t n) -> p t n", n=WCOLS))
                p = 2 + c // 2
                empty_modsum(p, c % 2, {2: gate[:, :, :], 3: shifts[:, :, 1], 4: shifts[:, :, 0]}[p])
            act.drain()
            for t in range(TILES):
                act.activation(sq[:, t, :], pj[:, t, 0:QKW], ACT.Square).then_inc(sq_made, 1)
            act.wait_ge(ss_made, 1)
            act.activation(heads_stat[:, 1, :], heads_stat[:, 0, :], ACT.Sqrt, bias=eps[:, :],
                           scale=1.0 / HD).then_inc(root_made, 1)
            for t in range(TILES):
                name = ("qkT", t, 0)
                empty(name, qkT[:, 0:8, t * P:(t + 1) * P], buffer(name)[:, :].rearrange("p (k t) -> p k t", t=P))
            attention(0, units0, HD ** -0.5, True)
            act.wait_ge(x_mixed, D // WCOLS)
            rms(range(TILES), 0)
            for half in range(2):
                empty_modsum(5, half, gate[:, :, :])
            empty_hT(0, "hT2", range(TILES))
            empty_queries(0)
            experts_act(act, 0)
            act.wait_ge(y_read, TILES)
            rms(range(TILES), 0)
            empty_hT(1, "hT", range(TILES))
            for c in (0, 2):
                name = ("down", c)
                width = chunk(name).shape[2]
                empty(name, pm[:, :, c * WCOLS:c * WCOLS + width],
                      buffer(name)[:, :].rearrange("p (t n) -> p t n", n=WCOLS)[:, :, 0:width])
            wait_emptied(act, ("down", 1))
            act.drain()
            squares = [(pm[:, t, :], MLA_W) for t in range(TILES)]
            n_sq = TILES
            for n, (src, width) in enumerate(squares):
                if n:
                    act.wait_ge(sq_read, n)
                act.activation(sq1[:, 0:width], src, ACT.Square).then_inc(sq_made, 1)
            act.wait_ge(sq_read, n_sq)
            for c, width in enumerate((QL, KVL, ROPE)):
                ins = act.activation(heads_stat[:, 1, c * 4:c * 4 + 4], heads_stat[:, 0, c * 4:c * 4 + 4], ACT.Sqrt,
                                     bias=eps[:, :], scale=1.0 / width)
            ins.then_inc(root_made, 1)
            for t in range(TILES):
                name = ("latT", t)
                b = buffer(name)[:, :].rearrange("p (k t) -> p k t", t=P)
                wait_filled(act, name)
                at = slice(t * P, (t + 1) * P)
                if t < LAT_TILES:
                    act.activation(cqT[:, :, at], b[:, 0:3, :], ACT.Copy)
                act.activation(ckvT[:, :, at], b[:, 3:5, :], ACT.Copy)
                act.activation(kpT[:, at], b[:, 5, :], ACT.Copy).then_inc(act_emptied, 1)
            for c in (0, 2):
                name = ("uq", c)
                empty(name, qm[:, :, c * 512:(c + 1) * 512], buffer(name)[:, :].rearrange("p (t n) -> p t n", n=512))
            for c, dst in enumerate((kn, vm)):
                for t in range(0, TILES, 2):
                    empty(("ukv", c, t), dst[:, t, :], buffer(("ukv", c, t))[:, :])
            act.drain()
            wait_emptied(act, ("ukv", 1, 3))
            for t in range(LAT_TILES):
                act.wait_ge(sq_read, n_sq + t)
                act.activation(sq1[:, 0:1536], qm[:, t, :], ACT.Square).then_inc(sq_made, 1)
            for t in range(TILES):
                act.wait_ge(sq_read, n_sq + LAT_TILES + t)
                act.activation(sq1[:, 0:D], kn[:, t, :], ACT.Square).then_inc(sq_made, 1)
            act.wait_ge(sq_read, n_sq + LAT_TILES + TILES)
            act.activation(heads_stat[:, 1, 0:48], heads_stat[:, 0, 0:48], ACT.Sqrt, bias=eps[:, :], scale=1.0 / NOPE)
            act.activation(heads_stat[:, 1, 48:64], heads_stat[:, 0, 48:64], ACT.Sqrt, bias=eps[:, :],
                           scale=1.0 / ROPE).then_inc(root_made, 1)
            for t in range(LAT_TILES):
                name = ("qnT", t)
                empty(name, qnT[:, :, t * P:(t + 1) * P], buffer(name)[:, :].rearrange("p (k t) -> p k t", t=P))
            for t in range(TILES):
                name = ("knT", t)
                empty(name, knT[:, :, t * P:(t + 1) * P], buffer(name)[:, :].rearrange("p (k t) -> p k t", t=P))
            attention(1, units1, (NOPE + ROPE) ** -0.5, False)
            act.wait_ge(x_mixed, 2 * D // WCOLS)
            rms(range(LAT_TILES), 0)
            empty_hT(1, "hT2", range(LAT_TILES))
            empty_queries(1)
            experts_act(act, 1)

        @block.tensor
        def _(pe):
            pe.wait_ge(made, 5)
            pe.wait_ge(cond_silu, 1)
            silu = cond[:, 2, :].rearrange("p (k w) -> p k w", w=2)

            def mod_rows_job(p):
                name = ("mod", p)
                buffer_free(pe, name)
                for c in range(4):
                    wait_chunk(pe, ("mod", p, c))
                    for k in range(KD):
                        mm = pe.matmul(buffer(name)[0:2, c * WCOLS:(c + 1) * WCOLS], silu[:, k, :],
                                       chunk(("mod", p, c))[:, k, :], start=(k == 0), stop=(k == KD - 1))
                    mm.then_inc(w_used if c < 3 else filled, 1)

            def mod_sum(p, half):
                name = ("modsum", p, half)
                buffer_free(pe, name)
                pe.wait_ge(acc_made, 2 * (p - 2) + half + 1)
                for who in range(2):
                    mm = pe.matmul(buffer(name)[:, who * 512:(who + 1) * 512], ones[:, :], mod_acc[:, half, who, :],
                                   start=True, stop=True)
                mm.then_inc(filled, 1)

            def transposes(name, sources):
                buffer_free(pe, name)
                for n, src in enumerate(sources):
                    mm = pe.transpose(buffer(name)[:, n * P:n * P + P], src, ident[:, :])
                mm.then_inc(filled, 1)

            def product_all(name, c_name, tiles, width, kk, lhs):
                buffer_free(pe, name)
                wait_chunk(pe, c_name)
                w = chunk(c_name)
                for n, t in enumerate(tiles):
                    for k in range(kk):
                        mm = pe.matmul(buffer(name)[:, n * WCOLS:n * WCOLS + width], lhs[:, k, t * P:(t + 1) * P],
                                       w[:, k, :], start=(k == 0), stop=(k == kk - 1))
                mm.then_inc(filled, 1)

            def turn_h(layer, kind, tiles, made_):
                for n, t in enumerate(tiles):
                    pe.wait_ge(h_made, made_ - len(tiles) + n + 1)
                    transposes((kind, layer, t), [h[:, t, k * P:(k + 1) * P] for k in range(KD)])

            def attention(layer, units):
                last = 16 if layer == 0 else MH
                base = 0 if layer == 0 else len(units0)

                def scores(n):
                    t, k = units[n]
                    if base + n >= 2:
                        pe.wait_ge(probs_made, base + n - 1)
                    q_at = slice(t * P, (t + 1) * P)
                    k_at = slice(0, TOK) if t < LAT_TILES else slice(SEQ, TOK)
                    kk = keys_of(layer, t)
                    dst = ps_s[:, n % 2, 0:kk]
                    if layer == 0:
                        g, kh = divmod(k, 8)
                        half = slice(HD * (kh % 2), HD * (kh % 2) + HD)
                        mm = pe.matmul(dst, qkT[half, 5 * g + kh // 2, q_at], qkT[half, 5 * g + 4, k_at],
                                       start=True, stop=True)
                    else:
                        half = slice(ROPE * (k % 2), ROPE * (k % 2) + ROPE)
                        pe.matmul(dst, qnT[:, k, q_at], knT[:, k, k_at], start=True, stop=False)
                        mm = pe.matmul(dst, qpT[half, k // 2, q_at], kpT[half, k_at], start=False, stop=True)
                    mm.then_inc(scores_made, 1)

                def weigh_values(n):
                    t, k = units[n]
                    kk = keys_of(layer, t)
                    wait_emptied(pe, ("PT", layer, n))
                    if k == 0 and base + t:
                        pe.wait_ge(o_made, t if layer == 0 else TILES + t)
                    for i in range(kk // P):
                        key_tile = i if t < LAT_TILES else LAT_TILES + i
                        if layer == 0:
                            g, kh = divmod(k, 8)
                            v_at = QKW + 2 * HD * g + HD * (kh % 2)
                            rhs = pj[:, key_tile, v_at:v_at + HD]
                            o_at = slice(k * HD, (k + 1) * HD)
                        else:
                            rhs = vm[:, key_tile, k * VD:(k + 1) * VD]
                            o_at = slice(k * VD, (k + 1) * VD)
                        mm = pe.matmul(ps_o[:, o_at], probsT[:, n % 2, i * P:(i + 1) * P], rhs,
                                       start=(i == 0), stop=(i == kk // P - 1))
                    mm.then_inc(pv_done, 1)

                def turn_out(t):
                    pe.wait_ge(o_made, (0 if layer == 0 else TILES) + t + 1)
                    transposes(("OT", layer, t), [o_sb[:, i * P:(i + 1) * P] for i in range(KD)])

                scores(0)
                scores(1)
                for n, (t, k) in enumerate(units):
                    if n + 2 < len(units):
                        scores(n + 2)
                    pe.wait_ge(probs_made, base + n + 1)
                    transposes(("PT", layer, n), [probs[:, n % 2, i * P:(i + 1) * P]
                                                  for i in range(keys_of(layer, t) // P)])
                    if n:
                        weigh_values(n - 1)
                    if n >= 2 and ends_tile(units, n - 2):
                        turn_out(units[n - 2][0])
                weigh_values(len(units) - 1)
                turn_out(units[-1][0])

            def queries(layer):
                tiles = peer_tiles[layer]
                wait_emptied(pe, ("hT2", layer, tiles - 1))
                for k in range(2):
                    name = ("query", layer, k)
                    buffer_free(pe, name)
                    wait_chunk(pe, name)
                    for s in range(2):
                        for kk in range(KD):
                            mm = pe.matmul(buffer(name)[:, s * 512:s * 512 + tiles * P],
                                           chunk(name)[:, kk, s * P:(s + 1) * P], hTk[:, kk, 0:tiles * P],
                                           start=(kk == 0), stop=(kk == KD - 1))
                    mm.then_inc(filled, 1)

            for p in range(2):
                mod_rows_job(p)
            turn_h(0, "hT", range(TILES), H_MADE[0, 0])
            wait_emptied(pe, ("hT", 0, TILES - 1))
            for c in range(EVEN_W // WCOLS):
                product_all(("proj", c), ("proj", c), range(TILES), WCOLS, KD, hTk)
                mod_sum(2 + c // 2, c % 2)
            for t in range(TILES):
                pe.wait_ge(roped, t + 1)
                blocks = [pj[:, t, k * P:(k + 1) * P] for k in range(QKH // 2)]
                transposes(("qkT", t, 0), blocks[:8])
                transposes(("qkT", t, 1), blocks[8:])
            wait_emptied(pe, ("qkT", TILES - 1, 0))
            wait_emptied(pe, ("qkT", TILES - 1, 1))
            attention(0, units0)
            wait_emptied(pe, ("OT", 0, TILES - 1))
            for c in range(D // WCOLS):
                product_all(("out", 0, c), ("out", 0, c), range(TILES), WCOLS, KD, hTk)
            for half in range(2):
                mod_sum(5, half)
            turn_h(0, "hT2", range(TILES), H_MADE[0, 1])
            queries(0)
            experts_pe(pe, 0, silu)
            turn_h(1, "hT", range(TILES), H_MADE[1, 0])
            wait_emptied(pe, ("hT", 1, TILES - 1))
            for c in range(3):
                product_all(("down", c), ("down", c), range(TILES), chunk(("down", c)).shape[2], KD, hTk)
            for t in range(TILES):
                pe.wait_ge(roped, TILES + t + 1)
                name = ("latT", t)
                buffer_free(pe, name)
                for n in range(0 if t < LAT_TILES else 3, 5):
                    pe.transpose(buffer(name)[:, n * P:(n + 1) * P], pm[:, t, n * P:(n + 1) * P], ident[:, :])
                pe.transpose(buffer(name)[:, 5 * P:6 * P], o_sb[:, t * P:(t + 1) * P], ident[:, :]).then_inc(filled, 1)
            wait_emptied(pe, ("latT", TILES - 1))
            for c in range(3):
                name = ("uq", c)
                buffer_free(pe, name)
                wait_chunk(pe, name)
                for t in range(LAT_TILES):
                    for k in range(QL // P):
                        mm = pe.matmul(buffer(name)[:, t * 512:(t + 1) * 512], cqT[:, k, t * P:(t + 1) * P],
                                       chunk(name)[:, k, :], start=(k == 0), stop=(k == QL // P - 1))
                mm.then_inc(filled, 1)
            for c in range(2):
                wait_chunk(pe, ("ukv", c))
                for t in range(TILES):
                    name = ("ukv", c, t)
                    buffer_free(pe, name)
                    for half in range(2):
                        for k in range(KVL // P):
                            mm = pe.matmul(buffer(name)[:, half * 512:(half + 1) * 512], ckvT[:, k, t * P:(t + 1) * P],
                                           chunk(("ukv", c))[:, k, half * 512:(half + 1) * 512],
                                           start=(k == 0), stop=(k == KVL // P - 1))
                    mm.then_inc(filled, 1)
            for t in range(LAT_TILES):
                pe.wait_ge(roped, 2 * TILES + t + 1)
                transposes(("qnT", t), [qm[:, t, k * P:(k + 1) * P] for k in range(MH)])
                transposes(("qpT", t), [qm[:, t, (MH + k) * P:(MH + k + 1) * P] for k in range(MH // 2)])
            for t in range(TILES):
                pe.wait_ge(roped, 2 * TILES + LAT_TILES + t + 1)
                transposes(("knT", t), [kn[:, t, k * P:(k + 1) * P] for k in range(MH)])
            wait_emptied(pe, ("knT", TILES - 1))
            wait_emptied(pe, ("qpT", LAT_TILES - 1))
            attention(1, units1)
            wait_emptied(pe, ("OT", 1, LAT_TILES - 1))
            for c in range(D // WCOLS):
                product_all(("out", 1, c), ("out", 1, c), range(LAT_TILES), WCOLS, KD, hTk)
            turn_h(1, "hT2", range(LAT_TILES), H_MADE[1, 1])
            queries(1)
            experts_pe(pe, 1, silu)

        @block.vector
        def _(dve):
            dve.wait_ge(cond_exp, 1)
            dve.tensor_scalar(cond[:, 1, :], cond[:, 1, :], 1.0, None, ALU.add)
            dve.drain()
            dve.reciprocal(cond[:, 1, :], cond[:, 1, :])
            dve.drain()
            dve.tensor_tensor(cond[:, 2, :], cond[:, 0, :], cond[:, 1, :], ALU.mult).then_inc(cond_silu, 1)
            dve.wait_ge(consts_in, 16 * n_const_loads)
            dve.wait_ge(made, 5)
            dve.tensor_scalar(sinks[:, 1, :], sinks[:, 0, :], -1.0, None, ALU.mult)

            def mod_products(p, half):
                acc = mod_acc[:, half]
                if p > 2:
                    wait_filled(dve, ("modsum", p - 1, half))
                for k in range(KD):
                    kc, k_in = divmod(k, KD // 2)
                    name = ("modv", p, half, kc)
                    if k_in == 0:
                        wait_chunk(dve, name)
                    w = chunk(name)[:, k_in, :]
                    for who in range(2):
                        c = cond[:, 2, 2 * k + who:2 * k + who + 1]
                        if k == 0:
                            ins = dve.tensor_scalar(acc[:, who, :], w, c, None, ALU.mult)
                        else:
                            ins = dve.scalar_tensor_tensor(out=acc[:, who, :], in0=w, scalar=c, in1=acc[:, who, :],
                                                           op0=ALU.mult, op1=ALU.add)
                    if k_in == KD // 2 - 1:
                        ins.then_inc(modv_used, 1)
                    dve.drain()
                dve.wait_ge(bias_acc_in, 32 if p == 5 else 16)
                b_at = (0 if p == 5 else (p - 2) * D) + half * 512
                dve.tensor_tensor(acc[0:1], acc[0:1], bias_acc[0:1, b_at:b_at + 512].unsqueeze(1).broadcast_to([1, 2, 512]),
                                  ALU.add).then_inc(acc_made, 1)

            def empty(name, dst, src):
                wait_filled(dve, name)
                dve.tensor_copy(dst, src).then_inc(dve_emptied, 1)

            def empty_mod(p):
                name = ("mod", p)
                wait_filled(dve, name)
                dve.wait_ge(bias_in, 16 * (p + 2))
                if p:
                    dve.wait_ge(row_out, 16 * p)
                dve.tensor_tensor(row[0:2, :], buffer(name)[0:2, :], bias[0:2, :], ALU.add).then_inc(dve_emptied, 1)

            def norm(landed, tiles, count):
                wait_mod(dve, landed)
                for who in range(2 if len(tiles) > LAT_TILES else 1):
                    dve.scalar_tensor_tensor(out=mod[:, 2 * who, :], in0=mod[:, 2 * who, :], scalar=1.0, in1=gain,
                                             op0=ALU.add, op1=ALU.mult)
                dve.wait_ge(sumsq, count)
                dve.reciprocal(stat[:, 8:8 + len(tiles)], stat[:, 8:8 + len(tiles)])
                dve.drain()
                for t in tiles:
                    who = t // LAT_TILES
                    dve.scalar_tensor_tensor(out=h[:, t, :], in0=x[:, t, :], scalar=stat[:, 8 + t:9 + t],
                                             in1=mod[:, 2 * who, :], op0=ALU.mult, op1=ALU.mult)
                    dve.drain()
                    dve.tensor_tensor(h[:, t, :], h[:, t, :], mod[:, 2 * who + 1, :], ALU.add).then_inc(h_made, 1)

            def turn(v, t, n_heads, width=HD):
                cs = rope[:, t, 0, :].unsqueeze(1).broadcast_to([P, n_heads, width])
                sn = rope[:, t, 1, :].rearrange("p (i two) -> p i two", two=2)
                pairs = v.rearrange("p h (i two) -> p h i two", two=2)
                tmp = view(sq_tmp(n_heads), 0, n_heads, width)
                tpairs = tmp.rearrange("p h (i two) -> p h i two", two=2)
                for e in range(2):
                    dve.tensor_tensor(tpairs[:, :, :, e], pairs[:, :, :, 1 - e],
                                      sn[:, :, e].unsqueeze(1).broadcast_to([P, n_heads, width // 2]), ALU.mult)
                dve.drain()
                dve.tensor_tensor(v, v, cs, ALU.mult)
                dve.drain()
                return dve.tensor_tensor(v, v, tmp, ALU.add)

            def sq_tmp(n_heads):
                return arena[:, 11264:11264 + n_heads * HD] if n_heads == QKH else arena[:, 18432 + 512:18432 + 512 + n_heads * HD]

            def scale_heads(v, stats, gains):
                heads, width = v.shape[1], v.shape[2]
                dve.tensor_tensor(v, v, stats.unsqueeze(2).broadcast_to([P, heads, width]), ALU.mult)
                dve.drain()
                return dve.tensor_tensor(v, v, gains, ALU.mult)

            def attention(layer, units, scale, sink):
                last = 16 if layer == 0 else MH
                base = 0 if layer == 0 else len(units0)
                width = HD if layer == 0 else VD

                def shift(n):
                    t, k = units[n]
                    s = ps_s[:, n % 2, 0:keys_of(layer, t)]
                    dve.wait_ge(scores_made, base + n + 1)
                    if sink and k >= 8 and t < LAT_TILES:
                        other = 1 - t
                        dve.tensor_tensor(s[:, other * P:(other + 1) * P], s[:, other * P:(other + 1) * P],
                                          wmask[:, t, :], ALU.add)
                        dve.drain()
                    dve.tensor_reduce(soft[:, 0, n:n + 1], s, AX.X, ALU.max, negate=True)
                    dve.drain()
                    if sink and k >= 8:
                        dve.tensor_scalar(soft[:, 1, n:n + 1], soft[:, 0, n:n + 1], scale, sinks[:, 1, k - 8:k - 7],
                                          ALU.mult, ALU.min).then_inc(scores_biased, 1)
                    else:
                        dve.tensor_scalar(soft[:, 1, n:n + 1], soft[:, 0, n:n + 1], scale, None,
                                          ALU.mult).then_inc(scores_biased, 1)
                    if sink and k == last - 1:
                        dve.drain()
                        dve.tensor_tensor(stat[:, 16:24], soft[:, 1, n - 7:n + 1], sinks[:, 0, :],
                                          ALU.add).then_inc(sink_shift, 1)

                def divide(n):
                    t = units[n][0]
                    first = n - last + 1
                    dve.wait_ge(probs_made, base + n + 1)
                    if sink:
                        dve.wait_ge(sink_exp, t + 1)
                        dve.tensor_tensor(soft[:, 2, first + 8:n + 1], soft[:, 2, first + 8:n + 1],
                                          stat[:, 24:32], ALU.add)
                        dve.drain()
                    dve.reciprocal(soft[:, 3, first:n + 1], soft[:, 2, first:n + 1])
                    dve.drain()
                    dve.wait_ge(pv_done, base + n + 1)
                    if t or layer:
                        wait_filled(dve, ("OT", layer, t - 1) if t else ("latT", TILES - 1))
                    dve.tensor_tensor(o_sb.rearrange("p (k w) -> p k w", w=width),
                                      ps_o[:, :].rearrange("p (k w) -> p k w", w=width),
                                      soft[:, 3, first:n + 1].unsqueeze(2).broadcast_to([P, last, width]),
                                      ALU.mult).then_inc(o_made, 1)

                for n in range(len(units)):
                    shift(n)
                    if n >= 2 and ends_tile(units, n - 2):
                        divide(n - 2)
                divide(len(units) - 1)

            def add_mixed(layer, tiles):
                if layer == 0:
                    mod_products(5, 0)
                for c in range(D // WCOLS):
                    if layer == 0 and c == 2:
                        mod_products(5, 1)
                    name = ("out", layer, c)
                    b = buffer(name)[:, :].rearrange("p (t n) -> p t n", n=WCOLS)
                    wait_filled(dve, name)
                    if c == 0:
                        wait_mod(dve, f"gate{layer}")
                    at = slice(c * WCOLS, (c + 1) * WCOLS)
                    for who in range(tiles // LAT_TILES):
                        ts = slice(who * LAT_TILES, (who + 1) * LAT_TILES)
                        ins = dve.tensor_tensor(gated[:, ts, :], b[:, ts, :],
                                                gate[:, who, at].unsqueeze(1).broadcast_to([P, LAT_TILES, WCOLS]), ALU.mult)
                    ins.then_inc(dve_emptied, 1)
                    dve.drain()
                    dve.tensor_tensor(x[:, 0:tiles, at], x[:, 0:tiles, at], gated[:, 0:tiles, :],
                                      ALU.add).then_inc(x_mixed, 1)
                    dve.drain()

            for p in range(2):
                empty_mod(p)
            norm("mix0", range(TILES), 1)
            for p in range(2, 5):
                for half in range(2):
                    mod_products(p, half)
            for t in range(TILES):
                dve.wait_ge(sq_made, t + 1)
                ins = dve.tensor_reduce(heads_stat[:, 0, t * QKH:(t + 1) * QKH],
                                        sq[:, t, :].rearrange("p (h w) -> p h w", w=HD), AX.X, ALU.add)
            ins.then_inc(ss_made, 1)
            dve.wait_ge(root_made, 1)
            dve.reciprocal(heads_stat[:, 1, :], heads_stat[:, 1, :])
            dve.drain()
            for t in range(TILES):
                v = pj[:, t, 0:QKW].rearrange("p (h w) -> p h w", w=HD)
                ins = scale_heads(v, heads_stat[:, 1, t * QKH:(t + 1) * QKH],
                                  gain_qk.rearrange("p (h w) -> p h w", w=HD))
                if t < LAT_TILES:
                    dve.drain()
                    ins = turn(v, t, QKH)
                ins.then_inc(roped, 1)
            for t in range(TILES):
                name = ("qkT", t, 1)
                empty(name, qkT[:, 8:10, t * P:(t + 1) * P],
                      buffer(name)[:, 0:2 * P].rearrange("p (k t) -> p k t", t=P))
            attention(0, units0, HD ** -0.5, True)
            add_mixed(0, TILES)
            norm("ffn0", range(TILES), 2)
            experts_dve(dve, 0)
            norm("mix1", range(TILES), 3)
            name = ("down", 1)
            empty(name, pm[:, :, WCOLS:2 * WCOLS], buffer(name)[:, :].rearrange("p (t n) -> p t n", n=WCOLS))
            for t in range(TILES):
                dve.wait_ge(sq_made, TILES + t + 1)
                at = 0
                for c, width in enumerate((QL, KVL, ROPE)):
                    ins = dve.tensor_reduce(heads_stat[:, 0, c * 4 + t:c * 4 + t + 1], sq1[:, at:at + width], AX.X, ALU.add)
                    at += width
                ins.then_inc(sq_read, 1)
            dve.wait_ge(root_made, 2)
            dve.reciprocal(heads_stat[:, 1, 0:12], heads_stat[:, 1, 0:12])
            dve.drain()
            dve.wait_ge(bias_in, 16 * 4)
            for t in range(TILES):
                at = 0
                for c, width in enumerate((QL, KVL, ROPE)):
                    dve.scalar_tensor_tensor(out=pm[:, t, at:at + width], in0=pm[:, t, at:at + width],
                                             scalar=heads_stat[:, 1, c * 4 + t:c * 4 + t + 1], in1=gain_m[:, at:at + width],
                                             op0=ALU.mult, op1=ALU.mult)
                    at += width
                dve.drain()
                kp = pm[:, t, QL + KVL:MLA_W].unsqueeze(1)
                if t < LAT_TILES:
                    turn(kp, t, 1)
                    dve.drain()
                dve.tensor_copy(o_sb[:, t * P:(t + 1) * P].rearrange("p (two w) -> p two w", two=2),
                                kp.broadcast_to([P, 2, ROPE])).then_inc(roped, 1)
                dve.drain()
            name = ("uq", 1)
            empty(name, qm[:, :, 512:1024], buffer(name)[:, :].rearrange("p (t n) -> p t n", n=512))
            for c, dst in enumerate((kn, vm)):
                for t in range(1, TILES, 2):
                    empty(("ukv", c, t), dst[:, t, :], buffer(("ukv", c, t))[:, :])
            for t in range(LAT_TILES):
                dve.wait_ge(sq_made, 2 * TILES + t + 1)
                dve.tensor_reduce(heads_stat[:, 0, t * MH:(t + 1) * MH],
                                  sq1[:, 0:D].rearrange("p (h w) -> p h w", w=NOPE), AX.X, ALU.add)
                dve.tensor_reduce(heads_stat[:, 0, 48 + t * MH:48 + (t + 1) * MH],
                                  sq1[:, D:D + MH * ROPE].rearrange("p (h w) -> p h w", w=ROPE), AX.X,
                                  ALU.add).then_inc(sq_read, 1)
            for t in range(TILES):
                dve.wait_ge(sq_made, 2 * TILES + LAT_TILES + t + 1)
                ins = dve.tensor_reduce(heads_stat[:, 0, 16 + t * MH:16 + (t + 1) * MH],
                                        sq1[:, 0:D].rearrange("p (h w) -> p h w", w=NOPE), AX.X, ALU.add)
                ins.then_inc(sq_read, 1)
            dve.wait_ge(root_made, 3)
            dve.reciprocal(heads_stat[:, 1, 0:64], heads_stat[:, 1, 0:64])
            dve.drain()
            g_at = MLA_W
            gains = [gain_m[:, g_at:g_at + NOPE], gain_m[:, g_at + NOPE:g_at + NOPE + ROPE],
                     gain_m[:, g_at + NOPE + ROPE:g_at + 2 * NOPE + ROPE]]

            def over_heads(g):
                return g.unsqueeze(1).broadcast_to([P, MH, g.shape[1]])

            for t in range(LAT_TILES):
                v = qm[:, t, 0:D].rearrange("p (h w) -> p h w", w=NOPE)
                scale_heads(v, heads_stat[:, 1, t * MH:(t + 1) * MH], over_heads(gains[0]))
                v = qm[:, t, D:D + MH * ROPE].rearrange("p (h w) -> p h w", w=ROPE)
                scale_heads(v, heads_stat[:, 1, 48 + t * MH:48 + (t + 1) * MH], over_heads(gains[1]))
                dve.drain()
                turn(v, t, MH).then_inc(roped, 1)
                dve.drain()
            for t in range(TILES):
                v = kn[:, t, :].rearrange("p (h w) -> p h w", w=NOPE)
                scale_heads(v, heads_stat[:, 1, 16 + t * MH:16 + (t + 1) * MH], over_heads(gains[2])).then_inc(roped, 1)
            for t in range(LAT_TILES):
                name = ("qpT", t)
                empty(name, qpT[:, :, t * P:(t + 1) * P],
                      buffer(name)[:, 0:4 * P].rearrange("p (k t) -> p k t", t=P))
            attention(1, units1, (NOPE + ROPE) ** -0.5, False)
            add_mixed(1, LAT_TILES)
            norm("ffn1", range(LAT_TILES), 4)
            experts_dve(dve, 1)



def kernel(**inputs):
    import numpy as np
    import concourse.bacc as bacc
    from concourse.bass_utils import run_bass_kernel_spmd as run

    i = {k: np.asarray(v) for k, v in inputs.items()}
    layers = 2
    pair = [0, 4, 1, 5, 2, 6, 3, 7]
    head_cols = lambda at, hs: [at + h * 64 + j for h in hs for j in range(64)]
    A_Q, A_K, A_V, B_Q, B_K, B_V = 0, 512, 640, 768, 1280, 1408
    cols = (head_cols(A_Q, pair) + head_cols(A_K, [0, 1]) + head_cols(B_Q, pair) + head_cols(B_K, [0, 1])
            + head_cols(A_V, [0, 1]) + head_cols(B_V, [0, 1]))
    rows = head_cols(0, pair) + head_cols(512, pair)
    gain_qk = np.concatenate([np.tile(i["a_q_norm"][0], 8), np.tile(i["a_k_norm"][0], 2),
                              np.tile(i["b_q_norm"][0], 8), np.tile(i["b_k_norm"][0], 2)])
    uq = i["mla_w_uq"][0].reshape(384, 8, 192)
    uq = np.concatenate([uq[:, :, :128].reshape(384, -1), uq[:, :, 128:].reshape(384, -1)], 1)
    ukv = i["mla_w_ukv"][0].reshape(256, 8, 256)
    ukv = np.concatenate([ukv[:, :, :128].reshape(256, -1), ukv[:, :, 128:].reshape(256, -1)], 1)
    gain_m = np.concatenate([i["mla_q_a_norm"][0], i["mla_kv_a_norm"][0], i["mla_k_rope_norm"][0],
                             i["mla_q_nope_norm"][0], i["mla_q_rope_norm"][0], i["mla_k_nope_norm"][0]])
    pos = np.arange(256)
    inv = (np.float32(10000.0) ** (-np.arange(0, 32, 2, dtype=np.float32) / np.float32(32))).astype(np.float32)
    ang = np.concatenate([(pos // 64).astype(np.float32)[:, None] * inv,
                          (pos % 64).astype(np.float32)[:, None] * inv], 1)
    cos, sin = np.cos(ang), np.sin(ang)
    rope = np.stack([np.repeat(cos, 2, 1), np.stack([-sin, sin], -1).reshape(256, 64)], 1)
    rope = rope.reshape(2, 128, 2, 64).transpose(1, 0, 2, 3)
    q, k = np.arange(128)[:, None], np.arange(128)[None, :]
    wmask = np.stack([np.where(k <= q, 0, MASKED), np.where(k >= q, 0, MASKED)], 1).astype(np.float32)
    keysT = i["peer_sub_keys"].transpose(0, 4, 1, 2, 3).reshape(layers, 128, 8, 256)
    arrays = {
        "x": i["x"][0], "ctx": i["ctx"][0],
        "cond": np.stack([i["c"][0], i["c_ctx"]]).reshape(2, 8, 128).transpose(2, 1, 0).reshape(128, 16),
        "mod_w": i["mod_w"], "mod_b2": np.repeat(i["mod_b"][:, None], 2, 1),
        "mix_norm": i["mix_norm"], "ffn_norm": i["ffn_norm"],
        "even_w_in": i["even_w_in"][0][:, cols], "even_w_out": i["even_w_out"][0][rows],
        "gain_qk": gain_qk, "b_sink": i["b_sink"][0][pair], "rope": rope, "wmask": wmask,
        "mla_w_in": i["mla_w_in"][0], "mla_w_uq": uq, "mla_w_ukv": ukv, "mla_w_out": i["mla_w_out"][0],
        "gain_m": gain_m, "peer_w_query": i["peer_w_query"], "keysT": keysT,
        "peer_u": i["peer_u"].reshape(-1, 1024), "peer_v": i["peer_v"].reshape(-1, 1024),
    }
    arrays = {k: np.ascontiguousarray(v) for k, v in arrays.items()}
    nc = bacc.Bacc("TRN2", target_bir_lowering=False, num_devices=1)
    aps = {k: nc.dram_tensor(f"in_{k}", v.shape, mybir.dt.from_np(v.dtype), kind="ExternalInput").ap()
           for k, v in arrays.items()}
    out = nc.dram_tensor("out", (256, 1024), F32, kind="ExternalOutput").ap()
    build(nc, aps, out)
    r = run(nc, [{f"in_{k}": v for k, v in arrays.items()}], core_ids=[0])
    return np.asarray(r.results[0]["out"]).reshape(1, 256, 1024)
```

```python
from contextlib import ExitStack

import concourse.bass as bass
from concourse import mybir

F32 = mybir.dt.float32
U32 = mybir.dt.uint32
ALU = mybir.AluOpType
ACT = mybir.ActivationFunctionType
AX = mybir.AxisListType

P = 128
D = 1024
KD = D // P
SEQ, CTX_LEN = 256, 256
LAT_TILES = SEQ // P
TILES = LAT_TILES + CTX_LEN // P
TOK = TILES * P
EPS = 1e-6
MASKED = -1e30
REMOVED = -3.0e38

HD = 64
QKH = 20
QKW = QKH * HD
EVEN_W = QKW + 4 * HD

QL, KVL, ROPE, NOPE, VD, MH = 384, 256, 64, 128, 128, 8
MLA_W = QL + KVL + ROPE

PH, PK, TOPK = 8, 128, 16
HALF = 8
EXPERTS = PK * PK
WCOLS = 256
SLOTS = 4
LAT_ORDER = (2, 3, 0, 1)
STRIP_TILES = (1, 2)
STRIPS = len(STRIP_TILES) * PH
MODC = 3 * D // STRIPS


def build(nc, a, out):
    with ExitStack() as ctx:
        def sb(name, shape, dt=F32):
            return ctx.enter_context(nc.sbuf_tensor(name, shape, dt))

        def sem(name):
            return ctx.enter_context(nc.semaphore(name))

        LINE_STRIPS = -(-2 * D // MODC)
        QK_CHUNKS = QKW // WCOLS

        x = sb("x", [P, TILES, D])
        h = sb("h", [P, TILES, D])
        hT = sb("hT", [P, 4096])
        arena = sb("arena", [P, 25088])
        weights = sb("weights", [P, SLOTS, KD * WCOLS])
        mod = sb("mod", [P, 4, D])
        gate = sb("gate", [P, 2, D])
        ident = sb("ident", [P, P])
        ones = sb("ones", [P, P])
        rope = sb("rope", [P, LAT_TILES, 2, HD])
        wmask = sb("wmask", [P, 2, P])
        sinks = sb("sinks", [P, 2, 8])
        cond = sb("cond", [P, 3, KD * 2])
        stat = sb("stat", [P, 64])
        heads_stat = sb("heads_stat", [P, 2, 80])
        soft = sb("soft", [P, 4, 64])
        eps = sb("eps", [P, 1])
        iota16 = sb("iota16", [P, TOPK])
        mod_cols = sb("mod_cols", [P, 2, 2, KD])
        norm_cols = sb("norm_cols", [P, 2, KD])
        nope_cols = sb("nope_cols", [P, 2])

        w0 = ctx.enter_context(nc.psum_tensor("w0", [P, 1024], F32))
        w1 = ctx.enter_context(nc.psum_tensor("w1", [P, 1024], F32))
        work = (w0, w1)
        ps_s = ctx.enter_context(nc.psum_tensor("ps_s", [P, 2, 512], F32))
        ps_o = ctx.enter_context(nc.psum_tensor("ps_o", [P, 1024], F32))

        mod_rows = nc.dram_tensor("mod_rows", (2, 2, 6 * D), F32).ap()

        def view(base, at, *dims):
            n = 1
            for d in dims:
                n *= d
            v = base[:, at:at + n]
            if len(dims) == 2:
                v = v.rearrange("p (a b) -> p a b", b=dims[1])
            if len(dims) == 3:
                v = v.rearrange("p (a b c) -> p a b c", b=dims[1], c=dims[2])
            if len(dims) == 4:
                v = v.rearrange("p (a b c d) -> p a b c d", b=dims[1], c=dims[2], d=dims[3])
            return v

        hTk = view(hT, 0, KD, TOK)
        probs = view(arena, 16384, 2, 512)
        probsT = view(arena, 17408, 2, 512)
        o_sb = view(arena, 18432, 1024)
        gated = view(arena, 19456, D)
        row = view(arena, 20480, D)
        bias = view(arena, 21504, D)
        mod_acc = view(arena, 20480, 2, 2, 512)
        bias_acc = view(arena, 16384, 3 * D)
        bias_acc5 = view(arena, 11264, D)
        gain = view(arena, 22528, D)
        pj = view(arena, 0, TILES, EVEN_W)
        qkT = view(arena, 6144, QKH // 2, TOK)
        sq = view(arena, 11264, TILES, QKW)
        gain_qk = view(arena, 23552, QKW)
        turned = view(arena, 19456, 4, HD)
        mod_acc1 = view(arena, 0, 2, D)
        bias_acc1 = view(arena, 2816, 3 * D)
        pm = view(arena, 0, TILES, MLA_W)
        qm = view(arena, 2816, LAT_TILES, MH * (NOPE + ROPE))
        kn = view(arena, 5888, TILES, MH * NOPE)
        vm = view(arena, 9984, TILES, MH * VD)
        qnT = view(arena, 14080, MH, SEQ)
        sq_m = view(arena, 2816, TILES, MLA_W)
        sq_q = (view(arena, 0, 1536), view(arena, 16384, 1536))
        sq_k = (view(arena, 0, D), view(arena, D, D), view(arena, 16384, D), view(arena, 16384 + D, D))
        cqT = view(arena, 19456, QL // P, SEQ)
        qpT = view(arena, 20480, MH // 2, SEQ)
        ckvT = view(arena, 21504, KVL // P, TOK)
        gain_m = view(arena, 23552, 1024)
        kpT = view(arena, 24576, TOK)
        knT = h[:, :, :].rearrange("p a b -> p (a b)").rearrange("p (h t) -> p h t", t=TOK)
        urows = view(arena, 0, HALF, D)
        vrows = view(arena, 8192, HALF, D)
        queryT = view(arena, 16384, TILES * PH + 1, 2 * P)
        modf = mod[:, :, :].rearrange("p a b -> p (a b)")
        keysT = view(modf, 0, PH + 1, 2 * P)
        mod_w1 = view(modf, 2304, KD, MODC)
        scratch = weights[:, 0:2, :].rearrange("p s n -> p (s n)")
        query_w = view(weights[:, 2, :], 0, KD, WCOLS)
        diag = view(scratch, 0, HALF, P)
        q_now = view(scratch, 1024, 2, P)
        left = view(scratch, 1280, 2, P)
        cand = view(scratch, 1536, TOPK, TOPK)
        cand_left = view(scratch, 1792, 256)
        onehot = view(scratch, 2048, 2, TOPK, TOPK)
        top_v = view(scratch, 2560, 2, TOPK)
        top_i = view(scratch, 2592, 2, TOPK).bitcast(U32)
        top_if = view(scratch, 2624, 2, TOPK)
        best_v = view(scratch, 2656, TOPK)
        best_p = view(scratch, 2672, TOPK).bitcast(U32)
        pos_u = view(scratch, 2688, 2, TOPK).bitcast(U32)
        pos_f = view(scratch, 2720, 2, TOPK)
        picked = view(scratch, 2752, 2, TOPK)
        flat = view(scratch, 2784, TOPK)
        idx = view(scratch, 2800, TOPK).bitcast(U32)
        idx_u = view(scratch, 2816, TOPK).bitcast(U32)
        idx_v = view(scratch, 2832, TOPK).bitcast(U32)
        neg_best = view(scratch, 2848, 1)
        esum = view(scratch, 2849, 1)
        erec = view(scratch, 2850, 1)
        expv = view(scratch, 2852, TOPK)
        g_next = view(scratch, 2868, TOPK)
        g_now = view(scratch, 2884, TOPK)
        dots = view(scratch, 2900, 2, HALF)
        acts = view(scratch, 2916, 2, HALF)
        wts = view(scratch, 2932, 2, HALF)
        row1 = view(scratch, 2948, MODC)
        bias1 = view(scratch, 3140, MODC)
        mod_lines = (view(arena, 19456, P)[0:4 * KD], view(scratch, 3456, P)[0:4 * KD])

        peer_tiles = (TILES, LAT_TILES)
        SUM1_AT = {6: 3, 11: 4}
        LATE_SUM = 20
        jobs = {}
        emptied_by = {"act": 0, "dve": 0}

        def plan(name, engine):
            emptied_by[engine] += 1
            jobs[name] = (len(jobs), engine, emptied_by[engine])

        units0 = [(t, k) for t in range(TILES) for k in range(16)]
        units1 = [(t, k) for t in range(LAT_TILES) for k in range(MH)]

        def plan_attention(layer, units):
            for n in range(len(units)):
                plan(("PT", layer, n), "act")
                if layer == 0 and n == LATE_SUM:
                    plan(("modsum", *mod_half(5)), "act")
                if layer == 1 and n in SUM1_AT:
                    plan(("modsum1", SUM1_AT[n]), "act")
                if n >= 2 and ends_tile(units, n - 2):
                    plan(("OT", layer, units[n - 2][0]), "act")
            plan(("OT", layer, units[-1][0]), "act")

        def ends_tile(units, n):
            return n + 1 < len(units) and units[n + 1][0] != units[n][0]

        def mod_half(i):
            return 2 + i // 2, i % 2

        for p in range(2):
            plan(("mod", p), "dve")
        plan(("cols", 0), "dve")
        for t in range(TILES):
            plan(("hT", 0, t), "act")
        for c in range(EVEN_W // WCOLS):
            plan(("proj", c), "act")
            if c:
                plan(("modsum", *mod_half(c - 1)), "act")
        for t in range(TILES):
            plan(("qkT", t, 0), "act")
            plan(("qkT", t, 1), "dve")
        plan_attention(0, units0)
        def plan_to_experts(layer):
            for t in range(peer_tiles[layer]):
                plan(("out", layer, t), "dve")
                if layer == 1 and t == 1:
                    plan(("modsum1", 5), "act")
                if t:
                    plan(("hT2", layer, t - 1), "act")
            for k in range(2):
                plan(("query", layer, k), "act")
            plan(("hT2", layer, peer_tiles[layer] - 1), "act")

        plan_to_experts(0)
        for half in range(2):
            plan(("modsum", 5, half), "act")
        plan(("cols", 1), "dve")
        for t in range(TILES):
            plan(("hT", 1, t), "act")
        for c in (1, 2, 0):
            plan(("down", c), "dve" if c % 2 else "act")
        for t in LAT_ORDER:
            plan(("latT", t), "act")
        for c in range(3):
            plan(("uq", c), "dve" if c % 2 else "act")
        for c in range(2):
            for t in range(TILES):
                plan(("ukv", c, t), "dve" if t % 2 else "act")
        for t in range(LAT_TILES):
            plan(("qnT", t), "act")
            plan(("qpT", t), "dve")
        for t in range(TILES):
            plan(("knT", t), "act")
        plan_attention(1, units1)
        plan_to_experts(1)

        def cols(w, kk, n, width):
            return w.rearrange("(k p) n -> p k n", p=P)[:, 0:kk, n:n + width]

        def mod_by_rows(p, half, kc):
            w = a["mod_w"][0].rearrange("(k p) n -> p k n", p=P)
            at = p * D + half * 512
            return w[:, kc * (KD // 2):(kc + 1) * (KD // 2), at:at + 512]

        stream = []
        for p in (0, 1):
            stream += [(("mod", p, c), cols(a["mod_w"][0], KD, p * D + c * WCOLS, WCOLS)) for c in range(4)]
        for c in range(EVEN_W // WCOLS):
            stream += [(("proj", c), cols(a["even_w_in"], KD, c * WCOLS, WCOLS))]
            stream += [(("modv", 2 + c // 2, c % 2, kc), mod_by_rows(2 + c // 2, c % 2, kc)) for kc in range(2)]
        stream += [(("modv", 5, half, kc), mod_by_rows(5, half, kc)) for half in range(2) for kc in range(2)]
        stream += [(("out", 0, c), cols(a["even_w_out"], KD, c * WCOLS, WCOLS)) for c in range(D // WCOLS)]
        first_slot = {0: 0, len(stream) + 2: 2}
        stream += [(("query", 0, c), cols(a["peer_w_query"][0], KD, c * WCOLS, WCOLS)) for c in range(2)]
        stream += [(("down", c), cols(a["mla_w_in"], KD, c * WCOLS, min(WCOLS, MLA_W - c * WCOLS)))
                   for c in (1, 2, 0)]
        stream += [(("uq", c), cols(a["mla_w_uq"], QL // P, c * 512, 512)) for c in range(3)]
        stream += [(("ukv", c), cols(a["mla_w_ukv"], KVL // P, c * D, D)) for c in range(2)]
        stream += [(("modv1", p, kc), a["mod_w"][1].rearrange("(k p) n -> p k n", p=P)[:, 2 * kc:2 * kc + 2, p * D:(p + 1) * D])
                   for p in range(3, 6) for kc in range(KD // 2)]
        stream += [(("out", 1, c), cols(a["mla_w_out"], KD, c * WCOLS, WCOLS)) for c in range(D // WCOLS)]
        stream += [(("query", 1, c), cols(a["peer_w_query"][1], KD, c * WCOLS, WCOLS)) for c in range(2)]
        place, had, there = {}, [0] * SLOTS, [None] * SLOTS
        for i, (name, _) in enumerate(stream):
            slot = first_slot.get(i, 0) if i in first_slot else (slot + 1) % SLOTS
            had[slot] += 1
            place[name] = (slot, had[slot], there[slot])
            there[slot] = name
        source = dict(stream)
        assert all(place["query", layer, k][0] == 2 + k for layer in range(2) for k in range(2))

        def chunk(name):
            _, kk, width = source[name].shape
            return view(weights[:, place[name][0], :], 0, kk, width)

        consts_in = sem("consts_in")
        made = sem("made")
        cond_in = sem("cond_in")
        cond_exp = sem("cond_exp")
        cond_silu = sem("cond_silu")
        w_in = [sem(f"w_in{s}") for s in range(SLOTS)]
        w_used = sem("w_used")
        filled = sem("filled")
        act_emptied = sem("act_emptied")
        dve_emptied = sem("dve_emptied")
        bias_in = sem("bias_in")
        row_out = sem("row_out")
        mod_in = {k: sem(f"in_{k}") for k in ("mix0", "ffn0", "mix1", "gate1", "ffn1")}
        mod_made = sem("mod_made")
        x_squared = sem("x_squared")
        x_rooted = sem("x_rooted")
        h_made = sem("h_made")
        bias_acc_in = sem("bias_acc_in")
        modv_used = sem("modv_used")
        acc_made = sem("acc_made")
        sq_made = sem("sq_made")
        sq_read = sem("sq_read")
        root_made = sem("root_made")
        roped = sem("roped")
        scores_made = sem("scores_made")
        scores_biased = sem("scores_biased")
        probs_made = sem("probs_made")
        pv_done = sem("pv_done")
        sink_shift = sem("sink_shift")
        sink_exp = sem("sink_exp")
        o_made = sem("o_made")
        x_mixed = sem("x_mixed")
        keys_in = sem("keys_in")
        query_w_in = sem("query_w_in")
        query_filled = sem("query_filled")
        query_emptied = sem("query_emptied")
        q_copied = sem("q_copied")
        keys_scored = sem("keys_scored")
        scores_taken = sem("scores_taken")
        best_made = sem("best_made")
        best_exp = sem("best_exp")
        idx_made = sem("idx_made")
        idx_taken = sem("idx_taken")
        idx_staged = sem("idx_staged")
        u_in = [sem(f"u_in{j}") for j in range(HALF)]
        v_in = [sem(f"v_in{j}") for j in range(HALF)]
        u_used = sem("u_used")
        v_used = sem("v_used")
        acts_made = sem("acts_made")
        wts_made = sem("wts_made")
        diag_made = sem("diag_made")
        y_read = sem("y_read")
        mod1_in = sem("mod1_in")
        mod1_sum = sem("mod1_sum")
        mod1_row = sem("mod1_row")
        mod1_out = sem("mod1_out")
        out_done = sem("out_done")
        held = {e: sem(f"held_{e}") for e in ("act", "dve", "pool")}

        block = ctx.enter_context(nc.Block())

        def wait_filled(eng, name):
            eng.wait_ge(filled, jobs[name][0] + 1)

        def wait_emptied(eng, name):
            _, engine, count = jobs[name]
            eng.wait_ge(act_emptied if engine == "act" else dve_emptied, count)

        def wait_multiplied(eng, name):
            if name[0] == "mod" and name[2] < 3:
                eng.wait_ge(w_used, 3 * name[1] + name[2] + 1)
            elif name[0] == "modv":
                _, p, half, kc = name
                eng.wait_ge(modv_used, 4 * (p - 2) + 2 * half + kc + 1)
            elif name[0] == "modv1":
                eng.wait_ge(modv_used, 16 + 4 * (name[1] - 3) + name[2] + 1)
            elif name[0] == "mod":
                wait_filled(eng, name[:2])
            elif name[0] == "out":
                wait_filled(eng, ("out", name[1], peer_tiles[name[1]] - 1))
            elif name[0] == "ukv":
                wait_filled(eng, (*name, TILES - 1))
            else:
                wait_filled(eng, name)

        def wait_chunk(eng, name):
            slot, count, _ = place[name]
            eng.wait_ge(w_in[slot], 16 * count)

        names = list(jobs)

        def buffer_free(pe, name):
            n = jobs[name][0]
            if n >= 2:
                wait_emptied(pe, names[n - 2])

        def buffer(name):
            return work[jobs[name][0] % 2]

        heads_before = (0, TILES * PH)
        n_const_loads = 9

        LOADS = {"mix0": 2, "ffn0": 1, "mix1": 2, "gate1": 1, "ffn1": 1}

        def wait_mod(eng, what):
            if what == "gain0":
                eng.wait_ge(mod_in["ffn0"], 16)
                return
            if what in LOADS and what != "ffn0":
                eng.wait_ge(mod_in[what], 16 * LOADS[what])
            if what == "gate0":
                wait_emptied(eng, ("modsum", 2, 1))
            if what == "ffn0":
                wait_emptied(eng, ("modsum", 4, 1))
            if what == "ffn1":
                wait_emptied(eng, ("modsum1", 4))
            if what == "gate1b":
                wait_emptied(eng, ("modsum1", 5))
            if what == "gate0b":
                wait_emptied(eng, ("modsum", 5, 1))

        H_BEFORE = {("hT", 0): 0, ("hT2", 0): 4, ("hT", 1): 8, ("hT2", 1): 12}
        H_MADE = {(0, 1): 8, (1, 1): 14}

        def experts_pool(pool, layer):
            G0 = heads_before[layer]
            pool.wait_ge(h_made, H_MADE[layer, 1])
            pool.dma_start(keysT[:, 0:PH, :], a["keysT"][layer]).then_inc(keys_in, 16)
            pool.dma_start(keysT[:, PH, :], a["keysT"][layer][:, 0, :]).then_inc(keys_in, 16)

            def gather(dst, table, index, landed):
                pool.indirect_dma_start(dst, None, table, bass.IndirectOffsetOnAxis(ap=index, axis=0)).then_inc(landed, 16)

            def gather_u(G, half, j, free):
                if free:
                    pool.wait_ge(u_used, 16 * G + (HALF * (half - 1) + j + 1))
                    pool.sem_inc(held["pool"], 1)
                gather(urows[:, j, :], a["peer_u"], idx_u[:, half * HALF + j:half * HALF + j + 1], u_in[j])

            def gather_v(G, half, j, free):
                if free:
                    pool.wait_ge(v_used, 16 * G + (HALF * (half - 1) + j + 1))
                    pool.sem_inc(held["pool"], 1)
                gather(vrows[:, j, :], a["peer_v"], idx_v[:, half * HALF + j:half * HALF + j + 1], v_in[j])

            def head(G, first):
                free = not (first and layer == 0)
                pool.wait_ge(idx_made, G + (layer + 1))
                pool.sem_inc(held["pool"], 1)
                if not first:
                    pool.tensor_copy(idx_v[:, HALF:TOPK], idx_u[:, HALF:TOPK]).then_inc(idx_staged, 1)
                pool.tensor_copy(idx_u[:, 0:HALF], idx[:, 0:HALF]).then_inc(idx_staged, 1)
                pool.wait_ge(idx_staged, 3 * G + 1)
                pool.sem_inc(held["pool"], 1)
                for j in range(HALF):
                    gather_u(G, 0, j, free)
                    if not first:
                        gather_v(G - 1, 1, j, True)
                pool.tensor_copy(idx_u[:, HALF:TOPK], idx[:, HALF:TOPK]).then_inc(idx_taken, 1)
                pool.tensor_copy(idx_v[:, 0:HALF], idx_u[:, 0:HALF]).then_inc(idx_staged, 1)
                pool.wait_ge(idx_taken, G + 1)
                pool.sem_inc(held["pool"], 1)
                pool.wait_ge(idx_staged, 3 * G + 2)
                pool.sem_inc(held["pool"], 1)
                for j in range(HALF):
                    gather_u(G, 1, j, True)
                    gather_v(G, 0, j, free)

            n_heads = peer_tiles[layer] * PH
            head(G0, True)
            with pool.Fori(1, n_heads, 1) as n:
                head(n + G0, False)
            G = G0 + n_heads
            pool.tensor_copy(idx_v[:, HALF:TOPK], idx_u[:, HALF:TOPK]).then_inc(idx_staged, 1)
            pool.wait_ge(idx_staged, 3 * G)
            for j in range(HALF):
                gather_v(G - 1, 1, j, True)

        def empty(eng, name, dst, src):
            wait_filled(eng, name)
            if jobs[name][1] == "act":
                eng.activation(dst, src, ACT.Copy).then_inc(act_emptied, 1)
            else:
                eng.tensor_copy(dst, src).then_inc(dve_emptied, 1)

        def chunk_stats(which, c):
            return heads_stat[:, which, :].rearrange("p (t h) -> p t h", h=QKH)[:, :, 4 * c:4 * c + 4]

        def keys_of(layer, t):
            return TOK if t < LAT_TILES else CTX_LEN

        def empty_query(layer, k, src, tiles):
            src = src[:, :].rearrange("p (s t n) -> p t s n", s=2, n=P)[:, 0:tiles]
            dst = view(arena, 16384, peer_tiles[layer], PH, 2 * P)[:, 0:tiles, bass.ds(k, 1), :]
            return nc.scalar.activation(dst.rearrange("p t a (s n) -> p t (a s) n", n=P), src, ACT.Copy)

        def experts_act(act, layer, empty_modsum, root, shift_scale):
            G0 = heads_before[layer]
            n_heads = peer_tiles[layer] * PH

            def copy_query(G, n):
                if not (isinstance(G, int) and G == 0):
                    act.wait_ge(keys_scored, G)
                    act.sem_inc(held["act"], 1)
                act.activation(q_now, queryT[:, bass.ds(n, 1), :].rearrange("p a (s t) -> p (a s) t", t=P),
                               ACT.Copy).then_inc(q_copied, 1)

            def exp_best(G):
                act.wait_ge(best_made, G + 1)
                act.activation(expv, best_v, ACT.Exp, bias=neg_best, accum_out=esum).then_inc(best_exp, 1)

            def gelu(G, half):
                act.wait_ge(u_used, 16 * G + HALF * (half + 1))
                act.activation(acts[:, half, :], dots[:, half, :], ACT.Gelu).then_inc(acts_made, 1)

            def diags(G, half):
                act.wait_ge(wts_made, 2 * G + half + 1)
                for j in range(HALF):
                    if isinstance(G, int):
                        used = 16 * G + HALF * half - HALF + j + 1
                    else:
                        used = 16 * G + (HALF * half - HALF + j + 1)
                    if not (isinstance(used, int) and used <= 0):
                        act.wait_ge(v_used, used)
                    act.activation(diag[:, j, :], ident[:, :], ACT.Copy,
                                   scale=wts[:, half, j:j + 1]).then_inc(diag_made, 1)

            def next_query(q, k):
                act.wait_ge(query_filled, q + (PH * layer - 1))
                act.sem_inc(held["act"], 1)
                empty_query(layer, k, work[0], peer_tiles[layer]).then_inc(query_emptied, 1)
                act.drain()

            act.drain()
            act.activation(queryT[:, n_heads, :], queryT[:, 0, :], ACT.Copy)
            act.drain()
            E0 = G0 + layer
            copy_query(E0, 0)
            last_h = ("hT2", layer, peer_tiles[layer] - 1)
            empty(act, last_h, hTk[:, :, (peer_tiles[layer] - 1) * P:peer_tiles[layer] * P],
                  buffer(last_h)[:, :].rearrange("p (k t) -> p k t", t=P))
            if layer == 0:
                act.wait_ge(x_mixed, TILES)
                for half in range(2):
                    empty_modsum(5, half, gate[:, :, :])
            exp_best(E0)

            def body(n, first, query_head=None):
                G = G0 + n
                if not first:
                    gelu(G - 1, 1)
                    diags(G - 1, 1)
                if query_head is not None:
                    next_query(n + 1, query_head)
                copy_query(E0 + n + 1, n + 1)
                exp_best(E0 + n + 1)
                gelu(G, 0)
                diags(G, 0)

            body(0, True)
            with act.Fori(1, PH - 1, 1) as n:
                body(n, False, n + 1)
            body(PH - 1, False, 0)
            body(PH, False, 1)
            if layer == 0:
                with act.Fori(PH + 1, 3 * PH, 1) as n:
                    body(n, False)
                body(3 * PH, False)
                for t in range(3):
                    root("hT", 1, t)
                shift_scale(1, range(3))
                with act.Fori(3 * PH + 1, n_heads, 1) as n:
                    body(n, False)
            else:
                with act.Fori(PH + 1, n_heads, 1) as n:
                    body(n, False)
            gelu(G0 + n_heads - 1, 1)
            diags(G0 + n_heads - 1, 1)

        def experts_pe(pe, layer, silu, mod_sum, turn_lines, turn_h):
            G0 = heads_before[layer]
            E0 = G0 + layer
            tiles = peer_tiles[layer]

            def score_keys(E, k):
                pe.wait_ge(q_copied, E + 1)
                if not (isinstance(E, int) and E == 0):
                    pe.wait_ge(scores_taken, E)
                for s in range(2):
                    keys = keysT[:, bass.ds(k, 1), s * P:(s + 1) * P].rearrange("p a n -> p (a n)")
                    mm = pe.matmul(ps_s[:, 0, s * P:(s + 1) * P], q_now[:, s, :], keys, start=True, stop=True)
                mm.then_inc(keys_scored, 1)

            def sum_half(G, half, starts, stops, beside=()):
                for j in range(HALF):
                    pe.wait_ge(v_in[j], 16 * (2 * G + half) + 16)
                    pe.wait_ge(diag_made, 16 * G + (HALF * half + j + 1))
                    for b in range(2):
                        mm = pe.matmul(ps_o[:, b * 512:(b + 1) * 512], diag[:, j, :], vrows[:, j, b * 512:(b + 1) * 512],
                                       start=(starts and j == 0), stop=(stops and j == HALF - 1), skip_group_check=True)
                    mm.then_inc(v_used, 1)
                    for product in beside:
                        product(j)

            def query(q, s):
                def product(kk):
                    if s == 0 and kk == 0:
                        done = q - 2 + PH * layer
                        pe.wait_ge(query_w_in, 16 * done + 16)
                        if not (isinstance(done, int) and done == 0):
                            pe.wait_ge(query_emptied, done)
                    mm = pe.matmul(work[0][:, s * 512:s * 512 + tiles * P], query_w[:, kk, s * P:(s + 1) * P],
                                   hTk[:, kk, 0:tiles * P], start=(kk == 0), stop=(kk == KD - 1),
                                   skip_group_check=True)
                    if s and kk == KD - 1:
                        mm.then_inc(query_filled, 1)
                return (product,)

            def mod_strip(n):
                def product(k):
                    if k == 0:
                        pe.wait_ge(mod1_in, 32 * n + 32)
                        if not (isinstance(n, int) and n == 0):
                            pe.wait_ge(mod1_row, n)
                    mm = pe.matmul(ps_s[0:2, 1, 0:MODC], silu[:, k, :], mod_w1[:, k, :],
                                   start=(k == 0), stop=(k == KD - 1), skip_group_check=True)
                    if k == KD - 1:
                        mm.then_inc(mod1_sum, 1)
                return (product,)

            assert HALF == KD

            pe.wait_ge(keys_in, 32 * (layer + 1))
            score_keys(E0, 0)
            if layer == 0:
                for half in range(2):
                    mod_sum(5, half)
                wait_emptied(pe, ("modsum", 5, 1))
            wait_emptied(pe, ("hT2", layer, tiles - 1))
            for t in range(tiles):
                n0 = t * PH

                strips = layer == 0 and t in STRIP_TILES

                def head(k, queries):
                    score_keys(k + (E0 + n0 + 1), k + 1)
                    sum_half(k + (G0 + n0 - 1), 1, False, False,
                             mod_strip(k + (n0 - PH)) if strips else ())
                    sum_half(k + (G0 + n0), 0, False, False,
                             query(k + 2, 0) + query(k + 2, 1) if queries else ())

                if t == 0:
                    for product in query(2, 0) + query(2, 1):
                        for k in range(KD):
                            product(k)
                score_keys(E0 + n0 + 1, 1)
                if layer == 0 and t == 3:
                    pe.wait_ge(query_emptied, PH)
                    turn_lines(1)
                if t:
                    sum_half(G0 + n0 - 1, 1, False, True, mod_strip(n0 - PH) if strips else ())
                    pe.wait_ge(y_read, (0 if layer == 0 else TILES) + t)
                sum_half(G0 + n0, 0, True, False)
                if layer == 0 and t == 3:
                    turn_h("hT", 1, range(3))
                if t == 0:
                    with pe.Fori(1, PH - 2, 1) as k:
                        head(k, True)
                    head(PH - 2, True)
                    head(PH - 1, True)
                else:
                    with pe.Fori(1, PH, 1) as k:
                        head(k, False)
            sum_half(G0 + tiles * PH - 1, 1, False, True)

        def experts_dve(dve, layer, make_cols, over_rms):
            G0 = heads_before[layer]
            E0 = G0 + layer
            tiles = peer_tiles[layer]

            def choose(E):
                s = ps_s[:, 0, 0:2 * P].rearrange("p (s n) -> p s n", n=PK)
                dve.wait_ge(keys_scored, E + 1)
                dve.sem_inc(held["dve"], 1)
                for i in range(2):
                    dve.max(top_v[:, i, 0:8], s[:, i, :])
                dve.drain()
                for i in range(2):
                    dve.max_index(top_i[:, i, 0:8], top_v[:, i, 0:8], s[:, i, :])
                    ins = dve.match_replace(left[:, i, :], top_v[:, i, 0:8], s[:, i, :], REMOVED)
                ins.then_inc(scores_taken, 1)
                dve.drain()
                for i in range(2):
                    dve.max(top_v[:, i, 8:16], left[:, i, :])
                dve.drain()
                for i in range(2):
                    dve.max_index(top_i[:, i, 8:16], top_v[:, i, 8:16], left[:, i, :])
                dve.tensor_tensor(cand, top_v[:, 0, :].unsqueeze(2).broadcast_to([P, TOPK, TOPK]),
                                  top_v[:, 1, :].unsqueeze(1).broadcast_to([P, TOPK, TOPK]), ALU.add)
                dve.drain()
                dve.tensor_copy(top_if, top_i)
                flat_cand = cand.rearrange("p a b -> p (a b)")
                dve.max(best_v[:, 0:8], flat_cand)
                dve.drain()
                dve.max_index(best_p[:, 0:8], best_v[:, 0:8], flat_cand)
                dve.match_replace(cand_left, best_v[:, 0:8], flat_cand, REMOVED)
                dve.tensor_scalar(neg_best, best_v[:, 0:1], -1.0, None, ALU.mult)
                dve.drain()
                dve.max(best_v[:, 8:16], cand_left).then_inc(best_made, 1)
                dve.drain()
                dve.max_index(best_p[:, 8:16], best_v[:, 8:16], cand_left)
                dve.drain()
                dve.tensor_scalar(pos_u[:, 0, :], best_p, 4, None, ALU.logical_shift_right)
                dve.tensor_scalar(pos_u[:, 1, :], best_p, 15, None, ALU.bitwise_and)
                dve.drain()
                dve.tensor_copy(pos_f, pos_u)
                dve.drain()
                dve.tensor_tensor(onehot.rearrange("p s k a -> p (s k) a"),
                                  pos_f.rearrange("p s k -> p (s k)").unsqueeze(2).broadcast_to([P, 2 * TOPK, TOPK]),
                                  iota16[:, :].unsqueeze(1).broadcast_to([P, 2 * TOPK, TOPK]), ALU.is_equal)
                dve.drain()
                dve.tensor_tensor(onehot, onehot, top_if.unsqueeze(2).broadcast_to([P, 2, TOPK, TOPK]), ALU.mult)
                dve.drain()
                dve.tensor_reduce(picked.rearrange("p s k -> p (s k)"), onehot.rearrange("p s k a -> p (s k) a"),
                                  AX.X, ALU.add)
                dve.drain()
                dve.scalar_tensor_tensor(out=flat, in0=picked[:, 0, :], scalar=float(PK), in1=picked[:, 1, :],
                                         op0=ALU.mult, op1=ALU.add)
                dve.drain()
                if not (isinstance(E, int) and E == 0):
                    dve.wait_ge(idx_taken, E - layer)
                dve.tensor_scalar(idx, flat, float(layer * EXPERTS), None, ALU.add).then_inc(idx_made, 1)
                dve.wait_ge(best_exp, E + 1)
                dve.reciprocal(erec, esum)
                dve.drain()
                dve.tensor_scalar(g_next, expv, erec, None, ALU.mult)
                dve.drain()

            def dot(G, half, t, js):
                for j in js:
                    dve.wait_ge(u_in[j], 16 * (2 * G + half) + 16)
                    if j == 0 and not (isinstance(G, int) and G == 0):
                        dve.wait_ge(acts_made, 2 * G + half - 1)
                    u = urows[:, j, :]
                    dve.tensor_tensor_reduce(out=u, in0=u, in1=h[:, t, :], scale=1.0, scalar=0.0, op0=ALU.mult,
                                             op1=ALU.add, accum_out=dots[:, half, j:j + 1]).then_inc(u_used, 1)

            def weigh(G, half):
                dve.wait_ge(acts_made, 2 * G + half + 1)
                if not (isinstance(G, int) and G == 0):
                    dve.wait_ge(diag_made, 16 * G + (HALF * half - HALF))
                dve.tensor_tensor(wts[:, half, :], acts[:, half, :], g_now[:, half * HALF:(half + 1) * HALF],
                                  ALU.mult).then_inc(wts_made, 1)

            def add_tile(t):
                dve.wait_ge(v_used, 16 * (G0 + (t + 1) * PH))
                wait_mod(dve, f"gate{layer}b")
                y = h[:, t, :]
                of_tile = gate[:, t // LAT_TILES if layer == 0 else 1, :]
                dve.tensor_tensor(y, ps_o[:, :], of_tile, ALU.mult)
                dve.drain()
                dve.tensor_tensor(x[:, t, :], x[:, t, :], y, ALU.add).then_inc(y_read, 1)
                dve.drain()

            def strip(n):
                dve.wait_ge(mod1_sum, n + 1)
                dve.wait_ge(mod1_in, 32 * n + 32)
                if not (isinstance(n, int) and n == 0):
                    dve.wait_ge(mod1_out, 16 * n)
                dve.tensor_tensor(row1[0:2, :], ps_s[0:2, 1, 0:MODC], bias1[0:2, :], ALU.add).then_inc(mod1_row, 1)

            def head(n, t, first, in_tile):
                G = n + G0
                if first:
                    dot(G, 0, t, range(HALF))
                    dve.tensor_copy(g_now, g_next)
                    dve.drain()
                    choose(n + (E0 + 1))
                else:
                    dot(G, 0, t, range(4))
                    weigh(G - 1, 1)
                    dve.drain()
                    dve.tensor_copy(g_now, g_next)
                    dve.drain()
                    choose(n + (E0 + 1))
                    dot(G, 0, t, range(4, HALF))
                dot(G, 1, t, range(4))
                weigh(G, 0)
                if not in_tile and t:
                    add_tile(t - 1)
                    if layer == 0 and t == 3:
                        make_cols(1)
                        for tile in range(3):
                            over_rms(1, tile)
                dot(G, 1, t, range(4, HALF))
                if layer == 0 and t in STRIP_TILES:
                    strip(n - PH)

            choose(E0)
            for t in range(tiles):
                head(t * PH, t, t == 0, False)
                with dve.Fori(1, PH, 1) as k:
                    head(k + t * PH, t, False, True)
            weigh(G0 + tiles * PH - 1, 1)
            add_tile(tiles - 1)
        @block.sync
        def _(sp):
            sp.dma_start(cond[:, 0, :], a["cond"]).then_inc(cond_in, 16)

            def load(names_):
                for name in names_:
                    slot, _, before = place[name]
                    if before:
                        wait_multiplied(sp, before)
                    sp.dma_start(chunk(name), source[name]).then_inc(w_in[slot], 16)

            order = [name for name, _ in stream]
            load(order[:2])
            for t in range(LAT_TILES):
                sp.dma_start(x[:, t, :], a["x"][t * P:(t + 1) * P, :]).then_inc(consts_in, 16)
                sp.dma_start(x[:, LAT_TILES + t, :], a["ctx"][t * P:(t + 1) * P, :]).then_inc(consts_in, 16)
            sp.dma_start(rope[:, :, :, :], a["rope"]).then_inc(consts_in, 16)
            sp.dma_start(wmask[:, :, :], a["wmask"]).then_inc(consts_in, 16)
            sp.dma_start(sinks[:, 0, :], a["b_sink"].partition_broadcast(P)).then_inc(consts_in, 16)
            sp.dma_start(norm_cols[:, :, :], a["norm_cols"]).then_inc(consts_in, 16)
            sp.dma_start(nope_cols[:, :], a["nope_cols"]).then_inc(consts_in, 16)
            first1 = order.index(("down", 1))
            load(order[2:first1])

            def load_query(layer, k):
                src = a["peer_w_query"][layer].rearrange("(k p) n -> p k n", p=P)
                sp.dma_start(query_w, src[:, :, bass.ds(k * WCOLS, WCOLS)]).then_inc(query_w_in, 16)

            def load_loop_queries(layer):
                load_query(layer, 2)
                with sp.Fori(1, PH - 2, 1) as n:
                    sp.wait_ge(query_filled, n + PH * layer)
                    load_query(layer, n + 2)
                for n in range(PH - 2, PH):
                    sp.wait_ge(query_filled, n + PH * layer)
                    load_query(layer, n - (PH - 2))

            sp.wait_ge(h_made, H_MADE[0, 1])
            wait_filled(sp, ("query", 0, 1))

            def store_strip(n):
                sp.wait_ge(mod1_row, n + 1)
                sp.dma_start(mod_rows[1, :, bass.ds(n * MODC, MODC)], row1[0:2, :]).then_inc(mod1_out, 16)

            def strip(n, first):
                at = bass.ds(n * MODC, MODC)
                if not first:
                    sp.wait_ge(mod1_sum, n)
                sp.dma_start(mod_w1, a["mod_w"][1].rearrange("(k p) n -> p k n", p=P)[:, :, at]).then_inc(mod1_in, 16)
                if not first:
                    store_strip(n - 1)
                sp.dma_start(bias1[0:2, :], a["mod_b2"][1, :, at]).then_inc(mod1_in, 16)

            load_loop_queries(0)
            strip(0, True)
            with sp.Fori(1, LINE_STRIPS + 2, 1) as n:
                strip(n, False)
            sp.wait_ge(mod1_out, 16 * LINE_STRIPS)
            for who in range(2):
                src = mod_rows[1, who, 0:2 * D].rearrange("(q n) -> q n", n=P)
                sp.dma_start(mod_lines[1][who * 2 * KD:(who + 1) * 2 * KD], src).then_inc(mod_in["mix1"], 16)
            with sp.Fori(LINE_STRIPS + 2, STRIPS, 1) as n:
                strip(n, False)
            store_strip(STRIPS - 1)
            sp.wait_ge(y_read, TILES)
            sp.wait_ge(mod1_out, 16 * STRIPS)
            load(order[first1:])
            wait_filled(sp, ("query", 1, 1))
            load_loop_queries(1)
            for t in range(LAT_TILES):
                sp.wait_ge(y_read, TILES + t + 1)
                sp.dma_start(out[t * P:(t + 1) * P, :], x[:, t, :]).then_inc(out_done, 16)
            sp.wait_ge(out_done, 16 * LAT_TILES)
            sp.wait_ge(mod1_out, 16 * STRIPS)

        @block.gpsimd
        def _(pool):
            pool.memset(ident[:, :], 0.0).then_inc(made, 1)
            pool.wait_ge(made, 1)
            pool.affine_select(out=ident[:, :], in_=ident[:, :], compare_op=ALU.not_equal, fill=1.0,
                               base=0, pattern=[[-1, P]], channel_multiplier=1).then_inc(made, 1)
            pool.iota(iota16[:, :], [[1, TOPK]], base=0, channel_multiplier=0,
                      allow_small_or_imprecise_dtypes=True).then_inc(made, 1)
            pool.memset(eps[:, :], EPS).then_inc(made, 1)
            pool.memset(ones[:, :], 1.0).then_inc(made, 1)

            def broadcast(what, dst, src):
                pool.dma_start(dst, src.partition_broadcast(P)).then_inc(mod_in[what], 16)

            def piece(layer, who, p):
                return mod_rows[layer, who, p * D:(p + 1) * D]

            def load_lines(what, layer):
                for who in range(2):
                    src = mod_rows[layer, who, 0:2 * D].rearrange("(q n) -> q n", n=P)
                    pool.dma_start(mod_lines[layer][who * 2 * KD:(who + 1) * 2 * KD], src).then_inc(mod_in[what], 16)

            def make_rows(pieces):
                for p in pieces:
                    if p:
                        pool.wait_ge(dve_emptied, jobs[("mod", p - 1)][2])
                    pool.dma_start(bias[0:2, :], a["mod_b2"][0, :, p * D:(p + 1) * D]).then_inc(bias_in, 16)
                    wait_emptied(pool, ("mod", p))
                    pool.dma_start(mod_rows[0, :, p * D:(p + 1) * D], row[0:2, :]).then_inc(row_out, 16)
                    pool.wait_ge(row_out, 16 * (p + 1))

            pool.dma_start(gain_qk, a["gain_qk"].partition_broadcast(P)).then_inc(bias_in, 16)
            pool.dma_start(bias_acc[0:1, :], a["mod_b2"][0, 0:1, 2 * D:5 * D]).then_inc(bias_acc_in, 16)
            make_rows((0, 1))
            load_lines("mix0", 0)
            broadcast("ffn0", gain, a["ffn_norm"][0])
            pool.wait_ge(roped, QK_CHUNKS)
            pool.dma_start(bias_acc5[0:1, :], a["mod_b2"][0, 0:1, 5 * D:6 * D]).then_inc(bias_acc_in, 16)
            experts_pool(pool, 0)
            pool.wait_ge(y_read, TILES)
            pool.wait_ge(mod1_out, 16 * STRIPS)
            pool.dma_start(gain_m, a["gain_m"].partition_broadcast(P)).then_inc(bias_in, 16)
            broadcast("gate1", gate[:, 0, :], piece(1, 0, 2))
            broadcast("ffn1", gain, a["ffn_norm"][1])
            wait_emptied(pool, ("qpT", LAT_TILES - 1))
            wait_emptied(pool, ("knT", TILES - 1))
            pool.dma_start(bias_acc1[0:1, :], a["mod_b2"][1, 0:1, 3 * D:6 * D]).then_inc(bias_acc_in, 16)
            experts_pool(pool, 1)

        @block.scalar
        def _(act):
            act.wait_ge(cond_in, 16)
            act.activation(cond[:, 1, :], cond[:, 0, :], ACT.Exp, scale=-1.0).then_inc(cond_exp, 1)
            act.wait_ge(consts_in, 16 * n_const_loads)
            act.wait_ge(made, 5)

            def root(kind, layer, t):
                act.wait_ge(x_squared, H_BEFORE[kind, layer] + t + 1)
                act.activation(stat[:, 8 + t:9 + t], stat[:, t:t + 1], ACT.Sqrt, bias=eps[:, :],
                               scale=1.0 / D).then_inc(x_rooted, 1)

            def shift_scale(layer, tiles):
                wait_emptied(act, ("cols", layer))
                for t in tiles:
                    name = ("hT", layer, t)
                    who = t // LAT_TILES
                    wait_filled(act, name)
                    for k in range(KD):
                        ins = act.activation(hTk[:, k, t * P:(t + 1) * P], buffer(name)[:, k * P:(k + 1) * P],
                                             ACT.Identity, bias=mod_cols[:, who, 0, k:k + 1],
                                             scale=mod_cols[:, who, 1, k:k + 1])
                    ins.then_inc(act_emptied, 1)

            def empty_hT(layer, kind, tiles):
                for t in tiles:
                    name = (kind, layer, t)
                    empty(act, name, hTk[:, :, t * P:(t + 1) * P],
                          buffer(name)[:, :].rearrange("p (k t) -> p k t", t=P))

            def attention(layer, units, scale, sink):
                base = 0 if layer == 0 else len(units0)

                def exp(n):
                    t, k = units[n]
                    act.wait_ge(scores_biased, base + n + 1)
                    if n >= 2:
                        wait_filled(act, ("PT", layer, n - 2))
                    kk = keys_of(layer, t)
                    act.activation(probs[:, n % 2, 0:kk], ps_s[:, n % 2, 0:kk], ACT.Exp, scale=scale,
                                   bias=soft[:, 1, n:n + 1], accum_out=soft[:, 2, n:n + 1]).then_inc(probs_made, 1)
                    if sink and k == 15:
                        act.wait_ge(sink_shift, t + 1)
                        act.activation(stat[:, 24:32], stat[:, 16:24], ACT.Exp).then_inc(sink_exp, 1)

                def turned_out(t):
                    name = ("OT", layer, t)
                    empty(act, name, hTk[:, :, t * P:(t + 1) * P],
                          buffer(name)[:, :].rearrange("p (k t) -> p k t", t=P))

                exp(0)
                for n, (t, k) in enumerate(units):
                    if n + 1 < len(units):
                        exp(n + 1)
                    if n >= 2:
                        act.wait_ge(pv_done, base + n - 1)
                    kk = keys_of(layer, t)
                    name = ("PT", layer, n)
                    empty(act, name, probsT[:, n % 2, 0:kk], buffer(name)[:, 0:kk])
                    if layer == 0 and n == LATE_SUM:
                        empty_modsum(*mod_half(5), mod_places[mod_half(5)[0]])
                    if layer == 1 and n in SUM1_AT:
                        empty_modsum1(SUM1_AT[n])
                    if n >= 2 and ends_tile(units, n - 2):
                        turned_out(units[n - 2][0])
                turned_out(units[-1][0])

            def empty_modsum1(p):
                name = ("modsum1", p)
                empty(act, name, {3: mod[:, 1, :], 4: mod[:, 0, :], 5: gate[:, 1, :]}[p], buffer(name)[:, :])

            def empty_modsum(p, half, dst):
                name = ("modsum", p, half)
                empty(act, name, dst[:, :, half * 512:(half + 1) * 512],
                      buffer(name)[:, :].rearrange("p (w n) -> p w n", n=512))

            def to_experts(layer):
                root("hT2", layer, 0)
                for t in range(1, peer_tiles[layer]):
                    if layer == 1:
                        empty_modsum1(5)
                    empty_hT(layer, "hT2", (t - 1,))
                    root("hT2", layer, t)
                for k in range(2):
                    wait_filled(act, ("query", layer, k))
                    empty_query(layer, k, buffer(("query", layer, k)), 1).then_inc(act_emptied, 1)
                experts_act(act, layer, empty_modsum, root, shift_scale)

            for t in range(TILES):
                root("hT", 0, t)
            shift_scale(0, range(TILES))
            shifts = mod[:, :, :].rearrange("p (w two) n -> p w two n", two=2)
            mod_places = {2: gate[:, :, :], 3: shifts[:, :, 1], 4: shifts[:, :, 0]}
            for c in range(EVEN_W // WCOLS):
                name = ("proj", c)
                empty(act, name, pj[:, :, c * WCOLS:(c + 1) * WCOLS],
                      buffer(name)[:, :].rearrange("p (t n) -> p t n", n=WCOLS))
                if c < QK_CHUNKS:
                    act.drain()
                    for t in range(TILES):
                        for n in range(4):
                            at = slice(c * WCOLS + n * HD, c * WCOLS + n * HD + HD)
                            act.activation(sq[:, t, at], pj[:, t, at], ACT.Square,
                                           accum_out=heads_stat[:, 0, t * QKH + 4 * c + n:t * QKH + 4 * c + n + 1])
                    act.drain()
                    act.activation(chunk_stats(1, c), chunk_stats(0, c), ACT.Sqrt, bias=eps[:, :],
                                   scale=1.0 / HD).then_inc(root_made, 1)
                if c:
                    p, half = mod_half(c - 1)
                    empty_modsum(p, half, mod_places[p])
            for t in range(TILES):
                name = ("qkT", t, 0)
                empty(act, name, qkT[:, 0:8, t * P:(t + 1) * P], buffer(name)[:, :].rearrange("p (k t) -> p k t", t=P))
            attention(0, units0, HD ** -0.5, True)
            to_experts(0)
            root("hT", 1, 3)
            shift_scale(1, (3,))
            name = ("down", 2)
            width = chunk(name).shape[2]
            empty(act, name, pm[:, :, 2 * WCOLS:2 * WCOLS + width],
                  buffer(name)[:, :].rearrange("p (t n) -> p t n", n=WCOLS)[:, :, 0:width])

            def sum_squares(c, tiles):
                at, width = ((0, QL), (QL, KVL), (QL + KVL, ROPE))[c]
                for t in tiles:
                    act.activation(sq_m[:, t, at:at + width], pm[:, t, at:at + width], ACT.Square,
                                   accum_out=heads_stat[:, 0, c * 4 + t:c * 4 + t + 1])
                act.drain()
                of = slice(c * 4 + tiles[0], c * 4 + tiles[0] + len(tiles))
                return act.activation(heads_stat[:, 1, of], heads_stat[:, 0, of], ACT.Sqrt, bias=eps[:, :],
                                      scale=1.0 / width)

            wait_emptied(act, ("down", 1))
            act.drain()
            sum_squares(1, range(TILES))
            sum_squares(2, range(TILES)).then_inc(root_made, 1)
            name = ("down", 0)
            empty(act, name, pm[:, 0:LAT_TILES, 0:WCOLS],
                  buffer(name)[:, 0:LAT_TILES * WCOLS].rearrange("p (t n) -> p t n", n=WCOLS))
            act.drain()
            sum_squares(0, range(LAT_TILES)).then_inc(root_made, 1)
            for t in LAT_ORDER:
                name = ("latT", t)
                b = buffer(name)[:, :].rearrange("p (k t) -> p k t", t=P)
                wait_filled(act, name)
                at = slice(t * P, (t + 1) * P)
                if t < LAT_TILES:
                    act.activation(cqT[:, :, at], b[:, 0:3, :], ACT.Copy)
                act.activation(ckvT[:, :, at], b[:, 3:5, :], ACT.Copy)
                act.activation(kpT[:, at], b[:, 5, :], ACT.Copy).then_inc(act_emptied, 1)
            for c in (0, 2):
                name = ("uq", c)
                empty(act, name, qm[:, :, c * 512:(c + 1) * 512], buffer(name)[:, :].rearrange("p (t n) -> p t n", n=512))
            wait_emptied(act, ("uq", 1))
            act.drain()
            for t in range(LAT_TILES):
                act.activation(sq_q[t], qm[:, t, :], ACT.Square).then_inc(sq_made, 1)
            empty(act, ("ukv", 0, 0), kn[:, 0, :], buffer(("ukv", 0, 0))[:, :])
            act.wait_ge(sq_read, LAT_TILES)
            act.activation(heads_stat[:, 1, 0:16], heads_stat[:, 0, 0:16], ACT.Sqrt, bias=eps[:, :], scale=1.0 / NOPE)
            act.activation(heads_stat[:, 1, 16:32], heads_stat[:, 0, 16:32], ACT.Sqrt, bias=eps[:, :],
                           scale=1.0 / ROPE).then_inc(root_made, 1)
            for t in range(TILES):
                if t == 2:
                    empty(act, ("ukv", 0, 2), kn[:, 2, :], buffer(("ukv", 0, 2))[:, :])
                if t % 2:
                    wait_emptied(act, ("ukv", 0, t))
                act.drain()
                act.activation(sq_k[t], kn[:, t, :], ACT.Square).then_inc(sq_made, 1)
            empty(act, ("ukv", 1, 0), vm[:, 0, :], buffer(("ukv", 1, 0))[:, :])
            act.wait_ge(sq_read, LAT_TILES + TILES)
            act.activation(heads_stat[:, 1, 32:64], heads_stat[:, 0, 32:64], ACT.Sqrt, bias=eps[:, :],
                           scale=1.0 / NOPE).then_inc(root_made, 1)
            empty(act, ("ukv", 1, 2), vm[:, 2, :], buffer(("ukv", 1, 2))[:, :])

            def empty_scaled(name, dst, gain_):
                wait_filled(act, name)
                act.activation(dst, buffer(name)[:, :].rearrange("p (k t) -> p k t", t=P), ACT.Copy,
                               scale=gain_).then_inc(act_emptied, 1)

            act.wait_ge(consts_in, 16 * n_const_loads)
            for t in range(LAT_TILES):
                empty_scaled(("qnT", t), qnT[:, :, t * P:(t + 1) * P], nope_cols[:, 0:1])
            for t in range(TILES):
                empty_scaled(("knT", t), knT[:, :, t * P:(t + 1) * P], nope_cols[:, 1:2])
            attention(1, units1, (NOPE + ROPE) ** -0.5, False)
            to_experts(1)

        @block.tensor
        def _(pe):
            pe.wait_ge(made, 5)
            pe.wait_ge(cond_silu, 1)
            silu = cond[:, 2, :].rearrange("p (k w) -> p k w", w=2)

            def mod_rows_job(p):
                name = ("mod", p)
                buffer_free(pe, name)
                for c in range(4):
                    wait_chunk(pe, ("mod", p, c))
                    for k in range(KD):
                        mm = pe.matmul(buffer(name)[0:2, c * WCOLS:(c + 1) * WCOLS], silu[:, k, :],
                                       chunk(("mod", p, c))[:, k, :], start=(k == 0), stop=(k == KD - 1))
                    mm.then_inc(w_used if c < 3 else filled, 1)

            def mod_sum(p, half):
                name = ("modsum", p, half)
                buffer_free(pe, name)
                pe.wait_ge(acc_made, 2 * (p - 2) + half + 1)
                for who in range(2):
                    mm = pe.matmul(buffer(name)[:, who * 512:(who + 1) * 512], ones[:, :], mod_acc[:, half, who, :],
                                   start=True, stop=True)
                mm.then_inc(filled, 1)

            def mod_sum1(p):
                name = ("modsum1", p)
                buffer_free(pe, name)
                pe.wait_ge(acc_made, 8 + p - 2)
                for b in range(2):
                    mm = pe.matmul(buffer(name)[:, b * 512:(b + 1) * 512], ones[:, :],
                                   mod_acc1[:, p % 2, b * 512:(b + 1) * 512], start=True, stop=True)
                mm.then_inc(filled, 1)

            def transposes(name, sources):
                buffer_free(pe, name)
                for n, src in enumerate(sources):
                    mm = pe.transpose(buffer(name)[:, n * P:n * P + P], src, ident[:, :])
                mm.then_inc(filled, 1)

            def project(c):
                name = ("proj", c)
                buffer_free(pe, name)
                wait_chunk(pe, name)
                for t in range(TILES):
                    for k in range(KD):
                        mm = pe.matmul(buffer(name)[:, t * WCOLS:(t + 1) * WCOLS], hTk[:, k, t * P:(t + 1) * P],
                                       chunk(name)[:, k, :], start=(k == 0), stop=(k == KD - 1))
                mm.then_inc(filled, 1)

            def mix(layer, t):
                name = ("out", layer, t)
                buffer_free(pe, name)
                for c in range(D // WCOLS):
                    if t == 0:
                        wait_chunk(pe, ("out", layer, c))
                    for k in range(KD):
                        mm = pe.matmul(buffer(name)[:, c * WCOLS:(c + 1) * WCOLS], hTk[:, k, t * P:(t + 1) * P],
                                       chunk(("out", layer, c))[:, k, :], start=(k == 0), stop=(k == KD - 1))
                mm.then_inc(filled, 1)

            def turn_lines(layer):
                name = ("cols", layer)
                buffer_free(pe, name)
                wait_mod(pe, f"mix{layer}")
                pe.transpose(buffer(name)[:, 0:4 * KD], mod_lines[layer], ident[0:4 * KD, 0:4 * KD]).then_inc(filled, 1)

            def turn_h(kind, layer, tiles):
                for t in tiles:
                    pe.wait_ge(h_made, H_BEFORE[kind, layer] + t + 1)
                    transposes((kind, layer, t), [h[:, t, k * P:(k + 1) * P] for k in range(KD)])

            def attention(layer, units):
                last = 16 if layer == 0 else MH
                base = 0 if layer == 0 else len(units0)

                def scores(n):
                    t, k = units[n]
                    if base + n >= 2:
                        pe.wait_ge(probs_made, base + n - 1)
                    q_at = slice(t * P, (t + 1) * P)
                    k_at = slice(0, TOK) if t < LAT_TILES else slice(SEQ, TOK)
                    kk = keys_of(layer, t)
                    dst = ps_s[:, n % 2, 0:kk]
                    if layer == 0:
                        g, kh = divmod(k, 8)
                        half = slice(HD * (kh % 2), HD * (kh % 2) + HD)
                        mm = pe.matmul(dst, qkT[half, 5 * g + kh // 2, q_at], qkT[half, 5 * g + 4, k_at],
                                       start=True, stop=True)
                    else:
                        half = slice(ROPE * (k % 2), ROPE * (k % 2) + ROPE)
                        pe.matmul(dst, qnT[:, k, q_at], knT[:, k, k_at], start=True, stop=False)
                        mm = pe.matmul(dst, qpT[half, k // 2, q_at], kpT[half, k_at], start=False, stop=True)
                    mm.then_inc(scores_made, 1)

                def weigh_values(n):
                    t, k = units[n]
                    kk = keys_of(layer, t)
                    wait_emptied(pe, ("PT", layer, n))
                    if k == 0 and base + t:
                        pe.wait_ge(o_made, t if layer == 0 else TILES + t)
                    for i in range(kk // P):
                        key_tile = i if t < LAT_TILES else LAT_TILES + i
                        if layer == 0:
                            g, kh = divmod(k, 8)
                            v_at = QKW + 2 * HD * g + HD * (kh % 2)
                            rhs = pj[:, key_tile, v_at:v_at + HD]
                            o_at = slice(k * HD, (k + 1) * HD)
                        else:
                            rhs = vm[:, key_tile, k * VD:(k + 1) * VD]
                            o_at = slice(k * VD, (k + 1) * VD)
                        mm = pe.matmul(ps_o[:, o_at], probsT[:, n % 2, i * P:(i + 1) * P], rhs,
                                       start=(i == 0), stop=(i == kk // P - 1))
                    mm.then_inc(pv_done, 1)

                def turn_out(t):
                    pe.wait_ge(o_made, (0 if layer == 0 else TILES) + t + 1)
                    transposes(("OT", layer, t), [o_sb[:, i * P:(i + 1) * P] for i in range(KD)])

                scores(0)
                scores(1)
                for n, (t, k) in enumerate(units):
                    if n + 2 < len(units):
                        scores(n + 2)
                    pe.wait_ge(probs_made, base + n + 1)
                    transposes(("PT", layer, n), [probs[:, n % 2, i * P:(i + 1) * P]
                                                  for i in range(keys_of(layer, t) // P)])
                    if layer == 0 and n == LATE_SUM:
                        mod_sum(*mod_half(5))
                    if layer == 1 and n in SUM1_AT:
                        mod_sum1(SUM1_AT[n])
                    if n:
                        weigh_values(n - 1)
                    if n >= 2 and ends_tile(units, n - 2):
                        turn_out(units[n - 2][0])
                weigh_values(len(units) - 1)
                turn_out(units[-1][0])

            def to_experts(layer):
                tiles = peer_tiles[layer]
                wait_emptied(pe, ("OT", layer, tiles - 1))
                for t in range(tiles):
                    mix(layer, t)
                    if layer == 1 and t == 1:
                        mod_sum1(5)
                    if t:
                        turn_h("hT2", layer, (t - 1,))
                wait_emptied(pe, ("hT2", layer, 0))
                for k in range(2):
                    name = ("query", layer, k)
                    buffer_free(pe, name)
                    wait_chunk(pe, name)
                    for s in range(2):
                        for kk in range(KD):
                            mm = pe.matmul(buffer(name)[:, s * 512:s * 512 + P], chunk(name)[:, kk, s * P:(s + 1) * P],
                                           hTk[:, kk, 0:P], start=(kk == 0), stop=(kk == KD - 1))
                    mm.then_inc(filled, 1)
                turn_h("hT2", layer, (tiles - 1,))
                experts_pe(pe, layer, silu, mod_sum, turn_lines, turn_h)

            for p in range(2):
                mod_rows_job(p)
            turn_lines(0)
            turn_h("hT", 0, range(TILES))
            wait_emptied(pe, ("hT", 0, TILES - 1))
            for c in range(EVEN_W // WCOLS):
                project(c)
                if c:
                    mod_sum(*mod_half(c - 1))
            pe.wait_ge(roped, QK_CHUNKS)
            for t in range(TILES):
                blocks = [pj[:, t, k * P:(k + 1) * P] for k in range(QKH // 2)]
                transposes(("qkT", t, 0), blocks[:8])
                transposes(("qkT", t, 1), blocks[8:])
            wait_emptied(pe, ("qkT", TILES - 1, 0))
            wait_emptied(pe, ("qkT", TILES - 1, 1))
            attention(0, units0)
            to_experts(0)
            turn_h("hT", 1, (3,))
            wait_emptied(pe, ("hT", 1, TILES - 1))
            for c in (1, 2, 0):
                name = ("down", c)
                buffer_free(pe, name)
                wait_chunk(pe, name)
                w = chunk(name)
                for t in range(TILES if c else LAT_TILES):
                    skip = QL - WCOLS if c == 1 and t >= LAT_TILES else 0
                    for k in range(KD):
                        mm = pe.matmul(buffer(name)[:, t * WCOLS + skip:t * WCOLS + w.shape[2]],
                                       hTk[:, k, t * P:(t + 1) * P], w[:, k, skip:],
                                       start=(k == 0), stop=(k == KD - 1))
                mm.then_inc(filled, 1)
            for n_done, t in enumerate(LAT_ORDER):
                pe.wait_ge(roped, QK_CHUNKS + n_done + 1)
                name = ("latT", t)
                buffer_free(pe, name)
                for n in range(0 if t < LAT_TILES else 3, 5):
                    pe.transpose(buffer(name)[:, n * P:(n + 1) * P], pm[:, t, n * P:(n + 1) * P], ident[:, :])
                pe.transpose(buffer(name)[:, 5 * P:6 * P], o_sb[:, t * P:(t + 1) * P], ident[:, :]).then_inc(filled, 1)
            wait_emptied(pe, ("latT", LAT_ORDER[-1]))
            for c in range(3):
                name = ("uq", c)
                buffer_free(pe, name)
                wait_chunk(pe, name)
                for t in range(LAT_TILES):
                    for k in range(QL // P):
                        mm = pe.matmul(buffer(name)[:, t * 512:(t + 1) * 512], cqT[:, k, t * P:(t + 1) * P],
                                       chunk(name)[:, k, :], start=(k == 0), stop=(k == QL // P - 1))
                mm.then_inc(filled, 1)
            for c in range(2):
                wait_chunk(pe, ("ukv", c))
                for t in range(TILES):
                    name = ("ukv", c, t)
                    buffer_free(pe, name)
                    for half in range(2):
                        for k in range(KVL // P):
                            mm = pe.matmul(buffer(name)[:, half * 512:(half + 1) * 512], ckvT[:, k, t * P:(t + 1) * P],
                                           chunk(("ukv", c))[:, k, half * 512:(half + 1) * 512],
                                           start=(k == 0), stop=(k == KVL // P - 1))
                    mm.then_inc(filled, 1)
            for t in range(LAT_TILES):
                pe.wait_ge(roped, QK_CHUNKS + TILES + t + 1)
                transposes(("qnT", t), [qm[:, t, k * P:(k + 1) * P] for k in range(MH)])
                transposes(("qpT", t), [qm[:, t, (MH + k) * P:(MH + k + 1) * P] for k in range(MH // 2)])
            for t in range(TILES):
                pe.wait_ge(roped, QK_CHUNKS + TILES + LAT_TILES + t + 1)
                transposes(("knT", t), [kn[:, t, k * P:(k + 1) * P] for k in range(MH)])
            wait_emptied(pe, ("knT", TILES - 1))
            wait_emptied(pe, ("qpT", LAT_TILES - 1))
            attention(1, units1)
            to_experts(1)

        @block.vector
        def _(dve):
            dve.wait_ge(cond_exp, 1)
            dve.tensor_scalar(cond[:, 1, :], cond[:, 1, :], 1.0, None, ALU.add)
            dve.drain()
            dve.reciprocal(cond[:, 1, :], cond[:, 1, :])
            dve.drain()
            dve.tensor_tensor(cond[:, 2, :], cond[:, 0, :], cond[:, 1, :], ALU.mult).then_inc(cond_silu, 1)
            dve.wait_ge(consts_in, 16 * n_const_loads)
            dve.wait_ge(made, 5)
            dve.tensor_scalar(sinks[:, 1, :], sinks[:, 0, :], -1.0, None, ALU.mult)

            def mod_product(p, half, k, who):
                acc = mod_acc[:, half]
                if p > 2 and k == 0 and who == 0:
                    wait_filled(dve, ("modsum", p - 1, half))
                kc, k_in = divmod(k, KD // 2)
                name = ("modv", p, half, kc)
                if k_in == 0 and who == 0:
                    wait_chunk(dve, name)
                w = chunk(name)[:, k_in, :]
                c = cond[:, 2, 2 * k + who:2 * k + who + 1]
                if k == 0:
                    ins = dve.tensor_scalar(acc[:, who, :], w, c, None, ALU.mult)
                else:
                    ins = dve.scalar_tensor_tensor(out=acc[:, who, :], in0=w, scalar=c, in1=acc[:, who, :],
                                                   op0=ALU.mult, op1=ALU.add)
                if k_in == KD // 2 - 1 and who:
                    ins.then_inc(modv_used, 1)

            def mod_bias(p, half):
                acc = mod_acc[:, half]
                dve.wait_ge(bias_acc_in, 32 if p == 5 else 16)
                row_ = bias_acc5 if p == 5 else bias_acc[:, (p - 2) * D:(p - 1) * D]
                dve.tensor_tensor(acc[0:1], acc[0:1],
                                  row_[0:1, half * 512:(half + 1) * 512].unsqueeze(1).broadcast_to([1, 2, 512]),
                                  ALU.add).then_inc(acc_made, 1)

            def mod_step1(step):
                p, k = 3 + step // KD, step % KD
                acc = mod_acc1[:, p % 2, :]
                name = ("modv1", p, k // 2)
                if p == 5 and k == 0:
                    wait_filled(dve, ("modsum1", 3))
                if k % 2 == 0:
                    wait_chunk(dve, name)
                w = chunk(name)[:, k % 2, :]
                c = cond[:, 2, 2 * k:2 * k + 1]
                if k == 0:
                    ins = dve.tensor_scalar(acc, w, c, None, ALU.mult)
                else:
                    ins = dve.scalar_tensor_tensor(out=acc, in0=w, scalar=c, in1=acc, op0=ALU.mult, op1=ALU.add)
                if k % 2:
                    ins.then_inc(modv_used, 1)
                dve.drain()
                if k == KD - 1:
                    dve.wait_ge(bias_acc_in, 48)
                    dve.tensor_tensor(acc[0:1], acc[0:1], bias_acc1[0:1, (p - 3) * D:(p - 2) * D],
                                      ALU.add).then_inc(acc_made, 1)

            def mod_products(p, half):
                for k in range(KD):
                    for who in range(2):
                        mod_product(p, half, k, who)
                    dve.drain()
                mod_bias(p, half)

            def empty_mod(p):
                name = ("mod", p)
                wait_filled(dve, name)
                dve.wait_ge(bias_in, 16 * (p + 2))
                if p:
                    dve.wait_ge(row_out, 16 * p)
                dve.tensor_tensor(row[0:2, :], buffer(name)[0:2, :], bias[0:2, :], ALU.add).then_inc(dve_emptied, 1)

            def inverse_rms(kind, layer, t):
                dve.tensor_tensor_reduce(out=h[:, t, :], in0=x[:, t, :], in1=x[:, t, :], scale=1.0, scalar=0.0,
                                         op0=ALU.mult, op1=ALU.add, accum_out=stat[:, t:t + 1]).then_inc(x_squared, 1)
                dve.wait_ge(x_rooted, H_BEFORE[kind, layer] + t + 1)
                dve.reciprocal(stat[:, 8 + t:9 + t], stat[:, 8 + t:9 + t])
                dve.drain()

            def make_scales(layer):
                wait_mod(dve, f"ffn{layer}")
                if layer == 0:
                    wait_mod(dve, "gain0")
                for who in range(peer_tiles[layer] // LAT_TILES):
                    dve.scalar_tensor_tensor(out=mod[:, 2 * who, :], in0=mod[:, 2 * who, :], scalar=1.0, in1=gain,
                                             op0=ALU.add, op1=ALU.mult)

            def norm(layer, t):
                inverse_rms("hT2", layer, t)
                who = t // LAT_TILES
                dve.scalar_tensor_tensor(out=h[:, t, :], in0=x[:, t, :], scalar=stat[:, 8 + t:9 + t],
                                         in1=mod[:, 2 * who, :], op0=ALU.mult, op1=ALU.mult)
                dve.drain()
                dve.tensor_tensor(h[:, t, :], h[:, t, :], mod[:, 2 * who + 1, :], ALU.add).then_inc(h_made, 1)

            def make_cols(layer):
                name = ("cols", layer)
                wait_filled(dve, name)
                b = buffer(name)[:, 0:4 * KD].rearrange("p (w q k) -> p w q k", w=2, q=2)
                dve.tensor_copy(mod_cols[:, :, 0, :], b[:, :, 0, :])
                for who in range(2):
                    ins = dve.scalar_tensor_tensor(out=mod_cols[:, who, 1, :], in0=b[:, who, 1, :], scalar=1.0,
                                                   in1=norm_cols[:, layer, :], op0=ALU.add, op1=ALU.mult)
                ins.then_inc(dve_emptied, 1)

            def over_rms(layer, t):
                inverse_rms("hT", layer, t)
                dve.tensor_scalar(h[:, t, :], x[:, t, :], stat[:, 8 + t:9 + t], None, ALU.mult).then_inc(h_made, 1)

            def turn(v, t, n_heads, tmp, width=HD):
                cs = rope[:, t, 0, :].unsqueeze(1).broadcast_to([P, n_heads, width])
                sn = rope[:, t, 1, :].rearrange("p (i two) -> p i two", two=2)
                pairs = v.rearrange("p h (i two) -> p h i two", two=2)
                tpairs = tmp.rearrange("p h (i two) -> p h i two", two=2)
                for e in range(2):
                    dve.tensor_tensor(tpairs[:, :, :, e], pairs[:, :, :, 1 - e],
                                      sn[:, :, e].unsqueeze(1).broadcast_to([P, n_heads, width // 2]), ALU.mult)
                dve.drain()
                dve.tensor_tensor(v, v, cs, ALU.mult)
                dve.drain()
                return dve.tensor_tensor(v, v, tmp, ALU.add)

            def swapped(n_heads):
                return view(arena, 18432 + 512, n_heads, HD)

            def over_heads_rms(v, stats):
                return dve.tensor_tensor(v, v, stats.unsqueeze(2).broadcast_to([P, v.shape[1], v.shape[2]]), ALU.mult)

            def scale_heads(v, stats, gains):
                over_heads_rms(v, stats)
                dve.drain()
                return dve.tensor_tensor(v, v, gains, ALU.mult)

            def attention(layer, units, scale, sink):
                last = 16 if layer == 0 else MH
                base = 0 if layer == 0 else len(units0)
                width = HD if layer == 0 else VD

                def shift(n):
                    t, k = units[n]
                    s = ps_s[:, n % 2, 0:keys_of(layer, t)]
                    dve.wait_ge(scores_made, base + n + 1)
                    if sink and k >= 8 and t < LAT_TILES:
                        other = 1 - t
                        dve.tensor_tensor(s[:, other * P:(other + 1) * P], s[:, other * P:(other + 1) * P],
                                          wmask[:, t, :], ALU.add)
                        dve.drain()
                    dve.tensor_reduce(soft[:, 0, n:n + 1], s, AX.X, ALU.max, negate=True)
                    dve.drain()
                    if sink and k >= 8:
                        dve.tensor_scalar(soft[:, 1, n:n + 1], soft[:, 0, n:n + 1], scale, sinks[:, 1, k - 8:k - 7],
                                          ALU.mult, ALU.min).then_inc(scores_biased, 1)
                    else:
                        dve.tensor_scalar(soft[:, 1, n:n + 1], soft[:, 0, n:n + 1], scale, None,
                                          ALU.mult).then_inc(scores_biased, 1)
                    if sink and k == last - 1:
                        dve.drain()
                        dve.tensor_tensor(stat[:, 16:24], soft[:, 1, n - 7:n + 1], sinks[:, 0, :],
                                          ALU.add).then_inc(sink_shift, 1)

                def divide(n):
                    t = units[n][0]
                    first = n - last + 1
                    dve.wait_ge(probs_made, base + n + 1)
                    if sink:
                        dve.wait_ge(sink_exp, t + 1)
                        dve.tensor_tensor(soft[:, 2, first + 8:n + 1], soft[:, 2, first + 8:n + 1],
                                          stat[:, 24:32], ALU.add)
                        dve.drain()
                    dve.reciprocal(soft[:, 3, first:n + 1], soft[:, 2, first:n + 1])
                    dve.drain()
                    dve.wait_ge(pv_done, base + n + 1)
                    if t or layer:
                        wait_filled(dve, ("OT", layer, t - 1) if t else ("latT", LAT_ORDER[-1]))
                    dve.tensor_tensor(o_sb.rearrange("p (k w) -> p k w", w=width),
                                      ps_o[:, :].rearrange("p (k w) -> p k w", w=width),
                                      soft[:, 3, first:n + 1].unsqueeze(2).broadcast_to([P, last, width]),
                                      ALU.mult).then_inc(o_made, 1)

                for n in range(len(units)):
                    shift(n)
                    if layer == 0 and n < 3 * 2 * KD:
                        i, step = divmod(n, 2 * KD)
                        mod_product(*mod_half(5 + i), step // 2, step % 2)
                        if step == 2 * KD - 1:
                            dve.drain()
                            mod_bias(*mod_half(5 + i))
                    if layer == 1:
                        for step in range(3 * n // 2, 3 * (n + 1) // 2):
                            mod_step1(step)
                    if n >= 2 and ends_tile(units, n - 2):
                        divide(n - 2)
                divide(len(units) - 1)

            def to_experts(layer):
                for t in range(peer_tiles[layer]):
                    name = ("out", layer, t)
                    wait_filled(dve, name)
                    if t == 0:
                        wait_mod(dve, f"gate{layer}")
                    dve.tensor_tensor(gated, buffer(name)[:, :], gate[:, t // LAT_TILES, :],
                                      ALU.mult).then_inc(dve_emptied, 1)
                    dve.drain()
                    dve.tensor_tensor(x[:, t, :], x[:, t, :], gated, ALU.add).then_inc(x_mixed, 1)
                    dve.drain()
                    norm(layer, t)
                experts_dve(dve, layer, make_cols, over_rms)

            for t in range(TILES):
                over_rms(0, t)
            for p in range(2):
                empty_mod(p)
            make_cols(0)

            def norm_heads(c):
                dve.wait_ge(root_made, c + 1)
                dve.reciprocal(chunk_stats(1, c), chunk_stats(1, c))
                dve.drain()
                cols_ = slice(c * WCOLS, (c + 1) * WCOLS)
                v = pj[:, :, cols_]
                for t in range(TILES):
                    vt = v[:, t, :].rearrange("p (h w) -> p h w", w=HD)
                    dve.tensor_tensor(vt, vt, chunk_stats(1, c)[:, t, :].unsqueeze(2).broadcast_to([P, 4, HD]), ALU.mult)
                dve.drain()
                ins = dve.tensor_tensor(v, v, gain_qk[:, cols_].unsqueeze(1).broadcast_to([P, TILES, WCOLS]), ALU.mult)
                for t in range(LAT_TILES):
                    dve.drain()
                    ins = turn(v[:, t, :].rearrange("p (h w) -> p h w", w=HD), t, 4, turned)
                ins.then_inc(roped, 1)

            for i in range(QK_CHUNKS):
                mod_products(*mod_half(i))
                norm_heads(i)
            for t in range(TILES):
                name = ("qkT", t, 1)
                empty(dve, name, qkT[:, 8:10, t * P:(t + 1) * P],
                      buffer(name)[:, 0:2 * P].rearrange("p (k t) -> p k t", t=P))
            attention(0, units0, HD ** -0.5, True)
            make_scales(0)
            to_experts(0)
            over_rms(1, 3)
            name = ("down", 1)
            wait_filled(dve, name)
            b = buffer(name)[:, :].rearrange("p (t n) -> p t n", n=WCOLS)
            dve.tensor_copy(pm[:, 0:LAT_TILES, WCOLS:2 * WCOLS], b[:, 0:LAT_TILES, :])
            dve.tensor_copy(pm[:, LAT_TILES:, QL:2 * WCOLS], b[:, LAT_TILES:, QL - WCOLS:]).then_inc(dve_emptied, 1)
            dve.wait_ge(bias_in, 16 * 4)
            dve.wait_ge(root_made, QK_CHUNKS + 1)
            dve.reciprocal(heads_stat[:, 1, 4:12], heads_stat[:, 1, 4:12])
            dve.drain()

            def scale_segment(c, t):
                at, width = ((0, QL), (QL, KVL), (QL + KVL, ROPE))[c]
                return dve.scalar_tensor_tensor(out=pm[:, t, at:at + width], in0=pm[:, t, at:at + width],
                                                scalar=heads_stat[:, 1, c * 4 + t:c * 4 + t + 1],
                                                in1=gain_m[:, at:at + width], op0=ALU.mult, op1=ALU.mult)

            def copy_rotary_key(t):
                kp = pm[:, t, QL + KVL:MLA_W].unsqueeze(1)
                return dve.tensor_copy(o_sb[:, t * P:(t + 1) * P].rearrange("p (two w) -> p two w", two=2),
                                       kp.broadcast_to([P, 2, ROPE]))

            for t in LAT_ORDER:
                scale_segment(1, t)
                scale_segment(2, t)
                dve.drain()
                if t < LAT_TILES:
                    turn(pm[:, t, QL + KVL:MLA_W].unsqueeze(1), t, 1, swapped(1))
                    dve.drain()
                ins = copy_rotary_key(t)
                if t >= LAT_TILES:
                    ins.then_inc(roped, 1)
                dve.drain()
            dve.wait_ge(root_made, QK_CHUNKS + 2)
            dve.reciprocal(heads_stat[:, 1, 0:2], heads_stat[:, 1, 0:2])
            dve.drain()
            for t in range(LAT_TILES):
                scale_segment(0, t).then_inc(roped, 1)
            gain_rope = gain_m[:, MLA_W + NOPE:MLA_W + NOPE + ROPE]

            def over_heads(g):
                return g.unsqueeze(1).broadcast_to([P, MH, g.shape[1]])

            def norm_query(t):
                over_heads_rms(qm[:, t, 0:D].rearrange("p (h w) -> p h w", w=NOPE),
                               heads_stat[:, 1, t * MH:(t + 1) * MH])
                v = qm[:, t, D:D + MH * ROPE].rearrange("p (h w) -> p h w", w=ROPE)
                scale_heads(v, heads_stat[:, 1, 16 + t * MH:16 + (t + 1) * MH], over_heads(gain_rope))
                dve.drain()
                turn(v, t, MH, swapped(MH)).then_inc(roped, 1)
                dve.drain()

            def sum_heads(dst, squares, width):
                return dve.tensor_reduce(dst, squares.rearrange("p (h w) -> p h w", w=width), AX.X, ALU.add)

            name = ("uq", 1)
            empty(dve, name, qm[:, :, 512:1024], buffer(name)[:, :].rearrange("p (t n) -> p t n", n=512))
            for t in range(LAT_TILES):
                dve.wait_ge(sq_made, t + 1)
                sum_heads(heads_stat[:, 0, t * MH:(t + 1) * MH], sq_q[t][:, 0:D], NOPE)
                sum_heads(heads_stat[:, 0, 16 + t * MH:16 + (t + 1) * MH], sq_q[t][:, D:], ROPE).then_inc(sq_read, 1)
            empty(dve, ("ukv", 0, 1), kn[:, 1, :], buffer(("ukv", 0, 1))[:, :])
            dve.wait_ge(root_made, QK_CHUNKS + 3)
            dve.reciprocal(heads_stat[:, 1, 0:32], heads_stat[:, 1, 0:32])
            dve.drain()
            norm_query(0)
            empty(dve, ("ukv", 0, 3), kn[:, 3, :], buffer(("ukv", 0, 3))[:, :])
            for t in range(TILES):
                dve.wait_ge(sq_made, LAT_TILES + t + 1)
                sum_heads(heads_stat[:, 0, 32 + t * MH:32 + (t + 1) * MH], sq_k[t], NOPE).then_inc(sq_read, 1)
            empty(dve, ("ukv", 1, 1), vm[:, 1, :], buffer(("ukv", 1, 1))[:, :])
            norm_query(1)
            empty(dve, ("ukv", 1, 3), vm[:, 3, :], buffer(("ukv", 1, 3))[:, :])
            dve.wait_ge(root_made, QK_CHUNKS + 4)
            dve.reciprocal(heads_stat[:, 1, 32:64], heads_stat[:, 1, 32:64])
            dve.drain()
            for t in range(TILES):
                over_heads_rms(kn[:, t, :].rearrange("p (h w) -> p h w", w=NOPE),
                               heads_stat[:, 1, 32 + t * MH:32 + (t + 1) * MH]).then_inc(roped, 1)
            for t in range(LAT_TILES):
                name = ("qpT", t)
                empty(dve, name, qpT[:, :, t * P:(t + 1) * P],
                      buffer(name)[:, 0:4 * P].rearrange("p (k t) -> p k t", t=P))
            attention(1, units1, (NOPE + ROPE) ** -0.5, False)
            make_scales(1)
            to_experts(1)


def kernel(**inputs):
    import numpy as np
    import concourse.bacc as bacc
    from concourse.bass_utils import run_bass_kernel_spmd as run

    i = {k: np.asarray(v) for k, v in inputs.items()}
    layers = 2
    pair = [0, 4, 1, 5, 2, 6, 3, 7]
    head_cols = lambda at, hs: [at + h * 64 + j for h in hs for j in range(64)]
    A_Q, A_K, A_V, B_Q, B_K, B_V = 0, 512, 640, 768, 1280, 1408
    cols = (head_cols(A_Q, pair) + head_cols(A_K, [0, 1]) + head_cols(B_Q, pair) + head_cols(B_K, [0, 1])
            + head_cols(A_V, [0, 1]) + head_cols(B_V, [0, 1]))
    rows = head_cols(0, pair) + head_cols(512, pair)
    gain_qk = np.concatenate([np.tile(i["a_q_norm"][0], 8), np.tile(i["a_k_norm"][0], 2),
                              np.tile(i["b_q_norm"][0], 8), np.tile(i["b_k_norm"][0], 2)])
    uq = i["mla_w_uq"][0].reshape(384, 8, 192)
    uq = np.concatenate([uq[:, :, :128].reshape(384, -1), uq[:, :, 128:].reshape(384, -1)], 1)
    ukv = i["mla_w_ukv"][0].reshape(256, 8, 256)
    ukv = np.concatenate([ukv[:, :, :128].reshape(256, -1), ukv[:, :, 128:].reshape(256, -1)], 1)
    gain_m = np.concatenate([i["mla_q_a_norm"][0], i["mla_kv_a_norm"][0], i["mla_k_rope_norm"][0],
                             i["mla_q_nope_norm"][0], i["mla_q_rope_norm"][0], i["mla_k_nope_norm"][0]])
    pos = np.arange(256)
    inv = (np.float32(10000.0) ** (-np.arange(0, 32, 2, dtype=np.float32) / np.float32(32))).astype(np.float32)
    ang = np.concatenate([(pos // 64).astype(np.float32)[:, None] * inv,
                          (pos % 64).astype(np.float32)[:, None] * inv], 1)
    cos, sin = np.cos(ang), np.sin(ang)
    rope = np.stack([np.repeat(cos, 2, 1), np.stack([-sin, sin], -1).reshape(256, 64)], 1)
    rope = rope.reshape(2, 128, 2, 64).transpose(1, 0, 2, 3)
    q, k = np.arange(128)[:, None], np.arange(128)[None, :]
    wmask = np.stack([np.where(k <= q, 0, MASKED), np.where(k >= q, 0, MASKED)], 1).astype(np.float32)
    keysT = i["peer_sub_keys"].transpose(0, 4, 1, 2, 3).reshape(layers, 128, 8, 256)
    arrays = {
        "x": i["x"][0], "ctx": i["ctx"][0],
        "cond": np.stack([i["c"][0], i["c_ctx"]]).reshape(2, 8, 128).transpose(2, 1, 0).reshape(128, 16),
        "mod_w": i["mod_w"], "mod_b2": np.repeat(i["mod_b"][:, None], 2, 1),
        "norm_cols": i["mix_norm"].reshape(layers, 8, 128).transpose(2, 0, 1),
        "nope_cols": np.stack([i["mla_q_nope_norm"][0], i["mla_k_nope_norm"][0]], 1), "ffn_norm": i["ffn_norm"],
        "even_w_in": i["even_w_in"][0][:, cols], "even_w_out": i["even_w_out"][0][rows],
        "gain_qk": gain_qk, "b_sink": i["b_sink"][0][pair], "rope": rope, "wmask": wmask,
        "mla_w_in": i["mla_w_in"][0], "mla_w_uq": uq, "mla_w_ukv": ukv, "mla_w_out": i["mla_w_out"][0],
        "gain_m": gain_m, "peer_w_query": i["peer_w_query"], "keysT": keysT,
        "peer_u": i["peer_u"].reshape(-1, 1024), "peer_v": i["peer_v"].reshape(-1, 1024),
    }
    arrays = {k: np.ascontiguousarray(v) for k, v in arrays.items()}
    nc = bacc.Bacc("TRN2", target_bir_lowering=False, num_devices=1)
    aps = {k: nc.dram_tensor(f"in_{k}", v.shape, mybir.dt.from_np(v.dtype), kind="ExternalInput").ap()
           for k, v in arrays.items()}
    out = nc.dram_tensor("out", (256, 1024), F32, kind="ExternalOutput").ap()
    build(nc, aps, out)
    r = run(nc, [{f"in_{k}": v for k, v in arrays.items()}], core_ids=[0])
    return np.asarray(r.results[0]["out"]).reshape(1, 256, 1024)
```
